# Optimizing a Trainium2 kernel written in Bass

```python
import jax, jax.numpy as jnp
from jax import lax
import numpy as np

D_MODEL = 1024
BATCH = 1
SEQ = 256
DEPTH = 2

N_CONV_LAYERS = DEPTH // 2
N_MLA_LAYERS = DEPTH - N_CONV_LAYERS
CONV_WIDTH = 3
V_HEAD_DIM = 128
N_HEADS = D_MODEL // V_HEAD_DIM
QK_NOPE_DIM = 128
QK_ROPE_DIM = 64
KV_LORA_RANK = D_MODEL // 4
Q_LORA_RANK = 3 * D_MODEL // 8
D_FF = -(-8 * D_MODEL // (3 * 256)) * 256
ROPE_THETA = 10000.0
RMS_EPS = 1e-6
Q_BLOCK = 128


def rms_norm(x, g):
    xf = x.astype(jnp.float32)
    y = xf * lax.rsqrt(jnp.mean(xf * xf, axis=-1, keepdims=True) + RMS_EPS)
    return (y * g.astype(jnp.float32)).astype(x.dtype)

def rope_tables(positions):
    inv_freq = ROPE_THETA ** (-jnp.arange(0, QK_ROPE_DIM, 2, dtype=jnp.float32) / QK_ROPE_DIM)
    ang = positions.astype(jnp.float32)[..., None] * inv_freq
    return jnp.cos(ang), jnp.sin(ang)

def apply_rope(x, cos, sin):
    cos = cos.astype(x.dtype)
    sin = sin.astype(x.dtype)
    x1, x2 = jnp.split(x, 2, axis=-1)
    return jnp.concatenate([x1 * cos - x2 * sin, x1 * sin + x2 * cos], axis=-1)

def short_conv_mixer(h, w_in, conv_w, w_out):
    s = h.shape[1]
    u = h @ w_in
    gate_b, gate_c, val = jnp.split(u, 3, axis=-1)
    z = gate_c * val
    zp = jnp.pad(z, ((0, 0), (CONV_WIDTH - 1, 0), (0, 0)))
    conv = sum(conv_w[k] * zp[:, k:k + s] for k in range(CONV_WIDTH))
    return (gate_b * conv) @ w_out

def swiglu_ffn(h, w13, w2):
    g, u = jnp.split(h @ w13, 2, axis=-1)
    return (jax.nn.silu(g) * u) @ w2

def shared_mla_kv(h, kv_norm_g, w_dkv, kv_latent_norm_g, w_ukv, cos, sin):
    b, s, _ = h.shape
    hn = rms_norm(h, kv_norm_g)
    ckv = hn @ w_dkv
    c_lat = rms_norm(ckv[..., :KV_LORA_RANK], kv_latent_norm_g)
    k_pe = apply_rope(ckv[..., KV_LORA_RANK:], cos, sin)
    kv = (c_lat @ w_ukv).reshape(b, s, N_HEADS, QK_NOPE_DIM + V_HEAD_DIM)
    k_nope, v = kv[..., :QK_NOPE_DIM], kv[..., QK_NOPE_DIM:]
    return k_nope, k_pe, v

def causal_block_attention(q_nope, q_pe, k_nope, k_pe, v):
    b, s = q_nope.shape[:2]
    nb = s // Q_BLOCK
    qn = q_nope.reshape(b, nb, Q_BLOCK, N_HEADS, QK_NOPE_DIM).transpose(1, 0, 2, 3, 4)
    qr = q_pe.reshape(b, nb, Q_BLOCK, N_HEADS, QK_ROPE_DIM).transpose(1, 0, 2, 3, 4)
    starts = jnp.arange(nb, dtype=jnp.int32) * Q_BLOCK
    k_idx = jnp.arange(s, dtype=jnp.int32)
    scale = (QK_NOPE_DIM + QK_ROPE_DIM) ** -0.5
    neg = jnp.finfo(jnp.float32).min

    def one_block(args):
        qn_b, qr_b, start = args
        sc = (jnp.einsum('bqhd,bkhd->bhqk', qn_b, k_nope)
              + jnp.einsum('bqhr,bkr->bhqk', qr_b, k_pe))
        sc = sc.astype(jnp.float32) * scale
        q_idx = start + jnp.arange(Q_BLOCK, dtype=jnp.int32)
        mask = k_idx[None, :] <= q_idx[:, None]
        p = jax.nn.softmax(jnp.where(mask, sc, neg), axis=-1).astype(v.dtype)
        return jnp.einsum('bhqk,bkhd->bqhd', p, v)

    out = lax.map(one_block, (qn, qr, starts))
    return out.transpose(1, 0, 2, 3, 4).reshape(b, s, N_HEADS, V_HEAD_DIM)

def mla_mixer(h, w_dq, q_norm_g, w_uq, w_o, k_nope, k_pe, v, cos_h, sin_h):
    b, s, _ = h.shape
    cq = rms_norm(h @ w_dq, q_norm_g)
    q = (cq @ w_uq).reshape(b, s, N_HEADS, QK_NOPE_DIM + QK_ROPE_DIM)
    q_nope = q[..., :QK_NOPE_DIM]
    q_pe = apply_rope(q[..., QK_NOPE_DIM:], cos_h, sin_h)
    attn = causal_block_attention(q_nope, q_pe, k_nope, k_pe, v)
    return attn.reshape(b, s, N_HEADS * V_HEAD_DIM) @ w_o

def first_inputs(seed: int = 0) -> dict:
    key = jax.random.key(seed)
    ks = iter(jax.random.split(key, 32))
    f32 = jnp.float32
    res_scale = (2 * DEPTH) ** -0.5

    def w(shape, fan_in, extra=1.0):
        return jax.random.normal(next(ks), shape, f32) * (fan_in ** -0.5) * extra

    def gain(shape):
        return 1.0 + 0.02 * jax.random.normal(next(ks), shape, f32)

    na, nm = N_CONV_LAYERS, N_MLA_LAYERS
    x = jax.random.normal(next(ks), (BATCH, SEQ, D_MODEL), f32)
    positions = jnp.broadcast_to(jnp.arange(SEQ, dtype=jnp.int32), (BATCH, SEQ))
    return {
        "x": x,
        "positions": positions,
        "conv_norm_g": gain((na, D_MODEL)),
        "conv_w_in": w((na, D_MODEL, 3 * D_MODEL), D_MODEL),
        "conv_w": w((na, CONV_WIDTH, D_MODEL), CONV_WIDTH),
        "conv_w_out": w((na, D_MODEL, D_MODEL), D_MODEL, res_scale),
        "conv_ffn_norm_g": gain((na, D_MODEL)),
        "conv_ffn_w13": w((na, D_MODEL, 2 * D_FF), D_MODEL),
        "conv_ffn_w2": w((na, D_FF, D_MODEL), D_FF, res_scale),
        "kv_norm_g": gain((D_MODEL,)),
        "w_dkv": w((D_MODEL, KV_LORA_RANK + QK_ROPE_DIM), D_MODEL),
        "kv_latent_norm_g": gain((KV_LORA_RANK,)),
        "w_ukv": w((KV_LORA_RANK, N_HEADS * (QK_NOPE_DIM + V_HEAD_DIM)), KV_LORA_RANK),
        "mla_norm_g": gain((nm, D_MODEL)),
        "mla_w_dq": w((nm, D_MODEL, Q_LORA_RANK), D_MODEL),
        "mla_q_norm_g": gain((nm, Q_LORA_RANK)),
        "mla_w_uq": w((nm, Q_LORA_RANK, N_HEADS * (QK_NOPE_DIM + QK_ROPE_DIM)), Q_LORA_RANK),
        "mla_w_o": w((nm, N_HEADS * V_HEAD_DIM, D_MODEL), N_HEADS * V_HEAD_DIM, res_scale),
        "mla_ffn_norm_g": gain((nm, D_MODEL)),
        "mla_ffn_w13": w((nm, D_MODEL, 2 * D_FF), D_MODEL),
        "mla_ffn_w2": w((nm, D_FF, D_MODEL), D_FF, res_scale),
        "final_norm_g": gain((D_MODEL,)),
    }

def first_block(x, positions,
              conv_norm_g, conv_w_in, conv_w, conv_w_out,
              conv_ffn_norm_g, conv_ffn_w13, conv_ffn_w2,
              kv_norm_g, w_dkv, kv_latent_norm_g, w_ukv,
              mla_norm_g, mla_w_dq, mla_q_norm_g, mla_w_uq, mla_w_o,
              mla_ffn_norm_g, mla_ffn_w13, mla_ffn_w2,
              final_norm_g):
    cos, sin = rope_tables(positions)
    cos_h, sin_h = cos[:, :, None, :], sin[:, :, None, :]
    h = x
    k_nope = k_pe = v = None
    for i in range(DEPTH):
        if i < N_CONV_LAYERS:
            h = h + short_conv_mixer(rms_norm(h, conv_norm_g[i]), conv_w_in[i], conv_w[i], conv_w_out[i])
            h = h + swiglu_ffn(rms_norm(h, conv_ffn_norm_g[i]), conv_ffn_w13[i], conv_ffn_w2[i])
        else:
            if i == N_CONV_LAYERS:
                k_nope, k_pe, v = shared_mla_kv(h, kv_norm_g, w_dkv, kv_latent_norm_g, w_ukv, cos, sin)
            j = i - N_CONV_LAYERS
            h = h + mla_mixer(rms_norm(h, mla_norm_g[j]), mla_w_dq[j], mla_q_norm_g[j], mla_w_uq[j],
                              mla_w_o[j], k_nope, k_pe, v, cos_h, sin_h)
            h = h + swiglu_ffn(rms_norm(h, mla_ffn_norm_g[j]), mla_ffn_w13[j], mla_ffn_w2[j])
    return rms_norm(h, final_norm_g)


DEPTH_2 = 1

EPS = 1e-6
GRID_W = 64
D_MIX = D_MODEL

GLA_HEADS = 4
GLA_DK = 64
GLA_DV = 128
GLA_KEY_WIDTH = GLA_HEADS * GLA_DK
GLA_WIDTH = GLA_HEADS * GLA_DV
GLA_GATE_RANK = 16
GLA_GATE_NORM = 16.0
GLA_CHUNK = 64

ATT_HEADS = 8
ATT_KV_HEADS = 2
ATT_HEAD_DIM = 64
ATT_WIDTH = ATT_HEADS * ATT_HEAD_DIM
ATT_KV_WIDTH = ATT_KV_HEADS * ATT_HEAD_DIM

N_GROUPS = 8
EXPERTS_PER_GROUP = 8
N_EXPERTS = N_GROUPS * EXPERTS_PER_GROUP
TOP_K = 2
D_EXPERT = 512
MOE_BLOCK = 128

IN_SIZES = (GLA_KEY_WIDTH, GLA_KEY_WIDTH, GLA_WIDTH, GLA_WIDTH,
            GLA_GATE_RANK, GLA_GATE_RANK,
            ATT_WIDTH, ATT_KV_WIDTH, ATT_KV_WIDTH)
D_IN = 2336


def rms_norm_2(x, gain):
    x32 = x.astype(jnp.float32)
    y = x32 * lax.rsqrt(jnp.mean(x32 * x32, axis=-1, keepdims=True) + EPS)
    return y.astype(x.dtype) * gain

def gla_chunked(q, k, v, log_a):
    B, H, T, dk = q.shape
    dv = v.shape[-1]
    C = GLA_CHUNK
    N = T // C
    f32 = jnp.float32
    qf = q.astype(f32).reshape(B, H, N, C, dk)
    kf = k.astype(f32).reshape(B, H, N, C, dk)
    vf = v.astype(f32).reshape(B, H, N, C, dv)
    b = jnp.cumsum(log_a.astype(f32).reshape(B, H, N, C, dk), axis=3)
    b_ref = b[:, :, :, C // 2 - 1:C // 2, :]
    b_last = b[:, :, :, -1:, :]
    scores = jnp.einsum('bhncd,bhnsd->bhncs', qf * jnp.exp(b - b_ref), kf * jnp.exp(b_ref - b))
    mask = jnp.tril(jnp.ones((C, C), dtype=bool))
    scores = jnp.where(mask, scores, 0.0)
    o_intra = jnp.einsum('bhncs,bhnse->bhnce', scores, vf)
    chunk_kv = jnp.einsum('bhncd,bhnce->bhnde', kf * jnp.exp(b_last - b), vf)
    chunk_decay = jnp.exp(b_last[:, :, :, 0, :])

    def step(state, inp):
        decay, kv = inp
        return decay[..., None] * state + kv, state

    init = jnp.zeros((B, H, dk, dv), f32)
    _, states = lax.scan(step, init, (jnp.moveaxis(chunk_decay, 2, 0), jnp.moveaxis(chunk_kv, 2, 0)))
    states = jnp.moveaxis(states, 0, 2)
    o_inter = jnp.einsum('bhncd,bhnde->bhnce', qf * jnp.exp(b), states)
    return (o_intra + o_inter).reshape(B, H, T, dv).astype(v.dtype)

def gla_group(q, k, v, g, z_fwd, z_bwd, up_f, up_f_bias, up_b, up_b_bias, out_gain):
    B, T, _ = q.shape

    def heads(t, d):
        return t.reshape(B, T, GLA_HEADS, d).transpose(0, 2, 1, 3)

    qh = heads(q, GLA_DK) * (GLA_DK ** -0.5)
    kh = heads(k, GLA_DK)
    vh = heads(v, GLA_DV)
    la_f = heads(jax.nn.log_sigmoid((z_fwd @ up_f + up_f_bias).astype(jnp.float32)) / GLA_GATE_NORM, GLA_DK)
    la_b = heads(jax.nn.log_sigmoid((z_bwd @ up_b + up_b_bias).astype(jnp.float32)) / GLA_GATE_NORM, GLA_DK)
    o_f = gla_chunked(qh, kh, vh, la_f)
    flip = lambda t: jnp.flip(t, axis=2)
    o_b = flip(gla_chunked(flip(qh), flip(kh), flip(vh), flip(la_b)))
    o = rms_norm_2(o_f + o_b, out_gain)
    o = o.transpose(0, 2, 1, 3).reshape(B, T, GLA_WIDTH)
    return o * jax.nn.silu(g)

def axial_rope_tables(T):
    rows = T // GRID_W
    row = jnp.repeat(jnp.arange(rows), GRID_W).astype(jnp.float32)
    col = jnp.tile(jnp.arange(GRID_W), rows).astype(jnp.float32)
    axis_dim = ATT_HEAD_DIM // 2
    inv_freq = ROPE_THETA ** (-jnp.arange(0, axis_dim, 2, dtype=jnp.float32) / axis_dim)
    ang = jnp.concatenate([row[:, None] * inv_freq, col[:, None] * inv_freq], axis=-1)
    return jnp.cos(ang), jnp.sin(ang)

def apply_axial_rope(x, cos, sin):
    xr = x.astype(jnp.float32).reshape(*x.shape[:-1], -1, 2)
    x0, x1 = xr[..., 0], xr[..., 1]
    out = jnp.stack([x0 * cos - x1 * sin, x0 * sin + x1 * cos], axis=-1)
    return out.reshape(x.shape).astype(x.dtype)

def gqa_group(q, k, v, q_gain, k_gain, out_gain):
    B, T, _ = q.shape
    dh = ATT_HEAD_DIM
    G = ATT_HEADS // ATT_KV_HEADS
    qh = rms_norm_2(q.reshape(B, T, ATT_HEADS, dh).transpose(0, 2, 1, 3), q_gain)
    kh = rms_norm_2(k.reshape(B, T, ATT_KV_HEADS, dh).transpose(0, 2, 1, 3), k_gain)
    vh = v.reshape(B, T, ATT_KV_HEADS, dh).transpose(0, 2, 1, 3)
    cos, sin = axial_rope_tables(T)
    qh = apply_axial_rope(qh, cos, sin) * (dh ** -0.5)
    kh = apply_axial_rope(kh, cos, sin)
    nb = T // Q_BLOCK
    q_blocks = qh.reshape(B, ATT_KV_HEADS, G, nb, Q_BLOCK, dh).transpose(3, 0, 1, 2, 4, 5)

    def attend(qb):
        s = jnp.einsum('bkgqd,bksd->bkgqs', qb, kh).astype(jnp.float32)
        p = jax.nn.softmax(s, axis=-1).astype(vh.dtype)
        return jnp.einsum('bkgqs,bksd->bkgqd', p, vh)

    o = lax.map(attend, q_blocks)
    o = o.transpose(1, 0, 4, 2, 3, 5).reshape(B, T, ATT_WIDTH)
    return rms_norm_2(o, out_gain)

def hier_moe(x, w_group, b_group, w_expert, b_expert, w_gate, w_up, w_down):
    B, T, D = x.shape
    xt = x.reshape(-1, D)
    N = xt.shape[0]
    g_logits = (xt @ w_group + b_group).astype(jnp.float32)
    g_prob = jax.nn.softmax(g_logits, axis=-1)
    g_idx = jnp.argmax(g_logits, axis=-1)
    g_w = jnp.take_along_axis(g_prob, g_idx[:, None], axis=-1)
    e_logits = (xt @ w_expert + b_expert).astype(jnp.float32).reshape(N, N_GROUPS, EXPERTS_PER_GROUP)
    e_logits = jnp.take_along_axis(e_logits, g_idx[:, None, None], axis=1)[:, 0]
    top_val, top_idx = lax.top_k(e_logits, TOP_K)
    gate = g_w * jax.nn.softmax(top_val, axis=-1)
    expert_id = g_idx[:, None] * EXPERTS_PER_GROUP + top_idx

    M = N * TOP_K
    flat_e = expert_id.reshape(M).astype(jnp.int32)
    flat_tok = jnp.repeat(jnp.arange(N, dtype=jnp.int32), TOP_K)
    flat_gate = gate.reshape(M).astype(x.dtype)
    order = jnp.argsort(flat_e)
    se = flat_e[order]
    counts = jnp.bincount(flat_e, length=N_EXPERTS)
    starts = jnp.cumsum(counts) - counts
    padded = (counts + MOE_BLOCK - 1) // MOE_BLOCK * MOE_BLOCK
    pad_ends = jnp.cumsum(padded)
    pad_starts = pad_ends - padded
    dest = pad_starts[se] + (jnp.arange(M, dtype=jnp.int32) - starts[se])
    P = M + N_EXPERTS * MOE_BLOCK
    slot_tok = jnp.zeros((P,), jnp.int32).at[dest].set(flat_tok[order])
    slot_gate = jnp.zeros((P,), x.dtype).at[dest].set(flat_gate[order])
    nblk = P // MOE_BLOCK
    blk_start = jnp.arange(nblk, dtype=jnp.int32) * MOE_BLOCK
    blk_expert = jnp.minimum(jnp.searchsorted(pad_ends, blk_start, side='right'), N_EXPERTS - 1)
    xs = xt[slot_tok].reshape(nblk, MOE_BLOCK, D)

    def run_block(args):
        xb, e = args
        h = jax.nn.silu(xb @ w_gate[e]) * (xb @ w_up[e])
        return h @ w_down[e]

    ys = lax.map(run_block, (xs, blk_expert)).reshape(P, D)
    y = jnp.zeros((N, D), x.dtype).at[slot_tok].add(ys * slot_gate[:, None])
    return y.reshape(B, T, D)

def second_inputs(seed: int = 0) -> dict:
    key = jax.random.key(seed)
    ks = jax.random.split(key, 24)
    f32 = jnp.float32
    L = DEPTH_2

    def nrm(k, shape, scale):
        return jax.random.normal(k, shape, f32) * scale

    def gain(k, shape):
        return 1.0 + 0.02 * jax.random.normal(k, shape, f32)

    return {
        "x": nrm(ks[0], (BATCH, SEQ, D_MODEL), 1.0),
        "norm1_gain": gain(ks[1], (L, D_MODEL)),
        "w_in": nrm(ks[2], (L, D_MODEL, D_IN), D_MODEL ** -0.5),
        "gla_up_fwd": nrm(ks[3], (L, GLA_GATE_RANK, GLA_KEY_WIDTH), GLA_GATE_RANK ** -0.5),
        "gla_up_fwd_bias": nrm(ks[4], (L, GLA_KEY_WIDTH), 0.1),
        "gla_up_bwd": nrm(ks[5], (L, GLA_GATE_RANK, GLA_KEY_WIDTH), GLA_GATE_RANK ** -0.5),
        "gla_up_bwd_bias": nrm(ks[6], (L, GLA_KEY_WIDTH), 0.1),
        "gla_out_gain": gain(ks[7], (L, GLA_DV)),
        "q_norm_gain": gain(ks[8], (L, ATT_HEAD_DIM)),
        "k_norm_gain": gain(ks[9], (L, ATT_HEAD_DIM)),
        "att_out_gain": gain(ks[10], (L, ATT_WIDTH)),
        "w_out": nrm(ks[11], (L, D_MIX, D_MODEL), D_MIX ** -0.5),
        "norm2_gain": gain(ks[12], (L, D_MODEL)),
        "w_group": nrm(ks[13], (L, D_MODEL, N_GROUPS), D_MODEL ** -0.5),
        "b_group": nrm(ks[14], (L, N_GROUPS), 0.01),
        "w_expert": nrm(ks[15], (L, D_MODEL, N_EXPERTS), D_MODEL ** -0.5),
        "b_expert": nrm(ks[16], (L, N_EXPERTS), 0.01),
        "w_gate": nrm(ks[17], (L, N_EXPERTS, D_MODEL, D_EXPERT), D_MODEL ** -0.5),
        "w_up": nrm(ks[18], (L, N_EXPERTS, D_MODEL, D_EXPERT), D_MODEL ** -0.5),
        "w_down": nrm(ks[19], (L, N_EXPERTS, D_EXPERT, D_MODEL), D_EXPERT ** -0.5),
        "final_gain": gain(ks[20], (D_MODEL,)),
    }

def second_block(x, norm1_gain, w_in, gla_up_fwd, gla_up_fwd_bias, gla_up_bwd, gla_up_bwd_bias,
              gla_out_gain, q_norm_gain, k_norm_gain, att_out_gain, w_out, norm2_gain,
              w_group, b_group, w_expert, b_expert, w_gate, w_up, w_down, final_gain):
    split_points = np.cumsum(IN_SIZES)[:-1].tolist()
    h = x
    for l in range(DEPTH_2):
        u = rms_norm_2(h, norm1_gain[l])
        proj = u @ w_in[l]
        gq, gk, gv, gg, zf, zb, aq, ak, av = jnp.split(proj, split_points, axis=-1)
        o_gla = gla_group(gq, gk, gv, gg, zf, zb, gla_up_fwd[l], gla_up_fwd_bias[l],
                          gla_up_bwd[l], gla_up_bwd_bias[l], gla_out_gain[l])
        o_att = gqa_group(aq, ak, av, q_norm_gain[l], k_norm_gain[l], att_out_gain[l])
        mixed = jnp.concatenate([o_gla, o_att], axis=-1)
        h = h + mixed @ w_out[l]
        h = h + hier_moe(rms_norm_2(h, norm2_gain[l]), w_group[l], b_group[l], w_expert[l],
                         b_expert[l], w_gate[l], w_up[l], w_down[l])
    return rms_norm_2(h, final_gain)


def setup_inputs(seed=0):
    out = dict(first_inputs(seed))
    for name, value in second_inputs(seed + 1).items():
        if name != "x":
            out[name + "_2"] = value
    return out


def reference(
    x, positions, conv_norm_g, conv_w_in, conv_w, conv_w_out, conv_ffn_norm_g, conv_ffn_w13,
    conv_ffn_w2, kv_norm_g, w_dkv, kv_latent_norm_g, w_ukv, mla_norm_g, mla_w_dq, mla_q_norm_g,
    mla_w_uq, mla_w_o, mla_ffn_norm_g, mla_ffn_w13, mla_ffn_w2, final_norm_g, norm1_gain_2,
    w_in_2, gla_up_fwd_2, gla_up_fwd_bias_2, gla_up_bwd_2, gla_up_bwd_bias_2, gla_out_gain_2,
    q_norm_gain_2, k_norm_gain_2, att_out_gain_2, w_out_2, norm2_gain_2, w_group_2, b_group_2,
    w_expert_2, b_expert_2, w_gate_2, w_up_2, w_down_2, final_gain_2,
):
    x = first_block(
        x, positions, conv_norm_g, conv_w_in, conv_w, conv_w_out, conv_ffn_norm_g, conv_ffn_w13,
        conv_ffn_w2, kv_norm_g, w_dkv, kv_latent_norm_g, w_ukv, mla_norm_g, mla_w_dq,
        mla_q_norm_g, mla_w_uq, mla_w_o, mla_ffn_norm_g, mla_ffn_w13, mla_ffn_w2, final_norm_g,
    )
    return second_block(
        x, norm1_gain_2, w_in_2, gla_up_fwd_2, gla_up_fwd_bias_2, gla_up_bwd_2,
        gla_up_bwd_bias_2, gla_out_gain_2, q_norm_gain_2, k_norm_gain_2, att_out_gain_2,
        w_out_2, norm2_gain_2, w_group_2, b_group_2, w_expert_2, b_expert_2, w_gate_2, w_up_2,
        w_down_2, final_gain_2,
    )


_drawn_inputs = setup_inputs


def setup_inputs(seed=0):
    import zlib

    import numpy as np

    out = dict(_drawn_inputs(seed))
    spreads = {}
    factors = {'conv_ffn_norm_g': 3.571,
     'kv_norm_g': 6.471,
     'kv_latent_norm_g': 5.748,
     'mla_norm_g': 8.0,
     'mla_q_norm_g': 8.0,
     'mla_ffn_norm_g': 3.34,
     'gla_up_fwd_bias_2': 3.766,
     'gla_up_bwd_bias_2': 4.036,
     'gla_out_gain_2': 4.461,
     'q_norm_gain_2': 3.543,
     'k_norm_gain_2': 4.444,
     'att_out_gain_2': 4.831,
     'norm2_gain_2': 2.947,
     'b_group_2': 8.0,
     'b_expert_2': 7.219,
     'final_gain_2': 2.826}
    for name, (base, spread) in spreads.items():
        noise = np.random.default_rng([zlib.crc32(name.encode()), seed]).standard_normal(out[name].shape)
        drawn = base * np.exp(spread * noise) if base else spread * noise
        out[name] = __import__('jax').numpy.asarray(drawn.astype(out[name].dtype))
    for name, factor in factors.items():
        out[name] = (out[name] * factor).astype(out[name].dtype)
    return out
```

```python
import concourse.bass as bass
from concourse import mybir
import numpy as np

F32 = mybir.dt.float32
F32R = mybir.dt.float32r
I32 = mybir.dt.int32
U32 = mybir.dt.uint32
ALU = mybir.AluOpType
ACT = mybir.ActivationFunctionType
AX = mybir.AxisListType.X

P = 128
T = 256
TT = T // P
D = 1024
KD = D // P
EPS = 1e-6
DFF = 2816
JC = D // 256
JF = DFF // 256
HEADS = 8
NOPE = 128
ROPE = 64
VD = 128
QR = 384
KVR = 256
GH, DK, DV, CH = 4, 64, 128, 64
NCH = T // CH
AH, AKV, AD = 8, 2, 64
NG, EPG = 8, 8
NE = NG * EPG
DE = 512
CAP = 64
BIG_NEG = -3.0e38

UNIT = 2048
RAW = 6
SPLIT = 3
U_CONV = 0
N_CONV = 4 * JC
U_FFN1 = U_CONV + N_CONV
N_FFN = 3 * JF
U_MLA = U_FFN1 + N_FFN
N_MLA = 14
U_FFN2 = U_MLA + N_MLA
U_WIN = U_FFN2 + N_FFN
N_WIN = 10
U_WOUT = U_WIN + N_WIN
U_MOE = U_WOUT + 4
N_MOE = 6 * NE

ROWS = {}
_at = 0
for _name, _n in (("conv_norm", 8), ("ffn1_norm", 8), ("kv_norm", 8), ("mla_norm", 8), ("ffn2_norm", 8),
                  ("norm1", 8), ("conv_w", 24), ("kv_latent", 2), ("q_norm", 3), ("att_out", 4),
                  ("up_f_bias", 2), ("up_b_bias", 2), ("gla_out", 1)):
    ROWS[_name] = _at
    _at += _n
NROWS = _at

CONST = {}
_at = 0
for _name, _n in (("ident", 128), ("iota", 64), ("before", 128), ("ones", 128), ("causal", 384),
                  ("keep_f", 64), ("keep_b", 64), ("fold", 64), ("ax_cos", 64), ("ax_sin", 64),
                  ("freq", 32), ("half", 2)):
    CONST[_name] = (_at, _n)
    _at += _n
NCONST = _at


def shape_constants():
    c = np.zeros((P, NCONST), np.float32)

    def put(name, a):
        at, n = CONST[name]
        c[:, at:at + n] = a

    p = np.arange(P)
    put("ident", np.eye(P))
    put("iota", np.arange(64)[None, :] + 0 * p[:, None])
    put("before", p[:, None] < p[None, :])
    put("ones", 1.0)
    tri = np.where(p[None, :] <= p[:, None], 0.0, BIG_NEG)
    put("causal", np.concatenate([tri, np.zeros((P, P)), tri], axis=1))
    s, q = p[:, None] % 64, np.arange(64)[None, :]
    put("keep_f", s <= q)
    put("keep_b", s >= q)
    put("fold", s == q)
    inv = np.float32(10000.0) ** (-np.arange(0, 32, 2, dtype=np.float32) / np.float32(32))
    for tt in range(TT):
        t = tt * P + p
        row, col = (t // 64).astype(np.float32), (t % 64).astype(np.float32)
        ang = np.concatenate([row[:, None] * inv, col[:, None] * inv], axis=1).astype(np.float32)
        at = CONST["ax_cos"][0] + 32 * tt
        c[:, at:at + 32] = np.cos(ang)
        at = CONST["ax_sin"][0] + 32 * tt
        c[:, at:at + 32] = np.sin(ang)
    freq = np.float32(10000.0) ** (-np.arange(0, 64, 2, dtype=np.float32) / np.float32(64))
    put("freq", freq[None, :] + 0 * p[:, None])
    put("half", -0.5)
    return c


def program(nc, a, consts_d, out):
    sems = {}

    def s(name):
        if name not in sems:
            sems[name] = nc.alloc_semaphore(name)
        return sems[name]

    stages = {}
    for kind, runs in (
            ("ssq", [("cv", 1), ("ffn1", 1), ("mla", 1), ("lat", 1), ("ffn2", 1), ("end1", 1), ("n1", 1), ("g", 1), ("a", 1),
                     ("n2", 1), ("end", 1)]),
            ("mean", [("cv", 1), ("ffn1", 1), ("mla", 1), ("lat", 1), ("ffn2", 1), ("end1", 1), ("n1", 1), ("g", 1), ("qkn", 1),
                      ("a", 1), ("n2", 1), ("end", 1)]),
            ("rstd", [("cv", 1), ("ffn1", 1), ("mla", 1), ("lat", 1), ("ffn2", 1), ("end1", 1), ("n1", 1), ("g", 1), ("qkn", 1),
                      ("a", 1), ("n2", 1), ("end", 1)]),
            ("xn", [("cv", 2), ("ffn1", 2), ("mla", 2), ("ffn2", 2), ("n1", 2), ("n2", 2)]),
            ("T", [("cv", 4), ("ffn1", 4), ("mla", 4), ("ffn2", 4), ("n1", 4), ("n2", 4)]),
            ("hi", [("cvx", 4), ("ffn1x", 4), ("mlax", 4), ("mlaq", 4), ("cl", 1), ("cq", 2), ("ffn2x", 4), ("n1x", 4), ("og", 2),
                    ("mo", 2)]),
            ("lo", [("cvx", 4), ("ffn1x", 4), ("mlax", 4), ("mlaq", 4), ("cl", 1), ("cq", 2), ("ffn2x", 4), ("n1x", 4), ("og", 2),
                    ("mo", 2)]),
            ("h", [("cv", 1), ("ffn1", 1), ("mla", 1), ("ffn2", 1), ("end1", 1), ("mix", 1)])):
        base = 0
        for tag, n in runs:
            stages[f"{tag}_{kind}"] = (f"all_{kind}", base)
            base += n

    def mark(name, n):
        sem, base = stages.get(name, (name, 0))
        return s(sem), base + n

    def sb(name, shape, dt=F32):
        return nc.alloc_sbuf_tensor(name, shape, dt)

    raw = sb("raw", [P, RAW, UNIT])
    w_hi = sb("w_hi", [P, SPLIT, UNIT], F32R)
    w_lo = sb("w_lo", [P, SPLIT, UNIT], F32R)
    cst = sb("cst", [P, NCONST])
    pcol = sb("pcol", [P, NROWS])
    h = sb("h", [P, TT, D])
    xT_hi = sb("xT_hi", [P, KD, T], F32R)
    xT_lo = sb("xT_lo", [P, KD, T], F32R)
    xS_hi = sb("xS_hi", [P, KD, T], F32R)
    xS_lo = sb("xS_lo", [P, KD, T], F32R)
    aT_hi = xS_hi[:, 0:4, :].rearrange("p (s f) t -> p s f t", s=2)
    aT_lo = xS_lo[:, 0:4, :].rearrange("p (s f) t -> p s f t", s=2)
    wr = sb("wr", [P, KD, NG + NE])
    small = sb("small", [P, 256])
    WORK = 14336
    work = sb("work", [P, WORK])
    ps = nc.alloc_psum_tensor("ps", [P, 8, 512], F32)
    y_slots = nc.dram_tensor("y_slots", (NE * CAP, D), F32, kind="Internal").ap()

    def const(name):
        at, n = CONST[name]
        return cst[:, at:at + n]

    ident = const("ident")

    def col(name, i=0):
        return pcol[:, ROWS[name] + i:ROWS[name] + i + 1]

    def wk(at, n):
        assert at + n <= WORK
        return work[:, at:at + n]

    def bank(b, n=512, at=0):
        return ps[:, b, at:at + n]

    def num(u, i=None):
        return u if i is None else i * RAW + u

    def load(sp, u, unit, i=None):
        src, k, c = unit
        if u >= RAW:
            sp.wait_ge(s("lo_done"), num(u - RAW + 1, i))
        sp.dma_start(raw[:, u % RAW, 0:k * c].rearrange("p (k c) -> p k c", k=k), src)\
            .then_inc(s(f"raw_full{u % RAW}"), 16)

    def split_hi(act, u, n, i=None):
        rev = u // RAW + 1
        act.wait_ge(s(f"raw_full{u % RAW}"), 16 * rev if i is None else i * 16 + 16 * rev)
        if u >= SPLIT:
            act.wait_ge(s("used"), num(u - SPLIT + 1, i))
        act.activation(w_hi[:, u % SPLIT, 0:n], raw[:, u % RAW, 0:n], ACT.Copy).then_inc(s("hi_done"), 1)

    def split_lo(dve, u, n, i=None):
        dve.wait_ge(s("hi_done"), num(u + 1, i))
        dve.tensor_tensor(w_lo[:, u % SPLIT, 0:n], raw[:, u % RAW, 0:n],
                          w_hi[:, u % SPLIT, 0:n].bitcast(F32), ALU.subtract).then_inc(s("lo_done"), 1)

    def unit_ready(pe, u, i=None):
        pe.wait_ge(s("lo_done"), num(u + 1, i))

    def weights(u, k, c):
        v = u % SPLIT
        return (w_hi[:, v, 0:k * c].rearrange("p (k c) -> p k c", k=k),
                w_lo[:, v, 0:k * c].rearrange("p (k c) -> p k c", k=k))

    def passes(pe, out_ap, stat_hi, stat_lo, mov_hi, mov_lo, first, last):
        pe.matmul(out_ap, stat_hi, mov_hi, start=first, stop=False, skip_group_check=True)
        pe.matmul(out_ap, stat_hi, mov_lo, start=False, stop=False, skip_group_check=True)
        return pe.matmul(out_ap, stat_lo, mov_hi, start=False, stop=last, skip_group_check=True)

    def by_channel(pe, u, out_bank, x, i=None):
        unit_ready(pe, u, i)
        hi, lo = weights(u, KD, 256)
        for f in range(2):
            for k in range(KD):
                last = passes(pe, bank(out_bank, T, f * T), hi[:, k, f * P:(f + 1) * P], lo[:, k, f * P:(f + 1) * P],
                              x[0][:, k, :], x[1][:, k, :], k == 0, k == KD - 1)
        last.then_inc(s("used"), 1)

    def by_token(pe, u, outs, x, chunks, k, c, n, first, last_unit, cols=None, i=None):
        unit_ready(pe, u, i)
        hi, lo = weights(u, k, c)
        for tt in range(TT):
            for part in range(len(outs[tt])):
                for q, ch in enumerate(chunks):
                    cs = slice(part * n, part * n + n) if cols is None else cols
                    last = passes(pe, outs[tt][part], x[0][:, ch, tt * P:(tt + 1) * P], x[1][:, ch, tt * P:(tt + 1) * P],
                                  hi[:, q, cs], lo[:, q, cs], first and q == 0, last_unit and q == len(chunks) - 1)
        return last

    xT = (xT_hi, xT_lo)
    xS = (xS_hi, xS_lo)
    ACC = [[bank(4), bank(5)], [bank(6), bank(7)]]

    def clear_acc(pe):
        for tt in range(TT):
            for part in range(2):
                pe.matmul(ACC[tt][part][:, 0:P], zeros[:, :], zeros[:, :], start=True, stop=False, skip_group_check=True)

    def rows_by_chunk(v):
        return v.rearrange("(k p) c -> p k c", p=P)

    def conv_unit(kind, j):
        if kind == 3:
            return rows_by_chunk(a["conv_w_out"][0][256 * j:256 * j + 256, :]), 2, D
        return rows_by_chunk(a["conv_w_in"][0][:, kind * D + 256 * j:kind * D + 256 * j + 256]), KD, 256

    def ffn_unit(w13, w2, kind, j):
        if kind == 2:
            if isinstance(j, int):
                return rows_by_chunk(w2[256 * j:256 * j + 256, :]), 2, D
            return rows_by_chunk(w2[bass.ds(j * 256, 256), :]), 2, D
        if isinstance(j, int):
            return rows_by_chunk(w13[:, kind * DFF + 256 * j:kind * DFF + 256 * j + 256]), KD, 256
        return rows_by_chunk(w13[:, bass.ds(j * 256 + kind * DFF, 256)]), KD, 256

    mla_units = []
    for q in range(2):
        mla_units.append((rows_by_chunk(a["w_dkv"][512 * q:512 * q + 512, :]), 4, KVR + ROPE))
    for q in range(2):
        mla_units.append((rows_by_chunk(a["mla_w_dq"][0][512 * q:512 * q + 512, :]), 4, QR))
    for q in range(4):
        mla_units.append((rows_by_chunk(a["mla_w_uq"][0][:, 384 * q:384 * q + 384]), 3, 384))
    for q in range(2):
        mla_units.append((rows_by_chunk(a["w_ukv"][:, 1024 * q:1024 * q + 1024]), 2, 1024))
    for q in range(4):
        mla_units.append((rows_by_chunk(a["mla_w_o"][0][256 * q:256 * q + 256, :]), 2, D))
    win = a["w_in_2"][0]
    win_units = [(rows_by_chunk(win[:, c0:c0 + n]), KD, n)
                 for c0, n in [(256 * q, 256) for q in range(6)] + [(1536, 160)] + [(1568 + 256 * q, 256) for q in range(3)]]
    wout_units = [(rows_by_chunk(a["w_out_2"][0][256 * q:256 * q + 256, :]), 2, D) for q in range(4)]

    def moe_unit(q, e):
        half = q % 2
        if q < 4:
            w = a["w_gate_2" if q < 2 else "w_up_2"][0]
            v = w[bass.ds(e, 1), half * 512:half * 512 + 512, :]
        else:
            v = a["w_down_2"][0][bass.ds(e, 1), :, half * 512:half * 512 + 512]
        return v.rearrange("a (k p) c -> p (a k) c", p=P), 4, 512

    size = [0] * U_MOE
    for j in range(JC):
        for q in range(4):
            size[4 * j + q] = UNIT
    for u in range(U_FFN1, U_MLA):
        size[u] = UNIT
    for q, (_, k, c) in enumerate(mla_units):
        size[U_MLA + q] = k * c
    for u in range(U_FFN2, U_WIN):
        size[u] = UNIT
    for q, (_, k, c) in enumerate(win_units):
        size[U_WIN + q] = k * c
    for q in range(4):
        size[U_WOUT + q] = UNIT
    size += [UNIT] * 6

    def ahead_hi(act, u):
        split_hi(act, u + SPLIT, size[u + SPLIT])

    def ahead_lo(dve, u):
        split_lo(dve, u + SPLIT, size[u + SPLIT])

    zeros = sb("zeros", [P, P], F32R)

    steps = {"act": 0, "dve": 0}

    def act_step(act, ins):
        steps["act"] += 1
        ins.then_inc(s("act_steps"), 1)
        act.wait_ge(s("act_steps"), steps["act"])

    def dve_step(dve, ins):
        steps["dve"] += 1
        ins.then_inc(s("dve_steps"), 1)
        dve.wait_ge(s("dve_steps"), steps["dve"])

    XN = 0

    def norm_act(act, tag, after):
        act.wait_ge(*mark(after[0], after[1]))
        for tt in range(TT):
            last = act.activation(wk(2048, D), h[:, tt, :], ACT.Square, accum_out=small[:, tt:tt + 1])
            if tt == 0:
                act_step(act, last)
            else:
                last.then_inc(s("all_ssq"), 1)

    def norm_pool(pool, tag):
        pool.wait_ge(*mark(f"{tag}_mean", 1))
        pool.tensor_tensor(small[:, 4:6], small[:, 2:4], const("half"), ALU.pow).then_inc(s("all_rstd"), 1)

    def norm_dve(dve, tag):
        dve.wait_ge(*mark(f"{tag}_ssq", 1))
        dve.tensor_scalar(small[:, 2:4], small[:, 0:2], 1.0 / D, EPS, ALU.mult, ALU.add).then_inc(s("all_mean"), 1)
        dve.wait_ge(*mark(f"{tag}_rstd", 1))
        for tt in range(TT):
            dve.tensor_scalar(wk(XN + tt * D, D), h[:, tt, :], small[:, 4 + tt:5 + tt], None, ALU.mult)\
                .then_inc(s("all_xn"), 1)

    def norm_pe(pe, tag):
        pe.wait_ge(*mark(f"{tag}_xn", TT))
        for k in range(KD):
            for tt in range(TT):
                last = pe.transpose(bank(k // 2, P, (k % 2) * T + tt * P), wk(XN + tt * D + k * P, P), ident)
            if k % 2:
                last.then_inc(s("all_T"), 1)

    def operand_act(act, tag, psum_tag, banks, gain, dst, first=0, at=0, also=None):
        for b, (pb, n) in enumerate(banks):
            act.wait_ge(*mark(psum_tag, at + b + 1))
            if also is not None:
                act.wait_ge(*mark(also, b + 1))
            for q in range(n):
                k = first + 2 * b + q
                last = act.activation(dst[0][:, k, :], bank(pb, T, q * T), ACT.Copy, scale=gain(2 * b + q))
            last.then_inc(s("all_hi"), 1)

    def operand_dve(dve, tag, banks, gain, dst, first=0):
        for b, (pb, n) in enumerate(banks):
            dve.wait_ge(*mark(f"{tag}_hi", b + 1))
            for q in range(n):
                k = first + 2 * b + q
                last = dve.scalar_tensor_tensor(dst[1][:, k, :], bank(pb, T, q * T), gain(2 * b + q),
                                                dst[0][:, k, :].bitcast(F32), ALU.mult, ALU.subtract)
            last.then_inc(s("all_lo"), 1)

    NORM_BANKS = [(0, 2), (1, 2), (2, 2), (3, 2)]

    def add_acc(dve, units_done, tag):
        dve.wait_ge(s("used"), units_done)
        for tt in range(TT):
            last = dve.tensor_tensor(h[:, tt, :], h[:, tt, :],
                                     ps[:, 4 + 2 * tt:6 + 2 * tt, :].rearrange("p b n -> p (b n)"), ALU.add)
        last.then_inc(s("all_h"), 1)

    CV = 4096
    ZP = T + 2

    def conv_pe(pe):
        norm_pe(pe, "cv")
        pe.wait_ge(*mark("cvx_lo", 4))
        pe.wait_ge(s("zeros"), 1)
        clear_acc(pe)
        for j in range(JC):
            u = U_CONV + (3 * j if j == 0 else 4 * j - 1)
            for q in range(3):
                if j:
                    pe.wait_ge(s("cv_y"), 2 * j)
                by_channel(pe, u + q, q, xT)
            if j:
                conv_out(pe, j - 1, u + 3)
        conv_out(pe, JC - 1, U_CONV + N_CONV - 1)

    def conv_out(pe, j, u):
        pe.wait_ge(s("cv_alo"), j + 1)
        last = by_token(pe, u, ACC, (aT_hi[:, j % 2], aT_lo[:, j % 2]), [0, 1], 2, D, 512, False, j == JC - 1)
        last.then_inc(s("used"), 1)

    def conv_act(act):
        for u in range(SPLIT):
            split_hi(act, u, size[u])
        norm_act(act, "cv", ("h_loaded", 16))
        operand_act(act, "cvx", "cv_T", NORM_BANKS, lambda k: col("conv_norm", k), xT)
        for j in range(JC):
            u = U_CONV + (3 * j if j == 0 else 4 * j - 1)
            for q in range(3):
                ahead_hi(act, u + q)
            act.wait_ge(s("used"), u + 3)
            if j:
                act.wait_ge(s("cv_y"), 2 * j)
            act.activation(wk(CV, 512), bank(1), ACT.Copy).then_inc(s("cv_c"), 1)
            if j:
                ahead_hi(act, u + 3)
            act.wait_ge(s("cv_y"), 2 * j + 2)
            if j >= 2:
                act.wait_ge(s("used"), conv_out_unit(j - 2) + 1)
            act.activation(aT_hi[:, j % 2].rearrange("p f t -> p (f t)"), wk(CV + 2048, 512), ACT.Copy)\
                .then_inc(s("cv_ahi"), 1)
        ahead_hi(act, U_CONV + N_CONV - 1)

    def conv_out_unit(j):
        return U_CONV + (4 * j + 6 if j < JC - 1 else N_CONV - 1)

    def conv_dve(dve):
        for u in range(SPLIT):
            split_lo(dve, u, size[u])
        norm_dve(dve, "cv")
        operand_dve(dve, "cvx", NORM_BANKS, lambda k: col("conv_norm", k), xT)
        dve_step(dve, dve.memset(wk(CV + 512, 2 * ZP), 0.0))
        for j in range(JC):
            u = U_CONV + (3 * j if j == 0 else 4 * j - 1)
            for q in range(3):
                ahead_lo(dve, u + q)
            dve.wait_ge(s("cv_c"), j + 1)
            for f in range(2):
                z = wk(CV + 512 + f * ZP, ZP)
                t0, t1 = wk(CV + 1536, T), wk(CV + 1792, T)
                w = [col("conv_w", 8 * tap + 2 * j + f) for tap in range(3)]
                dve_step(dve, dve.tensor_tensor(z[:, 2:ZP], bank(2, T, f * T), wk(CV + f * T, T), ALU.mult))
                dve_step(dve, dve.tensor_scalar(t0, z[:, 0:T], w[0], None, ALU.mult))
                dve_step(dve, dve.scalar_tensor_tensor(t1, z[:, 1:T + 1], w[1], t0, ALU.mult, ALU.add))
                dve_step(dve, dve.scalar_tensor_tensor(t0, z[:, 2:ZP], w[2], t1, ALU.mult, ALU.add))
                if f == 0 and j:
                    dve.wait_ge(s("cv_ahi"), j)
                dve.tensor_tensor(wk(CV + 2048 + f * T, T), bank(0, T, f * T), t0, ALU.mult).then_inc(s("cv_y"), 1)
            if j:
                ahead_lo(dve, u + 3)
            dve.wait_ge(s("cv_ahi"), j + 1)
            dve.tensor_tensor(aT_lo[:, j % 2].rearrange("p f t -> p (f t)"), wk(CV + 2048, 512),
                              aT_hi[:, j % 2].rearrange("p f t -> p (f t)").bitcast(F32), ALU.subtract)\
                .then_inc(s("cv_alo"), 1)
        ahead_lo(dve, U_CONV + N_CONV - 1)
        add_acc(dve, U_CONV + N_CONV, "cv")

    FG = 4096

    def ffn_pe(pe, n, base):
        t = f"ffn{n}"
        norm_pe(pe, t)
        pe.wait_ge(*mark(f"{t}x_lo", 4))
        clear_acc(pe)

        def up(u, slot_j, i=None, jj=None):
            if jj is not None:
                pe.wait_ge(s(f"{t}_a"), jj)
            by_channel(pe, u, 0, xT, i)
            by_channel(pe, u + 1, 1, xT, i)

        def down(u, slot_j, jj, i=None, last_block=False):
            pe.wait_ge(s(f"{t}_alo"), jj)
            last = by_token(pe, u, ACC, (aT_hi[:, slot_j], aT_lo[:, slot_j]), [0, 1], 2, D, 512, False, last_block, i=i)
            last.then_inc(s("used"), 1)

        up(base, 0)
        with pe.Fori(0, (JF - 1) // 2) as i:
            for q in range(2):
                up(base + 2 + 3 * q, (1 + q) % 2, i, i * 2 + (1 + q))
                down(base + 4 + 3 * q, q % 2, i * 2 + (1 + q), i)
        down(base + N_FFN - 1, (JF - 1) % 2, JF, last_block=True)

    def ffn_act(act, n, base, after, gain):
        t = f"ffn{n}"
        norm_act(act, t, after)
        operand_act(act, f"{t}x", f"{t}_T", NORM_BANKS, gain, xT)

        def gate(u, jj, i=None):
            act.wait_ge(s("used"), num(u + 2, i))
            if jj is not None:
                act.wait_ge(s(f"{t}_a"), jj)
            act.activation(wk(FG, 512), bank(0), ACT.Silu).then_inc(s(f"{t}_silu"), 1)

        def a_hi(slot_j, jj, used, i=None):
            act.wait_ge(s(f"{t}_a"), jj)
            if used is not None:
                act.wait_ge(s("used"), num(used, i))
            act.activation(aT_hi[:, slot_j].rearrange("p f t -> p (f t)"), wk(FG + 512, 512), ACT.Copy)\
                .then_inc(s(f"{t}_ahi"), 1)

        ahead_hi(act, base)
        ahead_hi(act, base + 1)
        gate(base, None)
        a_hi(0, 1, None)
        with act.Fori(0, (JF - 1) // 2) as i:
            for q in range(2):
                u = base + 2 + 3 * q
                split_hi(act, u + SPLIT, UNIT, i)
                split_hi(act, u + SPLIT + 1, UNIT, i)
                gate(u, i * 2 + (1 + q), i)
                split_hi(act, u + SPLIT + 2, size[u + SPLIT + 2], i)
                a_hi((1 + q) % 2, i * 2 + (2 + q), u, i)
        ahead_hi(act, base + N_FFN - 1)

    def ffn_dve(dve, n, base, gain):
        t = f"ffn{n}"
        norm_dve(dve, t)
        operand_dve(dve, f"{t}x", NORM_BANKS, gain, xT)

        def gated(jj, jj0):
            dve.wait_ge(s(f"{t}_silu"), jj)
            if jj0 is not None:
                dve.wait_ge(s(f"{t}_ahi"), jj0)
                dve.wait_ge(s(f"{t}_alo"), jj0)
            dve.tensor_tensor(wk(FG + 512, 512), bank(1), wk(FG, 512), ALU.mult).then_inc(s(f"{t}_a"), 1)

        def a_lo(slot_j, jj):
            dve.wait_ge(s(f"{t}_ahi"), jj)
            dve.tensor_tensor(aT_lo[:, slot_j].rearrange("p f t -> p (f t)"), wk(FG + 512, 512),
                              aT_hi[:, slot_j].rearrange("p f t -> p (f t)").bitcast(F32), ALU.subtract)\
                .then_inc(s(f"{t}_alo"), 1)

        ahead_lo(dve, base)
        ahead_lo(dve, base + 1)
        gated(1, None)
        a_lo(0, 1)
        with dve.Fori(0, (JF - 1) // 2) as i:
            for q in range(2):
                u = base + 2 + 3 * q
                split_lo(dve, u + SPLIT, UNIT, i)
                split_lo(dve, u + SPLIT + 1, UNIT, i)
                gated(i * 2 + (2 + q), i * 2 + (1 + q))
                split_lo(dve, u + SPLIT + 2, size[u + SPLIT + 2], i)
                a_lo((1 + q) % 2, i * 2 + (2 + q))
        ahead_lo(dve, base + N_FFN - 1)
        add_acc(dve, base + N_FFN, t)

    def rstd_dve(dve, tag, groups, at, n):
        for first, count, width in groups:
            last = dve.tensor_scalar(small[:, at + first - groups[0][0]:at + first - groups[0][0] + count],
                                     small[:, first:first + count], 1.0 / width, EPS, ALU.mult, ALU.add)
        last.then_inc(s("all_mean"), 1)
        dve.wait_ge(*mark(f"{tag}_rstd", 1))

    def rstd_pool(pool, tag, at, n):
        pool.wait_ge(*mark(f"{tag}_mean", 1))
        pool.tensor_tensor(small[:, at + n:at + 2 * n], small[:, at:at + n],
                           const("half")[:, 0:1].broadcast_to([P, n]), ALU.pow).then_inc(s("all_rstd"), 1)

    CL, CQ, KPE = 0, 512, 1280
    QN, KN, VV = 2048, 4096, 6144
    QPE, QPT, KPT, RT = 8192, 9216, 10240, 10496
    ROT = 11520
    SM, PB, PT = 11648, 12416, 13184
    CHL = (xT_hi, xT_lo)
    SCALE = (NOPE + ROPE) ** -0.5
    cos_p = lambda tt: wk(ROT + 32 * tt, 32)
    sin_p = lambda tt: wk(ROT + 64 + 32 * tt, 32)

    def rope_tables_dve(dve):
        magic = 12582912.0
        dve.wait_ge(s("params"), 16 * 19)
        dve_step(dve, dve.tensor_copy(small[:, 20:22], pos_i[:, :]))
        ang, turns, r = wk(RT, 64), wk(RT + 64, 64), wk(RT + 128, 64)
        for tt in range(TT):
            dve_step(dve, dve.tensor_scalar(ang[:, 32 * tt:32 * tt + 32], const("freq"), small[:, 20 + tt:21 + tt], None, ALU.mult))
        dve_step(dve, dve.tensor_scalar(turns, ang, float(np.float32(1 / (2 * np.pi))), magic, ALU.mult, ALU.add))
        dve_step(dve, dve.tensor_scalar(turns, turns, -magic, None, ALU.add))
        c1 = 6.28125
        c2 = float(np.float32(np.round((2 * np.pi - c1) * 2 ** 20) / 2 ** 20))
        c3 = float(2 * np.pi - c1 - c2)
        for c, src in ((c1, ang), (c2, r), (c3, r)):
            dve_step(dve, dve.scalar_tensor_tensor(r, turns, -c, src, ALU.mult, ALU.add))
        dve_step(dve, dve.tensor_scalar(r, r, 3.1415925, -3.1415925, ALU.min, ALU.max))
        dve_step(dve, dve.tensor_scalar(ang, r, -1.0, None, ALU.mult))
        dve_step(dve, dve.tensor_tensor(ang, ang, r, ALU.max))
        dve.tensor_scalar(ang, ang, -1.0, float(np.pi / 2), ALU.mult, ALU.add).then_inc(s("angles"), 1)

    def rope_tables_act(act):
        act.wait_ge(s("angles"), 1)
        act.activation(wk(ROT, 64), wk(RT, 64), ACT.Sin).then_inc(s("rope_tables"), 1)
        act.activation(wk(ROT + 64, 64), wk(RT + 128, 64), ACT.Sin).then_inc(s("rope_tables"), 1)

    def halves_rope(dve, x, dst, tt, groups):
        cos = cos_p(tt)[:, None, :].broadcast_to([P, groups, 32])
        sin = sin_p(tt)[:, None, :].broadcast_to([P, groups, 32])
        t = [wk(RT + 256 * q, 32 * groups).rearrange("p (g c) -> p g c", c=32) for q in range(4)]
        x1, x2 = x[:, :, 0:32], x[:, :, 32:64]
        dve.tensor_tensor(t[0], x1, cos, ALU.mult)
        dve.tensor_tensor(t[1], x2, sin, ALU.mult)
        dve.tensor_tensor(t[2], x1, sin, ALU.mult)
        dve_step(dve, dve.tensor_tensor(t[3], x2, cos, ALU.mult))
        dve.tensor_tensor(dst[:, :, 0:32], t[0], t[1], ALU.subtract)
        dve_step(dve, dve.tensor_tensor(dst[:, :, 32:64], t[2], t[3], ALU.add))

    def mla_pe(pe):
        u = U_MLA
        norm_pe(pe, "mla")
        pe.wait_ge(*mark("mlax_lo", 4))
        for q in range(2):
            by_token(pe, u + q, [[bank(4, 320)], [bank(5, 320)]], xT, range(4 * q, 4 * q + 4), 4, 320, 320,
                     q == 0, q == 1).then_inc(s("used"), 1)
        pe.wait_ge(*mark("mlaq_lo", 4))
        for q in range(2):
            by_token(pe, u + 2 + q, [[bank(6, QR)], [bank(7, QR)]], xS, range(4 * q, 4 * q + 4), 4, QR, QR,
                     q == 0, q == 1).then_inc(s("used"), 1)
        pe.wait_ge(s("latents"), 1)
        for c in range(2):
            for tt in range(TT):
                last = pe.transpose(bank(0, P, c * T + tt * P), wk(CL + 256 * tt + c * P, P), ident)
        last.then_inc(s("lat_T"), 1)
        for c in range(3):
            for tt in range(TT):
                last = pe.transpose(bank(1 + c // 2, P, (c % 2) * T + tt * P), wk(CQ + QR * tt + c * P, P), ident)
            if c:
                last.then_inc(s("lat_T"), 1)
        for tt in range(TT):
            last = pe.transpose(bank(3, P, tt * P), wk(KPE + P * tt, P), ident)
        last.then_inc(s("lat_T"), 1)
        pe.wait_ge(*mark("cq_lo", 2))
        for q in range(4):
            unit_ready(pe, u + 4 + q)
            hi, lo = weights(u + 4 + q, 3, 384)
            if q >= 2:
                pe.wait_ge(s("qn_read"), q - 1)
            for hh in range(2):
                for k in range(3):
                    cs = slice(192 * hh, 192 * hh + NOPE)
                    passes(pe, bank(q % 2, T, hh * T), hi[:, k, cs], lo[:, k, cs], xS_hi[:, k, :], xS_lo[:, k, :], k == 0, k == 2)
            for tt in range(TT):
                for k in range(3):
                    ts = slice(tt * P, tt * P + P)
                    m = [w[:, k, :].rearrange("p (h c) -> p h c", c=192)[:, :, NOPE:192] for w in (hi, lo)]
                    last = passes(pe, bank(4 + tt, P, P * q).rearrange("p (h c) -> p h c", c=ROPE), xS_hi[:, k, ts], xS_lo[:, k, ts],
                                  m[0], m[1], k == 0, k == 2)
            last.then_inc(s("used"), 1)
        pe.wait_ge(*mark("cl_lo", 1))
        pe.wait_ge(s("kpt"), 1)
        for q in range(2):
            unit_ready(pe, u + 8 + q)
            hi, lo = weights(u + 8 + q, 2, 1024)
            if q:
                pe.wait_ge(s("kn_read"), 1)
                pe.wait_ge(s("v_read"), 1)
            for hh in range(4):
                for k in range(2):
                    cs = slice(256 * hh, 256 * hh + NOPE)
                    passes(pe, bank(2 + hh // 2, T, (hh % 2) * T), hi[:, k, cs], lo[:, k, cs], xT_hi[:, k, :], xT_lo[:, k, :], k == 0, k == 1)
            for tt in range(TT):
                for k in range(2):
                    ts = slice(tt * P, tt * P + P)
                    m = [w[:, k, :].rearrange("p (h c) -> p h c", c=256)[:, :, NOPE:256] for w in (hi, lo)]
                    last = passes(pe, bank(6 + tt).rearrange("p (h c) -> p h c", c=VD), xT_hi[:, k, ts], xT_lo[:, k, ts],
                                  m[0], m[1], k == 0, k == 1)
            last.then_inc(s("used"), 1)
        pe.wait_ge(s("qpe"), 1)
        pe.wait_ge(s("qn_read"), 4)
        for c in range(4):
            for tt in range(TT):
                last = pe.transpose(bank(c // 2, P, (c % 2) * T + tt * P), wk(QPE + 512 * tt + c * P, P), ident)
        last.then_inc(s("qpe_T"), 1)
        pe.wait_ge(s("qpt"), 1)
        pe.wait_ge(s("kn_read"), 2)
        pe.wait_ge(s("v_read"), 2)
        for t in range(HEADS + 2):
            if t < HEADS:
                r = slice(64 * (t % 2), 64 * (t % 2) + 64)
                b = 2 + t % 2
                if t >= 2:
                    pe.wait_ge(s("sc_read"), t - 1)
                for tt in range(TT):
                    o = bank(b, P * (tt + 1), P * tt)
                    qs = slice(T * t + P * tt, T * t + P * tt + P)
                    n = P * (tt + 1)
                    pe.matmul(o, work[:, QN + qs.start:QN + qs.stop], wk(KN + T * t, n), start=True, stop=False, skip_group_check=True)
                    last = pe.matmul(o, work[r, QPT + T * (t // 2) + P * tt:QPT + T * (t // 2) + P * tt + P],
                                     work[r, KPT:KPT + n], start=False, stop=True, skip_group_check=True)
                last.then_inc(s("scores"), 1)
            if 1 <= t <= HEADS:
                v = t - 1
                pe.wait_ge(s("probs"), v + 1)
                if v >= 2:
                    pe.wait_ge(s("pt_read"), v - 1)
                for q in range(3):
                    last = pe.transpose(bank(4 + v % 2, P, q * P), wk(PB + 384 * (v % 2) + q * P, P), ident)
                last.then_inc(s("probs_T"), 1)
            if t >= 2:
                v = t - 2
                pe.wait_ge(s("pt_read"), v + 1)
                if v >= 2:
                    pe.wait_ge(s("at_lo"), v - 1)
                o = 6 + v % 2
                pt = wk(PT + 384 * (v % 2), 384)
                pe.matmul(bank(o, T), wk(VV + VD * v, VD), pt[:, 0:T], start=True, stop=False, skip_group_check=True)
                pe.matmul(bank(o, P, P), wk(VV + 1024 + VD * v, VD), pt[:, T:384], start=False, stop=True, skip_group_check=True)\
                    .then_inc(s("att"), 1)
        pe.wait_ge(s("at_lo"), HEADS)
        for q in range(4):
            by_token(pe, u + 10 + q, ACC, xT, [2 * q, 2 * q + 1], 2, D, 512, q == 0, q == 3).then_inc(s("used"), 1)

    def mla_act(act):
        u = U_MLA
        norm_act(act, "mla", ("ffn1_h", 1))
        operand_act(act, "mlax", "mla_T", NORM_BANKS, lambda k: col("kv_norm", k), xT)
        operand_act(act, "mlaq", "mla_T", NORM_BANKS, lambda k: col("mla_norm", k), xS, also="mlax_lo")
        for q in range(4):
            ahead_hi(act, u + q)
        act.wait_ge(s("used"), u + 4)
        for q, (b, n) in enumerate(((4, KVR), (5, KVR), (6, QR), (7, QR))):
            last = act.activation(wk(2048, n), bank(b, n), ACT.Square, accum_out=small[:, 8 + q:9 + q])
            if q < 3:
                act_step(act, last)
        last.then_inc(s("all_ssq"), 1)
        operand_act(act, "cl", "lat_T", [(0, 2)], lambda k: col("kv_latent", k), xT)
        operand_act(act, "cq", "lat_T", [(1, 2), (2, 1)], lambda k: col("q_norm", k), xS, at=1)
        act.wait_ge(s("lat_T"), 4)
        act.activation(wk(KPT, T), bank(3, T), ACT.Copy).then_inc(s("kpt"), 1)
        for q in range(4):
            ahead_hi(act, u + 4 + q)
            act.wait_ge(s("used"), u + 5 + q)
            act.activation(wk(QN + 512 * q, 512), bank(q % 2), ACT.Copy).then_inc(s("qn_read"), 1)
        for q in range(2):
            ahead_hi(act, u + 8 + q)
            act.wait_ge(s("used"), u + 9 + q)
            act.activation(wk(KN + 1024 * q, 1024), ps[:, 2:4, :].rearrange("p b n -> p (b n)"), ACT.Copy).then_inc(s("kn_read"), 1)
        act.wait_ge(s("qpe_T"), 1)
        act.activation(wk(QPT, 1024), ps[:, 0:2, :].rearrange("p b n -> p (b n)"), ACT.Copy).then_inc(s("qpt"), 1)
        for t in range(HEADS + 2):
            if t < HEADS:
                m = 32 + 8 * (t % 2)
                act.wait_ge(s("smax"), t + 1)
                if t >= 2:
                    act.wait_ge(s("probs_T"), t - 1)
                for tt, (c0, n) in enumerate(((0, P), (P, T))):
                    last = act.activation(wk(PB + 384 * (t % 2) + c0, n), wk(SM + 384 * (t % 2) + c0, n), ACT.Exp,
                                          bias=small[:, m + 2 + tt:m + 3 + tt], scale=SCALE, accum_out=small[:, m + 4 + tt:m + 5 + tt])
                last.then_inc(s("exps"), 1)
            if 1 <= t <= HEADS:
                v = t - 1
                act.wait_ge(s("probs_T"), v + 1)
                if v >= 2:
                    act.wait_ge(s("att"), v - 1)
                act.activation(wk(PT + 384 * (v % 2), 384), bank(4 + v % 2, 384), ACT.Copy).then_inc(s("pt_read"), 1)
            if t >= 2:
                v = t - 2
                act.wait_ge(s("att"), v + 1)
                act.activation(xT_hi[:, v, :], bank(6 + v % 2, T), ACT.Copy).then_inc(s("at_hi"), 1)
        for q in range(4):
            ahead_hi(act, u + 10 + q)

    def mla_dve(dve):
        u = U_MLA
        norm_dve(dve, "mla")
        operand_dve(dve, "mlax", NORM_BANKS, lambda k: col("kv_norm", k), xT)
        operand_dve(dve, "mlaq", NORM_BANKS, lambda k: col("mla_norm", k), xS)
        for q in range(4):
            ahead_lo(dve, u + q)
        dve.wait_ge(*mark("lat_ssq", 1))
        rstd_dve(dve, "lat", [(8, 2, KVR), (10, 2, QR)], 12, 4)
        for tt in range(TT):
            dve.tensor_scalar(wk(CL + 256 * tt, 256), bank(4 + tt, KVR), small[:, 16 + tt:17 + tt], None, ALU.mult)
            dve_step(dve, dve.tensor_scalar(wk(CQ + QR * tt, QR), bank(6 + tt, QR), small[:, 18 + tt:19 + tt], None, ALU.mult))
        dve.wait_ge(s("rope_tables"), 2)
        for tt in range(TT):
            kp = wk(KPE + P * tt, P).rearrange("p (g c) -> p g c", c=64)
            halves_rope(dve, bank(4 + tt, ROPE, KVR)[:, None, :], kp[:, 0:1, :], tt, 1)
            last = dve.tensor_copy(kp[:, 1, :], kp[:, 0, :])
        last.then_inc(s("latents"), 1)
        operand_dve(dve, "cl", [(0, 2)], lambda k: col("kv_latent", k), xT)
        operand_dve(dve, "cq", [(1, 2), (2, 1)], lambda k: col("q_norm", k), xS)
        for q in range(4):
            ahead_lo(dve, u + 4 + q)
        dve.wait_ge(s("used"), u + 8)
        for tt in range(TT):
            x = bank(4 + tt).rearrange("p (g c) -> p g c", c=64)
            halves_rope(dve, x, wk(QPE + 512 * tt, 512).rearrange("p (g c) -> p g c", c=64), tt, HEADS)
        dve.sem_inc(s("qpe"), 1)
        for q in range(2):
            ahead_lo(dve, u + 8 + q)
            dve.wait_ge(s("used"), u + 9 + q)
            dve.tensor_copy(wk(VV, 2048).rearrange("p (t n) -> p t n", t=2)[:, :, 512 * q:512 * q + 512], ps[:, 6:8, :])\
                .then_inc(s("v_read"), 1)
        for t in range(HEADS + 2):
            if t < HEADS:
                m = 32 + 8 * (t % 2)
                sm = wk(SM + 384 * (t % 2), 384)
                dve.wait_ge(s("scores"), t + 1)
                if t >= 2:
                    dve.wait_ge(s("exps"), t - 1)
                dve.tensor_tensor(sm, bank(2 + t % 2, 384), const("causal"), ALU.add).then_inc(s("sc_read"), 1)
                dve.wait_ge(s("sc_read"), t + 1)
                dve.tensor_reduce(small[:, m:m + 1], sm[:, 0:P], AX, ALU.max)
                dve_step(dve, dve.tensor_reduce(small[:, m + 1:m + 2], sm[:, P:384], AX, ALU.max))
                dve.tensor_scalar(small[:, m + 2:m + 4], small[:, m:m + 2], -SCALE, None, ALU.mult).then_inc(s("smax"), 1)
                dve.wait_ge(s("exps"), t + 1)
                dve_step(dve, dve.reciprocal(small[:, m + 6:m + 8], small[:, m + 4:m + 6]))
                pb = wk(PB + 384 * (t % 2), 384)
                dve.tensor_scalar(pb[:, 0:P], pb[:, 0:P], small[:, m + 6:m + 7], None, ALU.mult)
                dve.tensor_scalar(pb[:, P:384], pb[:, P:384], small[:, m + 7:m + 8], None, ALU.mult).then_inc(s("probs"), 1)
            if t >= 2:
                v = t - 2
                dve.wait_ge(s("at_hi"), v + 1)
                dve.tensor_tensor(xT_lo[:, v, :], bank(6 + v % 2, T), xT_hi[:, v, :].bitcast(F32), ALU.subtract)\
                    .then_inc(s("at_lo"), 1)
        for q in range(4):
            ahead_lo(dve, u + 10 + q)
        add_acc(dve, u + 14, "mla")

    GROW = 9216

    def end1_dve(dve):
        dve.wait_ge(*mark("end1_ssq", 1))
        rstd_dve(dve, "end1", [(0, 2, D)], 2, 2)
        dve.wait_ge(s("grow"), 16)
        for tt in range(TT):
            last = dve.scalar_tensor_tensor(h[:, tt, :], h[:, tt, :], small[:, 4 + tt:5 + tt], wk(GROW, D), ALU.mult, ALU.mult)
        last.then_inc(s("all_h"), 1)

    def square_act(act, tag, after):
        act.wait_ge(*mark(after, 1))
        for tt in range(TT):
            last = act.activation(wk(2048, D), h[:, tt, :], ACT.Square, accum_out=small[:, tt:tt + 1])
            if tt == 0:
                act_step(act, last)
            else:
                last.then_inc(s("all_ssq"), 1)

    GQ, GK, GV, SG, ZT, QK, AV = 2048, 2560, 3072, 4096, 5120, 5632, 6912
    A = [0, 1024] + [7168 + 1024 * q for q in range(7)]
    LOGIT = 7168

    def blk(q, *dims):
        return wk(A[q], 1024)

    def dpt(q):
        return wk(A[q], 1024).rearrange("p (d r t) -> p d r t", d=2, r=2)

    def chunks(q, d):
        return wk(A[q] + 512 * d, 512).rearrange("p (g c) -> p g c", c=CH)

    REF = (CH // 2 - 1, CH // 2)
    LAST = (CH - 1, 0)

    def win_pe(pe):
        u = U_WIN
        norm_pe(pe, "n1")
        pe.wait_ge(*mark("n1x_lo", 4))
        by_channel(pe, u, 0, xT)
        by_channel(pe, u + 1, 1, xT)
        for q in range(4):
            outs = [[bank(2 + 2 * (q // 2) + tt, 256, 256 * (q % 2))] for tt in range(TT)]
            by_token(pe, u + 2 + q, outs, xT, range(KD), KD, 256, 256, True, True).then_inc(s("used"), 1)
        unit_ready(pe, u + 6)
        hi, lo = weights(u + 6, KD, 160)
        for z in range(2):
            for k in range(KD):
                last = passes(pe, bank(6, T, T * z), hi[:, k, 16 * z:16 * z + P], lo[:, k, 16 * z:16 * z + P],
                              xT_hi[:, k, :], xT_lo[:, k, :], k == 0, k == KD - 1)
        last.then_inc(s("used"), 1)
        pe.wait_ge(s("gqk_read"), 1)
        for q in range(2):
            outs = [[bank(7, 256, 256 * q)], [bank(0, 256, 256 * q)]]
            by_token(pe, u + 7 + q, outs, xT, range(KD), KD, 256, 256, True, True).then_inc(s("used"), 1)
        outs = [[bank(1, 256, 256 * tt)] for tt in range(TT)]
        by_token(pe, u + 9, outs, xT, range(KD), KD, 256, 256, True, True).then_inc(s("used"), 1)
        pe.wait_ge(s("zt"), 1)
        pe.wait_ge(s("qk_read"), 1)
        for d in range(2):
            for r in range(2):
                last = pe.matmul(bank(d, T, T * r), up[0:16, d, P * r:P * r + P], work[0:16, ZT + T * d:ZT + T * d + T],
                                 start=True, stop=True, skip_group_check=True)
        last.then_inc(s("logits"), 1)
        pe.wait_ge(s("qe_ke"), 1)
        pe.wait_ge(s("sg_read"), 1)
        for d in range(2):
            for n in range(NCH):
                for r in range(2):
                    for par in range(2):
                        rows = slice(64 * par, 64 * par + 64)
                        at = 512 * d + T * r + CH * n
                        c = ((d * 2 + n // 2) * 2 + r) * CH
                        half = slice(64 * (n % 2), 64 * (n % 2) + 64)
                        last = pe.matmul(ps[half, 4 + par, c:c + CH], work[rows, A[1] + at:A[1] + at + CH],
                                         work[rows, A[0] + at:A[0] + at + CH], start=True, stop=True, skip_group_check=True)
        last.then_inc(s("gscores"), 1)
        pe.wait_ge(s("kl"), 1)
        pe.wait_ge(s("gv_read"), 1)
        for d in range(2):
            for tt in range(TT):
                for r in range(2):
                    last = pe.transpose(bank(2 + d, P, P * (2 * tt + r)), wk(A[8] + 512 * d + T * r + P * tt, P), ident)
        last.then_inc(s("kl_T"), 1)
        pe.wait_ge(s("klt"), 1)
        pe.wait_ge(s("gate_read"), 1)
        for d in range(2):
            for n in range(NCH):
                if n == (NCH - 1, 0)[d]:
                    continue
                rows = slice(64 * (n % 2), 64 * (n % 2) + 64)
                for r in range(2):
                    for par in range(2):
                        b = (6 + d) if n % 2 == 0 else d
                        c = ((n // 2) * 2 + r) * DV
                        k0 = A[6] + 512 * d + P * (2 * (n // 2) + r) + 64 * par
                        v0 = GV + 512 * (n // 2) + DV * (2 * r + par)
                        last = pe.matmul(ps[64 * par:64 * par + 64, b, c:c + DV], work[rows, k0:k0 + 64],
                                         work[rows, v0:v0 + DV], start=True, stop=True, skip_group_check=True)
        last.then_inc(s("kv"), 1)
        pe.wait_ge(s("masked"), 1)
        for tt in range(TT):
            for hd in range(GH):
                for d in range(2):
                    last = pe.matmul(bank(2 + tt, DV, DV * hd), wk(A[(3, 7)[d]] + 512 * tt + P * hd, P),
                                     wk(GV + 512 * tt + DV * hd, DV), start=d == 0, stop=d == 1, skip_group_check=True)
        last.then_inc(s("own"), 1)
        pe.wait_ge(s("states"), 1)
        for n in range(NCH):
            half = slice(64 * (n % 2), 64 * (n % 2) + 64)
            for r in range(2):
                for par in range(2):
                    rows = slice(64 * par, 64 * par + 64)
                    ds = [d for d in range(2) if n != (0, NCH - 1)[d]]
                    for d in ds:
                        q0 = A[4] + 512 * d + T * r + CH * n
                        st = A[(5, 8)[d]] + 256 * (n - 1 if d == 0 else n) + DV * r
                        c = ((n // 2) * 2 + r) * DV
                        last = pe.matmul(ps[half, 4 + par, c:c + DV], work[rows, q0:q0 + CH], work[rows, st:st + DV],
                                         start=d == ds[0], stop=d == ds[-1], skip_group_check=True)
        last.then_inc(s("past"), 1)
        pe.wait_ge(s("og"), 1)
        for hd in range(GH):
            for tt in range(TT):
                last = pe.transpose(bank(6 + hd // 2, P, (hd % 2) * T + P * tt), wk(A[6] + 512 * tt + DV * hd, P), ident)
            if hd % 2:
                last.then_inc(s("og_T"), 1)
        gqa_pe(pe)

    def win_act(act):
        u = U_WIN
        norm_act(act, "n1", ("end1_h", 1))
        operand_act(act, "n1x", "n1_T", NORM_BANKS, lambda k: col("norm1", k), xT)
        ahead_hi(act, u)
        ahead_hi(act, u + 1)
        act.wait_ge(s("used"), u + 2)
        act.activation(wk(GQ, 1024), ps[:, 0:2, :].rearrange("p b n -> p (b n)"), ACT.Copy).then_inc(s("gqk_read"), 1)
        for q in range(2, 6):
            ahead_hi(act, u + q)
        act.wait_ge(s("used"), u + 6)
        act.activation(wk(SG, 1024), ps[:, 4:6, :].rearrange("p b n -> p (b n)"), ACT.Silu).then_inc(s("sg_read"), 1)
        for q in range(6, 10):
            ahead_hi(act, u + q)
        act.wait_ge(s("used"), u + 10)
        for tt in range(TT):
            for r in range(2):
                dst = wk(QK + 640 * tt, 512).rearrange("p (i r c) -> p i r c", r=2, c=AD)[:, :, r, :]
                act.activation(dst, bank((7, 0)[tt], 256, 256 * r).rearrange("p (i c) -> p i c", c=AD), ACT.Copy)
            act.activation(wk(QK + 640 * tt + 512, P), bank(1, P, 256 * tt), ACT.Copy)
            last = act.activation(wk(AV + P * tt, P), bank(1, P, 256 * tt + P), ACT.Copy)
        last.then_inc(s("qk_read"), 1)
        act.wait_ge(s("logits"), 1)
        for d, name in enumerate(("up_f_bias", "up_b_bias")):
            for r in range(2):
                last = act.activation(dpt(2)[:, d, r, :], bank(d, T, T * r), ACT.Identity, bias=col(name, r))
        last.then_inc(s("gate_read"), 1)
        act.wait_ge(s("absx"), 1)
        act_step(act, act.activation(blk(5), blk(3), ACT.Exp, scale=-1.0))
        act.activation(blk(3), blk(5), ACT.Ln, bias=1.0).then_inc(s("softplus"), 1)
        act.wait_ge(s("d1d3"), 1)
        act.activation(blk(4), blk(2), ACT.Exp).then_inc(s("e"), 1)
        act.activation(blk(6), blk(2), ACT.Exp, scale=-1.0).then_inc(s("e"), 1)
        act.activation(blk(7), blk(3), ACT.Exp).then_inc(s("e"), 1)
        act.wait_ge(s("e"), 3)
        act.activation(blk(2), blk(5), ACT.Exp).then_inc(s("e"), 1)
        act.wait_ge(s("kl_T"), 1)
        act.activation(blk(6), ps[:, 2:4, :].rearrange("p b n -> p (b n)"), ACT.Copy).then_inc(s("klt"), 1)
        act.wait_ge(s("past"), 1)
        act.activation(blk(0), ps[:, 4:6, :].rearrange("p b n -> p (b n)"), ACT.Copy).then_inc(s("past_read"), 1)
        act.wait_ge(s("osum"), 1)
        for q in range(8):
            last = act.activation(wk(A[2] + P * q, P), wk(A[1] + P * q, P), ACT.Square, accum_out=small[:, 64 + q:65 + q])
        last.then_inc(s("all_ssq"), 1)
        operand_act(act, "og", "og_T", [(6, 2), (7, 2)], lambda k: col("gla_out"), xT)
        gqa_act(act)
        for q in range(1):
            ahead_hi_last(act)

    def ahead_hi_last(act):
        split_hi(act, U_WOUT + 3, UNIT)

    def win_dve(dve):
        u = U_WIN
        norm_dve(dve, "n1")
        operand_dve(dve, "n1x", NORM_BANKS, lambda k: col("norm1", k), xT)
        for q in range(4):
            ahead_lo(dve, u + q)
        dve.wait_ge(s("used"), u + 4)
        dve.tensor_copy(wk(GV, 1024), ps[:, 2:4, :].rearrange("p b n -> p (b n)")).then_inc(s("gv_read"), 1)
        for q in range(4, 7):
            ahead_lo(dve, u + q)
        dve.wait_ge(s("used"), u + 7)
        dve.tensor_copy(work[0:16, ZT:ZT + 512], ps[0:16, 6, :]).then_inc(s("zt"), 1)
        for q in range(7, 10):
            ahead_lo(dve, u + q)
        dve.wait_ge(s("gate_read"), 1)
        dve.wait_ge(s("gqk_read"), 1)
        dve.tensor_scalar(blk(4), blk(2), 0.0, 1.0 / 16, ALU.min, ALU.mult)
        dve_step(dve, dve.tensor_scalar(blk(3), blk(2), -1.0, None, ALU.mult))
        dve.tensor_tensor(blk(3), blk(3), blk(2), ALU.max).then_inc(s("absx"), 1)
        dve.tensor_scalar(wk(GQ, 512), wk(GQ, 512), DK ** -0.5, None, ALU.mult)
        dve.wait_ge(s("softplus"), 1)
        dve_step(dve, dve.scalar_tensor_tensor(blk(2), blk(3), -1.0 / 16, blk(4), ALU.mult, ALU.add))
        for g in range(2 * NCH):
            dve.tensor_tensor_scan(chunks(5, 0)[:, g, :], const("ones")[:, 0:CH], chunks(2, 0)[:, g, :], 0.0, ALU.mult, ALU.add)
            last = dve.tensor_tensor_scan(chunks(4, 1)[:, g, :], const("ones")[:, 0:CH], chunks(2, 1)[:, g, :], 0.0, ALU.mult, ALU.add)
        dve_step(dve, last)
        for g in range(2 * NCH):
            last = dve.scalar_tensor_tensor(chunks(5, 1)[:, g, :], chunks(2, 1)[:, g, :], chunks(4, 1)[:, g, CH - 1:CH],
                                            chunks(4, 1)[:, g, :], ALU.add, ALU.subtract)
        dve_step(dve, last)
        for d in range(2):
            b = chunks(5, d)
            dve.tensor_tensor(chunks(2, d), b, b[:, :, REF[d]:REF[d] + 1].broadcast_to([P, 2 * NCH, CH]), ALU.subtract)
            last = dve.tensor_tensor(chunks(3, d), b[:, :, LAST[d]:LAST[d] + 1].broadcast_to([P, 2 * NCH, CH]), b, ALU.subtract)
        last.then_inc(s("d1d3"), 1)
        dve.wait_ge(s("e"), 1)
        for d in range(2):
            dve.tensor_tensor(wk(A[0] + 512 * d, 512), wk(GQ, 512), wk(A[4] + 512 * d, 512), ALU.mult)
        dve.wait_ge(s("e"), 2)
        for d in range(2):
            last = dve.tensor_tensor(wk(A[1] + 512 * d, 512), wk(GK, 512), wk(A[6] + 512 * d, 512), ALU.mult)
        last.then_inc(s("qe_ke"), 1)
        dve.wait_ge(s("e"), 3)
        for d in range(2):
            last = dve.tensor_tensor(wk(A[8] + 512 * d, 512), wk(GK, 512), wk(A[7] + 512 * d, 512), ALU.mult)
        last.then_inc(s("kl"), 1)
        dve.wait_ge(s("kl"), 1)
        dve.memset(blk(7), 0.0)
        dve.wait_ge(s("e"), 4)
        dve_step(dve, dve.memset(blk(3), 0.0))
        for d in range(2):
            last = dve.tensor_tensor(wk(A[4] + 512 * d, 512), wk(GQ, 512), wk(A[2] + 512 * d, 512), ALU.mult)
        dve_step(dve, last)
        dve.wait_ge(s("gscores"), 1)
        for d in range(2):
            for half in range(2):
                rows = slice(64 * half, 64 * half + 64)
                at = CONST["keep_b" if d else "keep_f"][0]
                mask = cst[rows, at:at + 64].bitcast(U32)[:, None, :].broadcast_to([64, 4, 64])
                for par in range(2):
                    dst = work[rows, A[(3, 7)[d]]:A[(3, 7)[d]] + 1024].rearrange("p (g c) -> p g c", c=2 * P)[:, :, par * P + 64 * half:par * P + 64 * half + 64]
                    src = ps[rows, 4 + par, 256 * d:256 * d + 256].rearrange("p (g c) -> p g c", c=64)
                    last = dve.copy_predicated(dst, mask, src)
        last.then_inc(s("masked"), 1)
        dve.wait_ge(s("kv"), 1)
        dve.wait_ge(s("kl_T"), 1)

        def added(d, n, r):
            return bank((6 + d) if n % 2 == 0 else d, DV, ((n // 2) * 2 + r) * DV)

        for q in range(3):
            for d in range(2):
                n = q + 1 if d == 0 else 2 - q
                m = n - 1 if d == 0 else n + 1
                for r in range(2):
                    dst = wk(A[(5, 8)[d]] + 256 * (n - 1 if d == 0 else n) + DV * r, DV)
                    if q == 0:
                        last = dve.tensor_copy(dst, added(d, m, r))
                    else:
                        prev = wk(A[(5, 8)[d]] + 256 * (m - 1 if d == 0 else m) + DV * r, DV)
                        at = A[2] + 512 * d + T * r + CH * m + LAST[d]
                        last = dve.scalar_tensor_tensor(dst, prev, work[:, at:at + 1], added(d, m, r), ALU.mult, ALU.add)
            if q < 2:
                dve_step(dve, last)
        last.then_inc(s("states"), 1)
        dve.wait_ge(s("past_read"), 1)
        dve.wait_ge(s("own"), 1)
        for tt in range(TT):
            for par in range(2):
                o = lambda v: v.rearrange("p (r q c) -> p r q c", q=2, c=DV)[:, :, par, :]
                last = dve.tensor_tensor(o(wk(A[1] + 512 * tt, 512)), o(bank(2 + tt)),
                                         wk(A[0] + 512 * par + 256 * tt, 256).rearrange("p (r c) -> p r c", c=DV), ALU.add)
        last.then_inc(s("osum"), 1)
        dve.wait_ge(*mark("g_ssq", 1))
        rstd_dve(dve, "g", [(64, 8, DV)], 72, 8)
        for q in range(8):
            last = dve.scalar_tensor_tensor(wk(A[6] + P * q, P), wk(A[1] + P * q, P), small[:, 80 + q:81 + q],
                                            wk(SG + P * q, P), ALU.mult, ALU.mult)
        last.then_inc(s("og"), 1)
        operand_dve(dve, "og", [(6, 2), (7, 2)], lambda k: col("gla_out"), xT)
        gqa_dve(dve)
        split_lo(dve, U_WOUT + 3, UNIT)
        add_acc(dve, U_WOUT + 4, "mix")

    SQ, T1, T2, QR2 = 0, 0, 7168, 7168 + 1280
    QT, KT, PB2, PT2 = 9728, 10752, 11008, 12032
    OA, ON = 0, 1024

    def slot(hd):
        return hd % 4, hd // 4

    def gqa_pe(pe):
        pe.wait_ge(s("qk"), 1)
        pe.wait_ge(s("past_read"), 1)
        for c in range(4):
            for tt in range(TT):
                last = pe.transpose(bank(c // 2, P, (c % 2) * T + P * tt), wk(QR2 + 640 * tt + P * c, P), ident)
        last.then_inc(s("aqT"), 1)
        for tt in range(TT):
            last = pe.transpose(bank(2, P, P * tt), wk(QR2 + 640 * tt + 512, P), ident)
        last.then_inc(s("akT"), 1)
        pe.wait_ge(s("akt"), 1)
        pe.wait_ge(*mark("og_lo", 2))
        for t in range(AH + 2):
            if t < AH:
                c, par = slot(t)
                rows = slice(64 * par, 64 * par + 64)
                if t >= 2:
                    pe.wait_ge(s("aexps"), t - 1)
                for tt in range(TT):
                    last = pe.matmul(bank(2 + t % 2, T, T * tt), work[rows, QT + T * c + P * tt:QT + T * c + P * tt + P],
                                     work[rows, KT:KT + T], start=True, stop=True, skip_group_check=True)
                last.then_inc(s("ascores"), 1)
            if 1 <= t <= AH:
                v = t - 1
                pe.wait_ge(s("aexps"), v + 1)
                if v >= 2:
                    pe.wait_ge(s("apt_read"), v - 1)
                for kk in range(TT):
                    for tt in range(TT):
                        last = pe.transpose(bank(4 + v % 2, P, T * kk + P * tt), wk(PB2 + 512 * (v % 2) + T * tt + P * kk, P), ident)
                last.then_inc(s("aprobs_T"), 1)
            if t >= 2:
                v = t - 2
                pe.wait_ge(s("apt_read"), v + 1)
                for tt in range(TT):
                    for kk in range(TT):
                        last = pe.matmul(bank(6 + tt, AD, AD * v), wk(PT2 + 512 * (v % 2) + T * kk + P * tt, P),
                                         wk(AV + P * kk + AD * (v // 4), AD), start=kk == 0, stop=kk == 1, skip_group_check=True)
                last.then_inc(s("aatt"), 1)
        pe.wait_ge(s("on"), 1)
        for c in range(4):
            for tt in range(TT):
                last = pe.transpose(bank(c // 2, P, (c % 2) * T + P * tt), wk(ON + 512 * tt + P * c, P), ident)
            if c % 2:
                last.then_inc(s("on_T"), 1)
        pe.wait_ge(*mark("mo_lo", 2))
        for q in range(4):
            by_token(pe, U_WOUT + q, ACC, xT, [2 * q, 2 * q + 1], 2, D, 512, q == 0, q == 3).then_inc(s("used"), 1)

    def gqa_act(act):
        act.wait_ge(s("aqT"), 1)
        act.activation(wk(QT, 1024), ps[:, 0:2, :].rearrange("p b n -> p (b n)"), ACT.Copy)
        act.wait_ge(s("akT"), 1)
        act.activation(wk(KT, T), bank(2, T), ACT.Copy).then_inc(s("akt"), 1)
        for t in range(AH + 1):
            if t < AH:
                m = 128 + 4 * t
                act.wait_ge(s("amax"), t + 1)
                if t >= 2:
                    act.wait_ge(s("aprobs_T"), t - 1)
                for tt in range(TT):
                    last = act.activation(wk(PB2 + 512 * (t % 2) + T * tt, T), bank(2 + t % 2, T, T * tt), ACT.Exp,
                                          bias=small[:, m + tt:m + tt + 1], scale=AD ** -0.5,
                                          accum_out=small[:, m + 2 + tt:m + 3 + tt])
                last.then_inc(s("aexps"), 1)
            if t >= 1:
                v = t - 1
                act.wait_ge(s("aprobs_T"), v + 1)
                if v >= 2:
                    act.wait_ge(s("aatt"), v - 1)
                act.activation(wk(PT2 + 512 * (v % 2), 512), bank(4 + v % 2), ACT.Copy).then_inc(s("apt_read"), 1)
        act.wait_ge(s("oa"), 1)
        for tt in range(TT):
            last = act.activation(wk(7168 + 512 * tt, 512), wk(OA + 512 * tt, 512), ACT.Square, accum_out=small[:, 164 + tt:165 + tt])
        last.then_inc(s("all_ssq"), 1)
        operand_act(act, "mo", "on_T", [(0, 2), (1, 2)], lambda k: col("att_out", k), xT, first=4)

    def gqa_dve(dve):
        qk = wk(QK, 1280)
        groups = lambda at: wk(at, 1280).rearrange("p (g c) -> p g c", c=AD)
        dve_step(dve, dve.tensor_tensor(wk(SQ, 1280 - 256), qk[:, 0:1024], qk[:, 0:1024], ALU.mult))
        dve_step(dve, dve.tensor_tensor(wk(7168, 256), qk[:, 1024:1280], qk[:, 1024:1280], ALU.mult))
        dve.tensor_reduce(small[:, 88:104], wk(SQ, 1024).rearrange("p (g c) -> p g c", c=AD), AX, ALU.add)
        dve_step(dve, dve.tensor_reduce(small[:, 104:108], wk(7168, 256).rearrange("p (g c) -> p g c", c=AD), AX, ALU.add))
        rstd_dve(dve, "qkn", [(88, 20, AD)], 170, 20)
        r = small[:, 190:210][:, :, None].broadcast_to([P, 20, AD])
        dve_step(dve, dve.tensor_tensor(groups(QK), groups(QK), r, ALU.mult))
        dve.wait_ge(s("rowp"), 16 * 4)
        for tt in range(TT):
            for g0, n, at in ((0, 8, 0), (8, 2, 64)):
                v = groups(QK)[:, 10 * tt + g0:10 * tt + g0 + n, :]
                last = dve.tensor_tensor(v, v, rowp[:, at:at + 64][:, None, :].broadcast_to([P, n, AD]), ALU.mult)
        dve_step(dve, last)
        for tt in range(TT):
            x = wk(QK + 640 * tt, 640).rearrange("p (g c e) -> p g c e", e=2, c=32)
            o = wk(QR2 + 640 * tt, 640).rearrange("p (g c e) -> p g c e", e=2, c=32)
            c0, s0 = CONST["ax_cos"][0] + 32 * tt, CONST["ax_sin"][0] + 32 * tt
            cos = cst[:, c0:c0 + 32][:, None, :].broadcast_to([P, 10, 32])
            sin = cst[:, s0:s0 + 32][:, None, :].broadcast_to([P, 10, 32])
            t = [wk(at, 320).rearrange("p (g c) -> p g c", c=32) for at in (T1, T1 + 320, T2, T2 + 320)]
            dve.tensor_tensor(t[0], x[:, :, :, 0], cos, ALU.mult)
            dve.tensor_tensor(t[1], x[:, :, :, 1], sin, ALU.mult)
            dve.tensor_tensor(t[2], x[:, :, :, 0], sin, ALU.mult)
            dve_step(dve, dve.tensor_tensor(t[3], x[:, :, :, 1], cos, ALU.mult))
            dve.tensor_tensor(o[:, :, :, 0], t[0], t[1], ALU.subtract)
            dve_step(dve, dve.tensor_tensor(o[:, :, :, 1], t[2], t[3], ALU.add))
        dve.sem_inc(s("qk"), 1)
        for t in range(AH):
            m = 128 + 4 * t
            dve.wait_ge(s("ascores"), t + 1)
            dve_step(dve, dve.tensor_reduce(small[:, 210 + 2 * t:212 + 2 * t], bank(2 + t % 2).rearrange("p (t n) -> p t n", t=2), AX, ALU.max))
            dve.tensor_scalar(small[:, m:m + 2], small[:, 210 + 2 * t:212 + 2 * t], -(AD ** -0.5), None, ALU.mult).then_inc(s("amax"), 1)
        dve.wait_ge(s("aatt"), AH)
        sums = small[:, 128:160].rearrange("p (h c) -> p h c", c=4)[:, :, 2:4]
        inv = small[:, 112:128].rearrange("p (h c) -> p h c", c=2)
        dve_step(dve, dve.reciprocal(inv, sums))
        for tt in range(TT):
            last = dve.tensor_tensor(wk(OA + 512 * tt, 512).rearrange("p (h c) -> p h c", c=AD),
                                     bank(6 + tt).rearrange("p (h c) -> p h c", c=AD),
                                     inv[:, :, tt:tt + 1].broadcast_to([P, AH, AD]), ALU.mult)
        last.then_inc(s("oa"), 1)
        dve.wait_ge(*mark("a_ssq", 1))
        rstd_dve(dve, "a", [(164, 2, 512)], 166, 2)
        for tt in range(TT):
            last = dve.tensor_scalar(wk(ON + 512 * tt, 512), wk(OA + 512 * tt, 512), small[:, 168 + tt:169 + tt], None, ALU.mult)
        last.then_inc(s("on"), 1)
        operand_dve(dve, "mo", [(0, 2), (1, 2)], lambda k: col("att_out", k), xT, first=4)

    XN2, NROW, FROW, XT2 = 0, 3072, 4096, 5120
    LG, EL, EM = 7168, 7328, 7456
    ONE = 7584
    AA, RK, RANK, TMP = 7840, 7968, 8096, 8240
    GS, US, SI, AP_, YT, YS = 8448, 8960, 9472, 9728, 9984, 11008
    CR, CE, CW, CIN, CUP, CROW, CWR = 120, 224, 228, 232, 236, 240, 244
    x_rows = [v[:, :, :].rearrange("p k t -> p (k t)") for v in xS]
    xstat = [xT_hi[:, 4 * b:4 * b + 4, :].rearrange("p k t -> p (k t)").rearrange("p (k m) -> p k m", m=P) for b in range(2)]
    astat = xT_lo[:, 0:2, :].rearrange("p k t -> p (k t)").rearrange("p (k m) -> p k m", m=P)

    def router_pe(pe):
        norm_pe(pe, "n2")
        pe.wait_ge(s("xt2"), 4)
        for tt in range(TT):
            for k in range(KD):
                last = pe.matmul(bank(4 + tt, NG + NE), wk(XT2 + T * k + P * tt, P), wr[:, k, :], start=k == 0, stop=k == KD - 1,
                                 skip_group_check=True)
        last.then_inc(s("rlogits"), 1)
        pe.wait_ge(s("choices"), 1)
        a0, a1 = wk(AA, NE), wk(AA + NE, NE)
        pe.matmul(bank(6, NE), const("before"), a0, start=True, stop=True, skip_group_check=True)
        pe.matmul(bank(6, NE, NE), const("ones"), a0, start=True, stop=False, skip_group_check=True)
        pe.matmul(bank(6, NE, NE), const("before"), a1, start=False, stop=True, skip_group_check=True)
        pe.matmul(bank(6, NE, 2 * NE), const("ones"), a0, start=True, stop=False, skip_group_check=True)
        pe.matmul(bank(6, NE, 2 * NE), const("ones"), a1, start=False, stop=True, skip_group_check=True).then_inc(s("ranks"), 1)

    def router_act(act):
        square_act(act, "n2", "mix_h")
        act.wait_ge(*mark("n2_xn", TT))
        act.activation(x_rows[0], wk(XN2, 2048), ACT.Copy).then_inc(s("rows_hi"), 1)
        for b in range(4):
            act.wait_ge(*mark("n2_T", b + 1))
            act.activation(wk(XT2 + 512 * b, 512), bank(b), ACT.Copy).then_inc(s("xt2"), 1)
        for tt in range(TT):
            m = 40 * tt
            act.wait_ge(s("gmax"), tt + 1)
            act.activation(wk(TMP + 16 * tt, NG), wk(LG + 72 * tt, NG), ACT.Exp, bias=small[:, m + 8:m + 9],
                           accum_out=small[:, m + 9:m + 10]).then_inc(s("gsum"), 1)
        for tt in range(TT):
            m = 40 * tt
            act.wait_ge(s("vdiff"), tt + 1)
            act.activation(small[:, m + 31:m + 32], small[:, m + 30:m + 31], ACT.Exp).then_inc(s("vexp"), 1)

    def router_dve(dve):
        dve.wait_ge(*mark("n2_ssq", 1))
        rstd_dve(dve, "n2", [(0, 2, D)], 2, 2)
        dve.wait_ge(s("rows_loaded"), 32)
        for tt in range(TT):
            dve.scalar_tensor_tensor(wk(XN2 + D * tt, D), h[:, tt, :], small[:, 4 + tt:5 + tt], wk(NROW, D), ALU.mult, ALU.mult)\
                .then_inc(s("all_xn"), 1)
        dve.wait_ge(s("rows_hi"), 1)
        dve.tensor_tensor(x_rows[1], wk(XN2, 2048), x_rows[0].bitcast(F32), ALU.subtract).then_inc(s("rows_lo"), 1)
        dve.wait_ge(s("rlogits"), 1)
        iota = const("iota")
        for tt in range(TT):
            m = 40 * tt
            lg = wk(LG + 72 * tt, 72)
            dve_step(dve, dve.tensor_tensor(lg, bank(4 + tt, NG + NE), rowp[:, 128:200], ALU.add))
            dve_step(dve, dve.max(small[:, m:m + 8], lg[:, 0:NG]))
            dve.tensor_scalar(small[:, m + 8:m + 9], small[:, m:m + 1], -1.0, None, ALU.mult).then_inc(s("gmax"), 1)
            dve_step(dve, dve.max_index(top_i[:, 16 * tt:16 * tt + 8], small[:, m:m + 8], lg[:, 0:NG]))
            dve_step(dve, dve.tensor_copy(small[:, m + 24:m + 25], top_i[:, 16 * tt:16 * tt + 1]))
            dve_step(dve, dve.tensor_scalar(wk(TMP + 32 + 8 * tt, 8), iota[:, 0:NG], small[:, m + 24:m + 25], None, ALU.is_equal))
            em = wk(EM + 64 * tt, 64)
            dve_step(dve, dve.tensor_tensor(em.rearrange("p (j g) -> p j g", g=NG), lg[:, NG:72].rearrange("p (g j) -> p j g", g=NG),
                                            wk(TMP + 32 + 8 * tt, 8)[:, None, :].broadcast_to([P, EPG, NG]), ALU.mult))
            el = wk(EL + 8 * tt, 8)
            dve_step(dve, dve.tensor_reduce(el, em.rearrange("p (j g) -> p j g", g=NG), AX, ALU.add))
            dve_step(dve, dve.max(small[:, m + 16:m + 24], el))
            dve_step(dve, dve.max_index(top_i[:, 16 * tt + 8:16 * tt + 16], small[:, m + 16:m + 24], el))
            dve_step(dve, dve.tensor_copy(small[:, m + 26:m + 28], top_i[:, 16 * tt + 8:16 * tt + 10]))
            dve_step(dve, dve.scalar_tensor_tensor(small[:, m + 28:m + 30], small[:, m + 24:m + 25].broadcast_to([P, 2]), float(EPG),
                                                   small[:, m + 26:m + 28], ALU.mult, ALU.add))
            dve.tensor_tensor(small[:, m + 30:m + 31], small[:, m + 17:m + 18], small[:, m + 16:m + 17], ALU.subtract).then_inc(s("vdiff"), 1)
            for c in range(2):
                last = dve.tensor_scalar(wk(ONE + 128 * tt + 64 * c, 64), iota, small[:, m + 28 + c:m + 29 + c], None, ALU.is_equal)
            dve_step(dve, last)
            last = dve.tensor_tensor(wk(AA + 64 * tt, 64), wk(ONE + 128 * tt, 64), wk(ONE + 128 * tt + 64, 64), ALU.add)
            if tt == 0:
                dve_step(dve, last)
        last.then_inc(s("choices"), 1)
        dve.wait_ge(s("gsum"), 2)
        dve.wait_ge(s("vexp"), 2)
        for tt in range(TT):
            m = 40 * tt
            dve_step(dve, dve.tensor_scalar(small[:, m + 32:m + 33], small[:, m + 31:m + 32], 1.0, None, ALU.add))
            dve_step(dve, dve.reciprocal(small[:, m + 33:m + 34], small[:, m + 32:m + 33]))
            dve_step(dve, dve.reciprocal(small[:, m + 34:m + 35], small[:, m + 9:m + 10]))
            dve_step(dve, dve.tensor_tensor(small[:, m + 36:m + 37], small[:, m + 33:m + 34], small[:, m + 34:m + 35], ALU.mult))
            dve_step(dve, dve.tensor_tensor(small[:, m + 37:m + 38], small[:, m + 36:m + 37], small[:, m + 31:m + 32], ALU.mult))
        dve.wait_ge(s("ranks"), 1)
        dve_step(dve, dve.tensor_copy(wk(RK, 128), bank(6, 128)))
        for tt in range(TT):
            m = 40 * tt
            for c in range(2):
                t = wk(TMP + 64, 64)
                dve_step(dve, dve.tensor_tensor(t, wk(ONE + 128 * tt + 64 * c, 64), wk(RK + 64 * tt, 64), ALU.mult))
                dve_step(dve, dve.tensor_reduce(small[:, CR + 2 * tt + c:CR + 1 + 2 * tt + c], t, AX, ALU.add))
            dve.tensor_copy(small[:, CE + 2 * tt:CE + 2 + 2 * tt], small[:, m + 28:m + 30])
            dve.tensor_copy(small[:, CW + 2 * tt:CW + 2 + 2 * tt], small[:, m + 36:m + 38])
            t = wk(TMP + 64, 64)
            dve_step(dve, dve.scalar_tensor_tensor(t, wk(RK + 64 * tt, 64), 1.0, wk(AA + 64 * tt, 64), ALU.add, ALU.mult))
            dve_step(dve, dve.tensor_scalar(wk(RANK + NE * tt, NE), t, -1.0, None, ALU.add))
        dve_step(dve, dve.tensor_reduce(small[:, 130:131], bank(6, NE, 2 * NE), AX, ALU.max))
        for q in range(3):
            last = dve.tensor_scalar(small[:, 131 + q:132 + q], small[:, 130:131], float(CAP * (q + 1)), None, ALU.is_gt)
        dve_step(dve, last)
        dve_step(dve, dve.tensor_reduce(small[:, 134:135], small[:, 131:134], AX, ALU.add))
        dve_step(dve, dve.tensor_scalar(small[:, 135:136], small[:, 134:135], 1.0, None, ALU.add))
        dve.tensor_copy(rounds_i[:, :], small[:, 135:136]).then_inc(s("rounds"), 1)

    MU = U_MOE
    STEP = U_MOE + 4
    assert NE % 2 == 0 and RAW == 6

    def rounds_of(eng):
        eng.wait_ge(s("rounds"), 1)
        return eng.value_load(rounds_i[0:1, 0:1], min_val=1, max_val=T // CAP)

    def expert_steps(eng, r, step):
        with eng.Fori(0, NE // 2 - 1) as i:
            for p in range(2):
                step(i * 2 + (1 + p), r * NE + i * 2 + (1 + p), r * NE + i * 2 + p, (1 + p) % 2, False)
        step(NE - 1, r * NE + (NE - 1), r * NE + (NE - 2), (NE - 1) % 2, True)

    def moe_sp(sp):
        n = rounds_of(sp)
        with sp.Fori(0, n) as r:
            for q in range(4):
                load(sp, MU + q, moe_unit(q, 0), r * NE)
            with sp.Fori(0, NE - 1) as i:
                for q in range(6):
                    load(sp, MU + 4 + q, moe_unit(q, i + 1 if q < 4 else i), r * NE + i)
            for q in range(2):
                load(sp, MU + 4 + q, moe_unit(4 + q, NE - 1), r * NE + (NE - 1))

    def moe_pe(pe):
        pe.wait_ge(s("rows_lo"), 1)

        def products(u, g, out_bank, stat, first, last_half):
            unit_ready(pe, u, g)
            hi, lo = weights(u, 4, 512)
            for k in range(4):
                st = stat(k)
                pe.matmul(bank(out_bank), st, hi[:, k, :], start=first and k == 0, stop=False, skip_group_check=True)
                last = pe.matmul(bank(out_bank), st, lo[:, k, :], start=False, stop=last_half and k == 3, skip_group_check=True)
            last.then_inc(s("used"), 1)

        def up_like(u, g, out_bank, par, q):
            products(u, g, out_bank, lambda k: xstat[par][:, 4 * q + k, :], q == 0, q == 1)

        def gather(E, ks):
            if ks[0] == 0:
                pe.wait_ge(s("sel"), E + 1)
            for k in ks:
                for part in range(2):
                    for tt in range(TT):
                        last = pe.matmul(bank(2 + k // 4, CAP, (k % 4) * P + CAP * part),
                                         x_rows[part][:, D * tt + P * k:D * tt + P * k + P], sel[:, tt, :],
                                         start=tt == 0, stop=tt == 1, skip_group_check=True)
                if k == 3:
                    last.then_inc(s("x_first"), 1)
                if k == 7:
                    last.then_inc(s("x_second"), 1)

        def fold_g(E):
            pe.wait_ge(s("g_read"), E + 1)
            for k in range(4):
                last = pe.matmul(bank(4, CAP, CAP * k), wk(GS + P * k, P), const("fold"),
                                 start=True, stop=True, skip_group_check=True)
            last.then_inc(s("g_T"), 1)

        def fold_u(E):
            pe.wait_ge(s("u_read"), E + 1)
            for k in range(4):
                last = pe.matmul(bank(7, CAP, CAP * k), wk(US + P * k, P), const("fold"),
                                 start=True, stop=True, skip_group_check=True)
            last.then_inc(s("u_T"), 1)

        def down(u, g, q):
            products(u + q, g, 5 + q, lambda k: astat[:, k, :], True, True)

        def step(e, E, g, par, last):
            pe.wait_ge(s("xa"), E + 1)
            pe.wait_ge(s("xd"), E + 1)
            up_like(STEP, g, 0, par, 0)
            fold_u(g)
            up_like(STEP + 1, g, 0, par, 1)
            if not last:
                gather(E + 1, (0, 1))
            up_like(STEP + 2, g, 1, par, 0)
            pe.wait_ge(s("si"), E)
            fold_g(E)
            up_like(STEP + 3, g, 1, par, 1)
            if not last:
                gather(E + 1, (2, 3, 4, 5))
            pe.wait_ge(s("a_lo"), E)
            down(STEP + 4, g, 0)
            if not last:
                gather(E + 1, (6, 7))
            down(STEP + 4, g, 1)

        n = rounds_of(pe)
        with pe.Fori(0, n) as r:
            g = r * NE
            gather(g, range(KD))
            pe.wait_ge(s("xa"), g + 1)
            pe.wait_ge(s("xd"), g + 1)
            for q in range(2):
                up_like(MU + q, g, 0, 0, q)
            gather(g + 1, (0, 1, 2, 3))
            up_like(MU + 2, g, 1, 0, 0)
            fold_g(g)
            up_like(MU + 3, g, 1, 0, 1)
            gather(g + 1, (4, 5, 6, 7))
            expert_steps(pe, r, step)
            fold_u(g + (NE - 1))
            pe.wait_ge(s("a_lo"), g + NE)
            for q in range(2):
                down(MU + 4, g + (NE - 1), q)

    def moe_act(act):
        act.wait_ge(s("rows_hi"), 1)
        act.activation(small[:, 250:251], cst[:, 0:1], ACT.Silu)
        n = rounds_of(act)

        def x_half(E, par):
            act.wait_ge(s("x_first"), E + 1)
            act.activation(xstat[par][:, 0:4, :].rearrange("p k m -> p (k m)"), bank(2), ACT.Copy).then_inc(s("xa"), 1)

        def g_out(u, g):
            act.wait_ge(s("used"), num(u + 1, g))
            act.activation(wk(GS, 512), bank(0), ACT.Copy).then_inc(s("g_read"), 1)

        def u_out(u, g):
            act.wait_ge(s("used"), num(u + 1, g))
            act.activation(wk(US, 512), bank(1), ACT.Copy).then_inc(s("u_read"), 1)

        def silu(E):
            act.wait_ge(s("g_T"), E + 1)
            act.activation(wk(SI, 256), bank(4, 256), ACT.Silu).then_inc(s("si"), 1)

        def a_hi(E):
            act.wait_ge(s("a_mul"), E + 1)
            act.activation(astat[:, :, 0:CAP], wk(AP_, 256).rearrange("p (k m) -> p k m", k=4), ACT.Copy).then_inc(s("a_hi"), 1)

        def y_low(u, g, q):
            act.wait_ge(s("used"), num(u + q + 1, g))
            act.activation(work[0:CAP, YT + 512 * q:YT + 512 * q + 512], ps[CAP:P, 5 + q, :], ACT.Copy).then_inc(s("y_low"), 1)

        def step(e, E, g, par, last):
            u = STEP
            split_hi(act, u + 3, UNIT, g)
            g_out(u + 1, g)
            a_hi(g)
            split_hi(act, u + 4, UNIT, g)
            split_hi(act, u + 5, UNIT, g)
            silu(E)
            u_out(u + 3, g)
            split_hi(act, u + 6, UNIT, g)
            if not last:
                x_half(E + 1, 1 - par)
            y_low(u + 4, g, 0)
            split_hi(act, u + 7, UNIT, g)
            y_low(u + 4, g, 1)
            if not last:
                split_hi(act, u + 8, UNIT, g)

        with act.Fori(0, n) as r:
            g = r * NE
            for q in range(3):
                split_hi(act, MU + q, UNIT, g)
            x_half(g, 0)
            split_hi(act, MU + 3, UNIT, g)
            g_out(MU + 1, g)
            split_hi(act, MU + 4, UNIT, g)
            split_hi(act, MU + 5, UNIT, g)
            silu(g)
            u_out(MU + 3, g)
            x_half(g + 1, 1)
            split_hi(act, MU + 6, UNIT, g)
            expert_steps(act, r, step)
            a_hi(g + (NE - 1))
            for q in range(2):
                y_low(MU + 4, g + (NE - 1), q)

    def moe_dve(dve):
        n = rounds_of(dve)

        def select(e, E, first=False):
            if not first:
                dve.wait_ge(s("x_second"), E)
            for tt in range(TT):
                if isinstance(e, int):
                    rank = wk(RANK + NE * tt + e, 1)
                else:
                    rank = work[:, bass.ds(e + (RANK + NE * tt), 1)]
                last = dve.tensor_scalar(sel[:, tt, :], const("iota"), rank, None, ALU.is_equal)
            last.then_inc(s("sel"), 1)

        def x_half(E, par):
            dve.wait_ge(s("x_second"), E + 1)
            dve.tensor_copy(xstat[par][:, 4:8, :].rearrange("p k m -> p (k m)"), bank(3)).then_inc(s("xd"), 1)

        def a_mul(E):
            dve.wait_ge(s("si"), E + 1)
            dve.wait_ge(s("u_T"), E + 1)
            dve.tensor_tensor(wk(AP_, 256), bank(7, 256), wk(SI, 256), ALU.mult).then_inc(s("a_mul"), 1)

        def a_lo(E):
            dve.wait_ge(s("a_hi"), E + 1)
            dve.tensor_tensor(astat[:, :, CAP:P], wk(AP_, 256).rearrange("p (k m) -> p k m", k=4),
                              astat[:, :, 0:CAP].bitcast(F32), ALU.subtract).then_inc(s("a_lo"), 1)

        def y_sum(E, q):
            if q == 0:
                dve.wait_ge(s("y_room"), E + 1)
            dve.wait_ge(s("y_low"), E * 2 + (q + 1))
            dve.tensor_tensor(work[0:CAP, YS + 512 * q:YS + 512 * q + 512], ps[0:CAP, 5 + q, :],
                              work[0:CAP, YT + 512 * q:YT + 512 * q + 512], ALU.add).then_inc(s("y_sum"), 1)

        def round_step(r, q, ins):
            ins.then_inc(s("round_steps"), 1)
            dve.wait_ge(s("round_steps"), r * ROUND_STEPS + (q + 1))

        def choices_in_round(r):
            c = lambda at: small[:, at:at + 4]
            round_step(r, 0, dve.tensor_scalar(c(CIN), c(CR), 0.0, None, ALU.is_ge))
            round_step(r, 1, dve.tensor_scalar(c(CUP), c(CR), float(CAP), None, ALU.is_lt))
            round_step(r, 2, dve.tensor_tensor(c(CIN), c(CIN), c(CUP), ALU.mult))
            round_step(r, 3, dve.tensor_tensor(c(CUP), c(CIN), c(CR), ALU.mult))
            round_step(r, 4, dve.scalar_tensor_tensor(c(CROW), c(CE), float(CAP), c(CUP), ALU.mult, ALU.add))
            round_step(r, 5, dve.tensor_tensor(c(CWR), c(CW), c(CIN), ALU.mult))
            dve.tensor_copy(slot_i[:, :], c(CROW)).then_inc(s("slots"), 1)

        def add_rows(r):
            for tt in range(TT):
                for c in range(2):
                    q = 2 * tt + c
                    dve.wait_ge(s(f"gathered{q}"), r * 16 + 16)
                    last = dve.scalar_tensor_tensor(h[:, tt, :], wk(GY[q], D), small[:, CWR + q:CWR + q + 1], h[:, tt, :],
                                                    ALU.mult, ALU.add)
                    round_step(r, 6 + q, last)
            dve.tensor_scalar(small[:, CR:CR + 4], small[:, CR:CR + 4], -float(CAP), None, ALU.add)
            round_step(r, 10, dve.tensor_scalar(wk(RANK, 2 * NE), wk(RANK, 2 * NE), -float(CAP), None, ALU.add))

        def step(e, E, g, par, last):
            u = STEP
            if not last:
                select(e + 1, E + 1)
            split_lo(dve, u + 3, UNIT, g)
            a_mul(g)
            split_lo(dve, u + 4, UNIT, g)
            a_lo(g)
            split_lo(dve, u + 5, UNIT, g)
            split_lo(dve, u + 6, UNIT, g)
            if not last:
                x_half(E + 1, 1 - par)
            y_sum(g, 0)
            split_lo(dve, u + 7, UNIT, g)
            y_sum(g, 1)
            if not last:
                split_lo(dve, u + 8, UNIT, g)

        ROUND_STEPS = 11
        with dve.Fori(0, n) as r:
            g = r * NE
            select(0, g, True)
            for q in range(3):
                split_lo(dve, MU + q, UNIT, g)
            x_half(g, 0)
            select(1, g + 1)
            split_lo(dve, MU + 3, UNIT, g)
            split_lo(dve, MU + 4, UNIT, g)
            choices_in_round(r)
            split_lo(dve, MU + 5, UNIT, g)
            x_half(g + 1, 1)
            split_lo(dve, MU + 6, UNIT, g)
            expert_steps(dve, r, step)
            a_mul(g + (NE - 1))
            a_lo(g + (NE - 1))
            for q in range(2):
                y_sum(g + (NE - 1), q)
            add_rows(r)
        dve.sem_inc(s("out_h"), 1)

    def moe_pool(pool, r):
        with pool.Fori(0, NE) as e:
            pool.wait_ge(s("y_sum"), r * (2 * NE) + e * 2 + 2)
            pool.dma_start(y_slots[bass.ds(e * CAP, CAP), :], work[0:CAP, YS:YS + D]).then_inc(s("y_stored"), 16)
            pool.wait_ge(s("y_stored"), r * (16 * NE) + e * 16 + 16)
            pool.sem_inc(s("y_room"), 1)

    GY = (5120, 6144, 12032, 13056)

    def end_pool(pool):
        n = rounds_of(pool)
        with pool.Fori(0, n) as r:
            moe_pool(pool, r)
            pool.wait_ge(s("slots"), r + 1)
            pool.sem_inc(s("gathers_may_start"), 1)
            for q in range(4):
                pool.indirect_dma_start(out=wk(GY[q], D), out_offset=None, in_=y_slots,
                                        in_offset=bass.IndirectOffsetOnAxis(ap=slot_i[:, q:q + 1], axis=0))\
                    .then_inc(s(f"gathered{q}"), 16)
        rstd_pool(pool, "end", 2, 2)

    def end_dve(dve):
        dve.wait_ge(*mark("end_ssq", 1))
        rstd_dve(dve, "end", [(0, 2, D)], 2, 2)
        for tt in range(TT):
            dve.scalar_tensor_tensor(wk(D * tt, D), h[:, tt, :], small[:, 4 + tt:5 + tt], wk(FROW, D), ALU.mult, ALU.mult)\
                .then_inc(s("result"), 1)

    def end_act(act):
        act.wait_ge(s("out_h"), 1)
        for tt in range(TT):
            last = act.activation(wk(2048, D), h[:, tt, :], ACT.Square, accum_out=small[:, tt:tt + 1])
            if tt == 0:
                act_step(act, last)
        last.then_inc(s("all_ssq"), 1)

    up = sb("up", [16, 2, 256])
    rowp = sb("rowp", [P, 2 * AD + NG + NE])
    pos_i = sb("pos_i", [P, TT], I32)
    top_i = sb("top_i", [P, 32], U32)
    slot_i = sb("slot_i", [P, 4], U32)
    rounds_i = sb("rounds_i", [P, 1], I32)
    sel = sb("sel", [P, TT, CAP], F32R)
    prow = wk(7168, P)

    with nc.Block() as block:
        @block.sync
        def _(sp):
            for j in range(JC):
                u = U_CONV + (3 * j if j == 0 else 4 * j - 1)
                for q in range(3):
                    load(sp, u + q, conv_unit(q, j))
                if j:
                    load(sp, u + 3, conv_unit(3, j - 1))
            load(sp, U_CONV + N_CONV - 1, conv_unit(3, JC - 1))
            for base, w13, w2, units, first in ((U_FFN1, "conv_ffn_w13", "conv_ffn_w2", mla_units, U_MLA),
                                                (U_FFN2, "mla_ffn_w13", "mla_ffn_w2", win_units + wout_units, U_WIN)):
                w13, w2 = a[w13][0], a[w2][0]
                for q in range(2):
                    load(sp, base + q, ffn_unit(w13, w2, q, 0))
                with sp.Fori(0, (JF - 1) // 2) as i:
                    for q in range(2):
                        j = i * 2 + (1 + q)
                        load(sp, base + 2 + 3 * q, ffn_unit(w13, w2, 0, j), i)
                        load(sp, base + 3 + 3 * q, ffn_unit(w13, w2, 1, j), i)
                        load(sp, base + 4 + 3 * q, ffn_unit(w13, w2, 2, i * 2 + q), i)
                load(sp, base + N_FFN - 1, ffn_unit(w13, w2, 2, JF - 1))
                for q, unit in enumerate(units):
                    load(sp, first + q, unit)
            moe_sp(sp)
            for tt in range(TT):
                sp.wait_ge(s("result"), tt + 1)
                sp.dma_start(out[0, P * tt:P * tt + P, :], wk(D * tt, D)).then_inc(s("stored"), 16)
            sp.wait_ge(s("stored"), 32)

        @block.gpsimd
        def _(pool):
            pool.memset(zeros[:, :].bitcast(F32), 0.0).then_inc(s("zeros"), 1)
            for t in ("cv", "ffn1", "mla"):
                rstd_pool(pool, t, 2, 2)
            rstd_pool(pool, "lat", 12, 4)
            pool.wait_ge(*mark("mla_h", 1))
            pool.dma_start(wk(GROW, D), a["final_norm_g"][None, :].broadcast_to([P, D])).then_inc(s("grow"), 16)
            rstd_pool(pool, "ffn2", 2, 2)
            rstd_pool(pool, "end1", 2, 2)
            rstd_pool(pool, "n1", 2, 2)
            rstd_pool(pool, "g", 72, 8)
            rstd_pool(pool, "qkn", 170, 20)
            rstd_pool(pool, "a", 166, 2)
            pool.wait_ge(*mark("mix_h", 1))
            pool.dma_start(wk(NROW, D), a["norm2_gain_2"].broadcast_to([P, D])).then_inc(s("rows_loaded"), 16)
            pool.dma_start(wk(FROW, D), a["final_gain_2"][None, :].broadcast_to([P, D])).then_inc(s("rows_loaded"), 16)
            rstd_pool(pool, "n2", 2, 2)
            pool.sem_inc(s("y_room"), 1)
            end_pool(pool)

        @block.scalar
        def _(act):
            act.dma_start(h[:, :, :], a["x"][0].rearrange("(t p) d -> p t d", p=P)).then_inc(s("h_loaded"), 16)
            act.dma_start(cst[:, :], consts_d).then_inc(s("params"), 16)
            with nc.allow_non_contiguous_dma(reason="256 words"):
                act.dma_start(pos_i[:, :], a["positions"][0].rearrange("(t p) -> p t", p=P)).then_inc(s("params"), 16)
            for name, src in (("conv_norm", "conv_norm_g"), ("ffn1_norm", "conv_ffn_norm_g"), ("kv_norm", "kv_norm_g"),
                              ("mla_norm", "mla_norm_g"), ("ffn2_norm", "mla_ffn_norm_g"), ("norm1", "norm1_gain_2"),
                              ("conv_w", "conv_w"), ("kv_latent", "kv_latent_norm_g"), ("q_norm", "mla_q_norm_g"),
                              ("att_out", "att_out_gain_2"), ("up_f_bias", "gla_up_fwd_bias_2"),
                              ("up_b_bias", "gla_up_bwd_bias_2"), ("gla_out", "gla_out_gain_2")):
                v = a[src]
                v = v.rearrange({1: "(k p) -> k p", 2: "a (k p) -> (a k) p", 3: "a b (k p) -> (a b k) p"}[len(v.shape)], p=P)
                n = v.shape[0]
                act.dma_start(work[ROWS[name]:ROWS[name] + n, 7168:7168 + P], v).then_inc(s("params"), 16)
            act.dma_start(up[:, 0, :], a["gla_up_fwd_2"][0]).then_inc(s("params"), 16)
            act.dma_start(up[:, 1, :], a["gla_up_bwd_2"][0]).then_inc(s("params"), 16)
            act.dma_start(wr[:, :, 0:NG], rows_by_chunk(a["w_group_2"][0])).then_inc(s("params"), 16)
            act.dma_start(wr[:, :, NG:NG + NE], rows_by_chunk(a["w_expert_2"][0])).then_inc(s("params"), 16)
            for at, n, src in ((0, AD, "q_norm_gain_2"), (AD, AD, "k_norm_gain_2"), (2 * AD, NG, "b_group_2"),
                               (2 * AD + NG, NE, "b_expert_2")):
                act.dma_start(rowp[:, at:at + n], a[src].broadcast_to([P, n])).then_inc(s("rowp"), 16)
            rope_tables_act(act)
            conv_act(act)
            ffn_act(act, 1, U_FFN1, ("cv_h", 1), lambda k: col("ffn1_norm", k))
            mla_act(act)
            ffn_act(act, 2, U_FFN2, ("mla_h", 1), lambda k: col("ffn2_norm", k))
            square_act(act, "end1", "ffn2_h")
            win_act(act)
            router_act(act)
            moe_act(act)
            end_act(act)

        @block.vector
        def _(dve):
            rope_tables_dve(dve)
            dve.wait_ge(s("pcol_T"), 1)
            dve.tensor_copy(pcol[:, :], bank(0, NROWS)).then_inc(s("pcol"), 1)
            dve.wait_ge(s("pcol"), 1)
            conv_dve(dve)
            ffn_dve(dve, 1, U_FFN1, lambda k: col("ffn1_norm", k))
            mla_dve(dve)
            ffn_dve(dve, 2, U_FFN2, lambda k: col("ffn2_norm", k))
            end1_dve(dve)
            win_dve(dve)
            router_dve(dve)
            moe_dve(dve)
            end_dve(dve)

        @block.tensor
        def _(pe):
            pe.wait_ge(s("params"), 16 * 19)
            pe.transpose(bank(0, NROWS), work[0:NROWS, 7168:7168 + P], ident[0:NROWS, 0:NROWS]).then_inc(s("pcol_T"), 1)
            pe.wait_ge(s("pcol"), 1)
            conv_pe(pe)
            ffn_pe(pe, 1, U_FFN1)
            mla_pe(pe)
            ffn_pe(pe, 2, U_FFN2)
            win_pe(pe)
            router_pe(pe)
            moe_pe(pe)


_INS = ["x", "positions", "conv_norm_g", "conv_w_in", "conv_w", "conv_w_out", "conv_ffn_norm_g", "conv_ffn_w13",
        "conv_ffn_w2", "kv_norm_g", "w_dkv", "kv_latent_norm_g", "w_ukv", "mla_norm_g", "mla_w_dq", "mla_q_norm_g",
        "mla_w_uq", "mla_w_o", "mla_ffn_norm_g", "mla_ffn_w13", "mla_ffn_w2", "final_norm_g", "norm1_gain_2",
        "w_in_2", "gla_up_fwd_2", "gla_up_fwd_bias_2", "gla_up_bwd_2", "gla_up_bwd_bias_2", "gla_out_gain_2",
        "q_norm_gain_2", "k_norm_gain_2", "att_out_gain_2", "w_out_2", "norm2_gain_2", "w_group_2", "b_group_2",
        "w_expert_2", "b_expert_2", "w_gate_2", "w_up_2", "w_down_2", "final_gain_2"]


def kernel(**inputs):
    import concourse.bacc as bacc
    from concourse.bass_utils import run_bass_kernel_spmd

    nc = bacc.Bacc("TRN2", target_bir_lowering=False, num_devices=1)
    arrays, aps = {}, {}
    for name in _INS:
        v = np.ascontiguousarray(inputs[name])
        arrays[f"in_{name}"] = v
        aps[name] = nc.dram_tensor(f"in_{name}", v.shape, mybir.dt.from_np(v.dtype), kind="ExternalInput").ap()
    arrays["consts"] = shape_constants()
    consts_d = nc.dram_tensor("consts", (P, NCONST), F32, kind="ExternalInput").ap()
    out = nc.dram_tensor("out_0", (1, T, D), F32, kind="ExternalOutput").ap()
    program(nc, aps, consts_d, out)
    r = run_bass_kernel_spmd(nc, [arrays], core_ids=[0])
    return r.results[0]["out_0"]
```

```python
import concourse.bass as bass
from concourse import mybir
import numpy as np

F32 = mybir.dt.float32
F32R = mybir.dt.float32r
I32 = mybir.dt.int32
U32 = mybir.dt.uint32
ALU = mybir.AluOpType
ACT = mybir.ActivationFunctionType
AX = mybir.AxisListType.X

P = 128
T = 256
TT = T // P
D = 1024
KD = D // P
EPS = 1e-6
DFF = 2816
JC = D // 256
JF = DFF // 256
HEADS = 8
NOPE = 128
ROPE = 64
VD = 128
QR = 384
KVR = 256
GH, DK, DV, CH = 4, 64, 128, 64
NCH = T // CH
AH, AKV, AD = 8, 2, 64
NG, EPG = 8, 8
NE = NG * EPG
DE = 512
CAP = 64
BIG_NEG = -3.0e38

UNIT = 2048
RAW = 6
SPLIT = 3
U_CONV = 0
N_CONV = 4 * JC
U_FFN1 = U_CONV + N_CONV
N_FFN = 3 * JF
U_MLA = U_FFN1 + N_FFN
N_MLA = 14
U_FFN2 = U_MLA + N_MLA
U_WIN = U_FFN2 + N_FFN
N_WIN = 10
U_WOUT = U_WIN + N_WIN
U_MOE = U_WOUT + 4

ROWS = {}
_at = 0
N_FIRST = 32
for _name, _n in (("conv_norm", 8), ("conv_w", 24), ("ffn1_norm", 8), ("kv_norm", 8), ("mla_norm", 8),
                  ("ffn2_norm", 8), ("norm1", 8), ("kv_latent", 2), ("q_norm", 3), ("att_out", 4),
                  ("up_f_bias", 2), ("up_b_bias", 2), ("gla_out", 1)):
    ROWS[_name] = _at
    _at += _n
NROWS = _at

CONST = {}
_at = 0
for _name, _n in (("ident", 128), ("iota", 64), ("before", 128), ("ones", 128), ("causal", 384),
                  ("keep_f", 64), ("keep_b", 64), ("fold", 64), ("ax_cos", 64), ("ax_sin", 64),
                  ("freq", 32), ("half", 2)):
    CONST[_name] = (_at, _n)
    _at += _n
NCONST = _at


def shape_constants():
    c = np.zeros((P, NCONST), np.float32)

    def put(name, a):
        at, n = CONST[name]
        c[:, at:at + n] = a

    p = np.arange(P)
    put("ident", np.eye(P))
    put("iota", np.arange(64)[None, :] + 0 * p[:, None])
    put("before", p[:, None] < p[None, :])
    put("ones", 1.0)
    tri = np.where(p[None, :] <= p[:, None], 0.0, BIG_NEG)
    put("causal", np.concatenate([tri, np.zeros((P, P)), tri], axis=1))
    s, q = p[:, None] % 64, np.arange(64)[None, :]
    put("keep_f", s <= q)
    put("keep_b", s >= q)
    put("fold", s == q)
    inv = np.float32(10000.0) ** (-np.arange(0, 32, 2, dtype=np.float32) / np.float32(32))
    for tt in range(TT):
        t = tt * P + p
        row, col = (t // 64).astype(np.float32), (t % 64).astype(np.float32)
        ang = np.concatenate([row[:, None] * inv, col[:, None] * inv], axis=1).astype(np.float32)
        at = CONST["ax_cos"][0] + 32 * tt
        c[:, at:at + 32] = np.cos(ang)
        at = CONST["ax_sin"][0] + 32 * tt
        c[:, at:at + 32] = np.sin(ang)
    freq = np.float32(10000.0) ** (-np.arange(0, 64, 2, dtype=np.float32) / np.float32(64))
    put("freq", freq[None, :] + 0 * p[:, None])
    put("half", -0.5)
    return c


def program(nc, a, consts_d, out):
    sems = {}

    def s(name):
        if name not in sems:
            sems[name] = nc.alloc_semaphore(name)
        return sems[name]

    stages = {}
    for kind, runs in (
            ("acc", [(t, 1) for t in ("cv", "ffn1", "mla", "ffn2", "mix")]),
            ("ssq", [("cv", 2), ("ffn1", 2), ("mla", 2), ("latq", 1), ("latkv", 1), ("ffn2", 2), ("end1", 4), ("g", 1), ("a", 1), ("n2", 2),
                     ("end", 2)]),
            ("mean", [("cv", 2), ("ffn1", 2), ("mla", 2), ("latq", 1), ("latkv", 1), ("ffn2", 2), ("end1", 4), ("qkn", 1), ("g", 1), ("a", 1),
                      ("n2", 2), ("end", 2)]),
            ("rstd", [("cv", 2), ("ffn1", 2), ("mla", 2), ("latq", 1), ("latkv", 1), ("ffn2", 2), ("end1", 4), ("qkn", 1), ("g", 1), ("a", 1),
                      ("n2", 2), ("end", 2)]),
            ("xn", [("cv", 2), ("ffn1", 2), ("mla", 2), ("ffn2", 2), ("n1", 2), ("n2", 2)]),
            ("T", [("cv", 4), ("ffn1", 4), ("mla", 4), ("ffn2", 4), ("n1", 4), ("n2", 4)]),
            ("hi", [("cvx", 4), ("ffn1x", 4), ("mlaq", 4), ("mlax", 4), ("cq", 2), ("cl", 1), ("ffn2x", 4), ("n1x", 4), ("og", 2),
                    ("mo", 2)]),
            ("lo", [("cvx", 4), ("ffn1x", 4), ("mlaq", 4), ("mlax", 4), ("cq", 2), ("cl", 1), ("ffn2x", 4), ("n1x", 4), ("og", 2),
                    ("mo", 2)]),
            ("h", [("cv", 2), ("ffn1", 2), ("mla", 2), ("ffn2", 4), ("mix", 2)])):
        base = 0
        for tag, n in runs:
            stages[f"{tag}_{kind}"] = (f"all_{kind}", base)
            base += n

    def mark(name, n):
        sem, base = stages.get(name, (name, 0))
        return s(sem), base + n

    def sb(name, shape, dt=F32):
        return nc.alloc_sbuf_tensor(name, shape, dt)

    raw = sb("raw", [P, RAW, UNIT])
    w_hi = sb("w_hi", [P, SPLIT, UNIT], F32R)
    w_lo = sb("w_lo", [P, SPLIT, UNIT], F32R)
    cst = sb("cst", [P, NCONST])
    pcol = sb("pcol", [P, NROWS])
    h = sb("h", [P, TT, D])
    xT_hi = sb("xT_hi", [P, KD, T], F32R)
    xT_lo = sb("xT_lo", [P, KD, T], F32R)
    xS_hi = sb("xS_hi", [P, KD, T], F32R)
    xS_lo = sb("xS_lo", [P, KD, T], F32R)
    aT_hi = xS_hi[:, 0:4, :].rearrange("p (s f) t -> p s f t", s=2)
    aT_lo = xS_lo[:, 0:4, :].rearrange("p (s f) t -> p s f t", s=2)
    wr = sb("wr", [P, KD, NG + NE])
    small = sb("small", [P, 256])
    WORK = 14336
    work = sb("work", [P, WORK])
    ps = nc.alloc_psum_tensor("ps", [P, 8, 512], F32)
    y_slots = nc.dram_tensor("y_slots", (T * 2 + CAP, D), F32, kind="Internal").ap()

    def const(name):
        at, n = CONST[name]
        return cst[:, at:at + n]

    ident = const("ident")

    def col(name, i=0):
        return pcol[:, ROWS[name] + i:ROWS[name] + i + 1]

    def wk(at, n):
        assert at + n <= WORK
        return work[:, at:at + n]

    def bank(b, n=512, at=0):
        return ps[:, b, at:at + n]

    def num(u, i=None):
        return u if i is None else i * RAW + u

    def load(sp, u, unit, i=None):
        src, k, c = unit
        if u >= RAW:
            sp.wait_ge(s("lo_done"), num(u - RAW + 1, i))
        sp.dma_start(raw[:, u % RAW, 0:k * c].rearrange("p (k c) -> p k c", k=k), src)\
            .then_inc(s(f"raw_full{u % RAW}"), 16)

    def split_hi(act, u, n, i=None):
        rev = u // RAW + 1
        act.wait_ge(s(f"raw_full{u % RAW}"), 16 * rev if i is None else i * 16 + 16 * rev)
        if u >= SPLIT:
            act.wait_ge(s("used"), num(u - SPLIT + 1, i))
        act.activation(w_hi[:, u % SPLIT, 0:n], raw[:, u % RAW, 0:n], ACT.Copy).then_inc(s("hi_done"), 1)

    def split_lo(dve, u, n, i=None):
        dve.wait_ge(s("hi_done"), num(u + 1, i))
        dve.tensor_tensor(w_lo[:, u % SPLIT, 0:n], raw[:, u % RAW, 0:n],
                          w_hi[:, u % SPLIT, 0:n].bitcast(F32), ALU.subtract).then_inc(s("lo_done"), 1)

    def unit_ready(pe, u, i=None):
        pe.wait_ge(s("lo_done"), num(u + 1, i))

    def weights(u, k, c):
        v = u % SPLIT
        return (w_hi[:, v, 0:k * c].rearrange("p (k c) -> p k c", k=k),
                w_lo[:, v, 0:k * c].rearrange("p (k c) -> p k c", k=k))

    def passes(pe, out_ap, stat_hi, stat_lo, mov_hi, mov_lo, first, last):
        pe.matmul(out_ap, stat_hi, mov_hi, start=first, stop=False, skip_group_check=True)
        pe.matmul(out_ap, stat_hi, mov_lo, start=False, stop=False, skip_group_check=True)
        return pe.matmul(out_ap, stat_lo, mov_hi, start=False, stop=last, skip_group_check=True)

    def by_channel(pe, u, out_bank, x, i=None, ready=None):
        unit_ready(pe, u, i)
        hi, lo = weights(u, KD, 256)
        for f in range(2):
            for k in range(KD):
                if ready is not None and f == 0 and k % 2 == 0:
                    pe.wait_ge(*mark(ready, k // 2 + 1))
                last = passes(pe, bank(out_bank, T, f * T), hi[:, k, f * P:(f + 1) * P], lo[:, k, f * P:(f + 1) * P],
                              x[0][:, k, :], x[1][:, k, :], k == 0, k == KD - 1)
        last.then_inc(s("used"), 1)

    def by_token(pe, u, outs, x, chunks, k, c, n, first, last_unit, cols=None, i=None, ends_sum=False, ready=None):
        unit_ready(pe, u, i)
        hi, lo = weights(u, k, c)
        for tt in range(TT):
            for part in range(len(outs[tt])):
                for q, ch in enumerate(chunks):
                    if ready is not None and tt == 0 and part == 0 and q % 2 == 0:
                        pe.wait_ge(*mark(ready, ch // 2 + 1))
                    cs = slice(part * n, part * n + n) if cols is None else cols
                    last = passes(pe, outs[tt][part], x[0][:, ch, tt * P:(tt + 1) * P], x[1][:, ch, tt * P:(tt + 1) * P],
                                  hi[:, q, cs], lo[:, q, cs], first and q == 0, last_unit and q == len(chunks) - 1)
            if ends_sum and tt == 0:
                last.then_inc(s("all_acc"), 1)
        return last

    xT = (xT_hi, xT_lo)
    xS = (xS_hi, xS_lo)
    ACC = [[bank(4), bank(5)], [bank(6), bank(7)]]

    def clear_acc(pe):
        for tt in range(TT):
            for part in range(2):
                pe.matmul(ACC[tt][part][:, 0:P], zeros[:, :], zeros[:, :], start=True, stop=False, skip_group_check=True)

    def rows_by_chunk(v):
        return v.rearrange("(k p) c -> p k c", p=P)

    def conv_unit(kind, j):
        if kind == 3:
            return rows_by_chunk(a["conv_w_out"][0][256 * j:256 * j + 256, :]), 2, D
        return rows_by_chunk(a["conv_w_in"][0][:, kind * D + 256 * j:kind * D + 256 * j + 256]), KD, 256

    def ffn_unit(w13, w2, kind, j):
        if kind == 2:
            if isinstance(j, int):
                return rows_by_chunk(w2[256 * j:256 * j + 256, :]), 2, D
            return rows_by_chunk(w2[bass.ds(j * 256, 256), :]), 2, D
        if isinstance(j, int):
            return rows_by_chunk(w13[:, kind * DFF + 256 * j:kind * DFF + 256 * j + 256]), KD, 256
        return rows_by_chunk(w13[:, bass.ds(j * 256 + kind * DFF, 256)]), KD, 256

    mla_units = []
    for q in range(2):
        mla_units.append((rows_by_chunk(a["mla_w_dq"][0][512 * q:512 * q + 512, :]), 4, QR))
    for q in range(2):
        mla_units.append((rows_by_chunk(a["w_dkv"][512 * q:512 * q + 512, :]), 4, KVR + ROPE))
    for q in range(4):
        mla_units.append((rows_by_chunk(a["mla_w_uq"][0][:, 384 * q:384 * q + 384]), 3, 384))
    for q in range(2):
        mla_units.append((rows_by_chunk(a["w_ukv"][:, 1024 * q:1024 * q + 1024]), 2, 1024))
    for q in range(4):
        mla_units.append((rows_by_chunk(a["mla_w_o"][0][256 * q:256 * q + 256, :]), 2, D))
    win = a["w_in_2"][0]
    win_units = [(rows_by_chunk(win[:, c0:c0 + n]), KD, n)
                 for c0, n in [(1536, 160), (0, 256), (256, 256), (2080, 256), (1568, 256), (1824, 256)]
                 + [(512 + 256 * q, 256) for q in range(4)]]
    wout_units = [(rows_by_chunk(a["w_out_2"][0][256 * q:256 * q + 256, :]), 2, D) for q in range(4)]

    def moe_unit(q, e):
        half = q % 2
        if q < 4:
            w = a["w_gate_2" if q < 2 else "w_up_2"][0]
            v = w[bass.ds(e, 1), half * 512:half * 512 + 512, :]
        else:
            v = a["w_down_2"][0][bass.ds(e, 1), :, half * 512:half * 512 + 512]
        return v.rearrange("a (k p) c -> p (a k) c", p=P), 4, 512

    size = [0] * U_MOE
    for j in range(JC):
        for q in range(4):
            size[4 * j + q] = UNIT
    for u in range(U_FFN1, U_MLA):
        size[u] = UNIT
    for q, (_, k, c) in enumerate(mla_units):
        size[U_MLA + q] = k * c
    for u in range(U_FFN2, U_WIN):
        size[u] = UNIT
    for q, (_, k, c) in enumerate(win_units):
        size[U_WIN + q] = k * c
    for q in range(4):
        size[U_WOUT + q] = UNIT
    size += [UNIT] * 6

    def ahead_hi(act, u):
        split_hi(act, u + SPLIT, size[u + SPLIT])

    def ahead_lo(dve, u):
        split_lo(dve, u + SPLIT, size[u + SPLIT])

    zeros = sb("zeros", [P, P], F32R)

    steps = {"act": 0, "dve": 0}

    def act_step(act, ins):
        steps["act"] += 1
        ins.then_inc(s("act_steps"), 1)
        act.wait_ge(s("act_steps"), steps["act"])

    def dve_step(dve, ins):
        steps["dve"] += 1
        ins.then_inc(s("dve_steps"), 1)
        dve.wait_ge(s("dve_steps"), steps["dve"])

    XN = 0

    def square(act, tag, q, tt):
        name, value = mark(f"{tag}_ssq", q)
        if value:
            act.wait_ge(name, value)
        act.activation(wk(2048, D), h[:, tt, :], ACT.Square, accum_out=small[:, tt:tt + 1]).then_inc(s("all_ssq"), 1)

    def norm_act(act, tag, after):
        for tt in range(TT):
            act.wait_ge(*after(tt))
            square(act, tag, tt, tt)

    def tile_rstd_pool(pool, tag, q, tt):
        pool.wait_ge(*mark(f"{tag}_mean", q + 1))
        pool.tensor_tensor(small[:, 4 + tt:5 + tt], small[:, 2 + tt:3 + tt], const("half")[:, 0:1], ALU.pow).then_inc(s("all_rstd"), 1)

    def norm_pool(pool, tag):
        for tt in range(TT):
            tile_rstd_pool(pool, tag, tt, tt)

    def tile_rstd_dve(dve, tag, q, tt):
        dve.wait_ge(*mark(f"{tag}_ssq", q + 1))
        dve.tensor_scalar(small[:, 2 + tt:3 + tt], small[:, tt:tt + 1], 1.0 / D, EPS, ALU.mult, ALU.add).then_inc(s("all_mean"), 1)
        dve.wait_ge(*mark(f"{tag}_rstd", q + 1))

    def normed_rows(dve, tt):
        dve.tensor_scalar(wk(XN + tt * D, D), h[:, tt, :], small[:, 4 + tt:5 + tt], None, ALU.mult).then_inc(s("all_xn"), 1)

    def norm_dve(dve, tag, add=None):
        for tt in range(TT):
            if add is not None:
                add_acc(dve, add[0], add[1], tt)
            tile_rstd_dve(dve, tag, tt, tt)
            normed_rows(dve, tt)

    def norm_pe(pe, tag):
        for tt in range(TT):
            pe.wait_ge(*mark(f"{tag}_xn", tt + 1))
            for k in range(KD):
                last = pe.transpose(bank(k // 2, P, (k % 2) * T + tt * P), wk(XN + tt * D + k * P, P), ident)
                if tt == TT - 1 and k % 2:
                    last.then_inc(s("all_T"), 1)

    def operand_act(act, tag, psum_tag, banks, gain, dst, first=0, at=0, also=None):
        for b, (pb, n) in enumerate(banks):
            act.wait_ge(*mark(psum_tag, at + b + 1))
            if also is not None:
                act.wait_ge(*mark(also, b + 1))
            for q in range(n):
                k = first + 2 * b + q
                last = act.activation(dst[0][:, k, :], bank(pb, T, q * T), ACT.Copy, scale=gain(2 * b + q))
            last.then_inc(s("all_hi"), 1)

    def operand_dve(dve, tag, banks, gain, dst, first=0):
        for b, (pb, n) in enumerate(banks):
            dve.wait_ge(*mark(f"{tag}_hi", b + 1))
            for q in range(n):
                k = first + 2 * b + q
                last = dve.scalar_tensor_tensor(dst[1][:, k, :], bank(pb, T, q * T), gain(2 * b + q),
                                                dst[0][:, k, :].bitcast(F32), ALU.mult, ALU.subtract)
            last.then_inc(s("all_lo"), 1)

    NORM_BANKS = [(0, 2), (1, 2), (2, 2), (3, 2)]

    def add_acc(dve, units_done, tag, tt):
        if tt == 0:
            dve.wait_ge(*mark(f"{tag}_acc", 1))
        else:
            dve.wait_ge(s("used"), units_done)
        dve.tensor_tensor(h[:, tt, :], h[:, tt, :], ps[:, 4 + 2 * tt:6 + 2 * tt, :].rearrange("p b n -> p (b n)"), ALU.add)\
            .then_inc(s("all_h"), 1)

    ROW_AT = 7168
    FIRST_ROWS = [("conv_norm", "conv_norm_g"), ("conv_w", "conv_w")]
    OTHER_ROWS = [("ffn1_norm", "conv_ffn_norm_g"), ("kv_norm", "kv_norm_g"),
                  ("mla_norm", "mla_norm_g"), ("ffn2_norm", "mla_ffn_norm_g"), ("norm1", "norm1_gain_2"),
                  ("kv_latent", "kv_latent_norm_g"), ("q_norm", "mla_q_norm_g"),
                  ("att_out", "att_out_gain_2"), ("up_f_bias", "gla_up_fwd_bias_2"),
                  ("up_b_bias", "gla_up_bwd_bias_2"), ("gla_out", "gla_out_gain_2")]
    N_PARAMS = len(OTHER_ROWS) + 5

    def parameter_columns(pe, part, b):
        n = (N_FIRST, NROWS - N_FIRST)[part]
        if part == 0:
            pe.wait_ge(s("first_params"), 16 * len(FIRST_ROWS))
        else:
            pe.wait_ge(s("params"), 16 * N_PARAMS)
        pe.transpose(bank(b, n), work[0:n, ROW_AT + P * part:ROW_AT + P * part + P], ident[0:n, 0:n]).then_inc(s("pcol_T"), 1)

    CV = 4096
    ZP = T + 2

    ROWS_AT = 2
    CONV_ORDER = (1, 2, 0)

    def conv_bank(j, q):
        return (3 * j + q) % 4

    def conv_first_unit(j):
        return U_CONV + (3 * j if j == 0 else 4 * j - 1)

    def conv_pe(pe):
        norm_pe(pe, "cv")
        pe.wait_ge(s("zeros"), 1)
        pe.wait_ge(s("pcol"), 1)
        clear_acc(pe)
        for j in range(JC):
            u = conv_first_unit(j)
            for q in range(3):
                if q == 0 and j == ROWS_AT + 1:
                    pe.wait_ge(s("pcol"), 2)
                if q == 0 and j >= 2:
                    pe.wait_ge(s("cv_y"), 2 * j - 2)
                if q == 1 and j:
                    pe.wait_ge(s("cv_c"), j)
                if q == 2 and j:
                    pe.wait_ge(s("cv_z"), j)
                by_channel(pe, u + q, conv_bank(j, q), xT, ready="cvx_lo" if j == q == 0 else None)
            if j == ROWS_AT:
                parameter_columns(pe, 1, conv_bank(j + 1, 0))
            if j:
                conv_out(pe, j - 1, u + 3)
        conv_out(pe, JC - 1, U_CONV + N_CONV - 1)

    def conv_out(pe, j, u):
        pe.wait_ge(s("cv_alo"), j + 1)
        last = by_token(pe, u, ACC, (aT_hi[:, j % 2], aT_lo[:, j % 2]), [0, 1], 2, D, 512, False, j == JC - 1,
                        ends_sum=j == JC - 1)
        last.then_inc(s("used"), 1)

    def conv_act(act):
        norm_act(act, "cv", lambda tt: (s(f"h_loaded{tt}"), 16))
        for u in range(SPLIT):
            split_hi(act, u, size[u])
        act.wait_ge(s("pcol"), 1)
        operand_act(act, "cvx", "cv_T", NORM_BANKS, lambda k: col("conv_norm", k), xT)
        for j in range(JC):
            u = conv_first_unit(j)

            def a_hi():
                act.wait_ge(s("cv_y"), 2 * j + 2)
                if j >= 2:
                    act.wait_ge(s("used"), conv_out_unit(j - 2) + 1)
                act.activation(aT_hi[:, j % 2].rearrange("p f t -> p (f t)"), wk(CV + 2048, 512), ACT.Copy)\
                    .then_inc(s("cv_ahi"), 1)

            act.wait_ge(s("used"), u + 1)
            if j:
                act.wait_ge(s("cv_z"), j)
            act.activation(wk(CV, 512), bank(conv_bank(j, 0)), ACT.Copy).then_inc(s("cv_c"), 1)
            ahead_hi(act, u)
            ahead_hi(act, u + 1)
            if j == JC - 1:
                a_hi()
            ahead_hi(act, u + 2)
            if j < JC - 1:
                a_hi()
            if j:
                ahead_hi(act, u + 3)
            if j == ROWS_AT:
                rope_tables_act(act)

    def conv_out_unit(j):
        return U_CONV + (4 * j + 6 if j < JC - 1 else N_CONV - 1)

    def conv_dve(dve):
        norm_dve(dve, "cv")
        split_lo(dve, 0, size[0])
        dve.wait_ge(s("pcol_T"), 1)
        dve.tensor_copy(pcol[:, 0:N_FIRST], bank(7, N_FIRST)).then_inc(s("pcol"), 1)
        dve.wait_ge(s("pcol"), 1)
        operand_dve(dve, "cvx", NORM_BANKS, lambda k: col("conv_norm", k), xT)
        for u in range(1, SPLIT):
            split_lo(dve, u, size[u])
        dve_step(dve, dve.memset(wk(CV + 512, 2 * ZP), 0.0))
        for j in range(JC):
            u = conv_first_unit(j)
            z = [wk(CV + 512 + f * ZP, ZP) for f in range(2)]
            t0, t1 = ([wk(at + 256 * q, T) for at in (CV + 1536, CV + 2560)] for q in range(2))
            w = [[col("conv_w", 8 * tap + 2 * j + f) for tap in range(3)] for f in range(2)]

            def each(op):
                for f in range(2):
                    last = op(f)
                dve_step(dve, last)

            def a_lo():
                dve.wait_ge(s("cv_ahi"), j + 1)
                dve.tensor_tensor(aT_lo[:, j % 2].rearrange("p f t -> p (f t)"), wk(CV + 2048, 512),
                                  aT_hi[:, j % 2].rearrange("p f t -> p (f t)").bitcast(F32), ALU.subtract)\
                    .then_inc(s("cv_alo"), 1)

            ahead_lo(dve, u)
            dve.wait_ge(s("cv_c"), j + 1)
            dve.wait_ge(s("used"), u + 2)
            for f in range(2):
                last = dve.tensor_tensor(z[f][:, 2:ZP], bank(conv_bank(j, 1), T, f * T), wk(CV + f * T, T), ALU.mult)
            last.then_inc(s("cv_z"), 1)
            dve.wait_ge(s("cv_z"), j + 1)
            each(lambda f: dve.tensor_scalar(t0[f], z[f][:, 0:T], w[f][0], None, ALU.mult))
            each(lambda f: dve.scalar_tensor_tensor(t1[f], z[f][:, 1:T + 1], w[f][1], t0[f], ALU.mult, ALU.add))
            each(lambda f: dve.scalar_tensor_tensor(t0[f], z[f][:, 2:ZP], w[f][2], t1[f], ALU.mult, ALU.add))
            ahead_lo(dve, u + 1)
            dve.wait_ge(s("used"), u + 3)
            if j:
                dve.wait_ge(s("cv_ahi"), j)
            for f in range(2):
                dve.tensor_tensor(wk(CV + 2048 + f * T, T), bank(conv_bank(j, 2), T, f * T), t0[f], ALU.mult)\
                    .then_inc(s("cv_y"), 1)
            if j == ROWS_AT:
                dve.wait_ge(s("pcol_T"), 2)
                dve.tensor_copy(pcol[:, N_FIRST:NROWS], bank(conv_bank(j + 1, 0), NROWS - N_FIRST)).then_inc(s("pcol"), 1)
            if j == JC - 1:
                a_lo()
            ahead_lo(dve, u + 2)
            if j < JC - 1:
                a_lo()
            if j:
                ahead_lo(dve, u + 3)
            if j == ROWS_AT:
                rope_tables_dve(dve)

    FG = 4096

    def ffn_pe(pe, n, base):
        t = f"ffn{n}"
        norm_pe(pe, t)
        clear_acc(pe)

        def up(u, parity, i=None, ready=None):
            by_channel(pe, u, 2 * parity, xT, i, ready)
            by_channel(pe, u + 1, 2 * parity + 1, xT, i)

        def down(u, slot_j, jj, i=None, last_block=False):
            pe.wait_ge(s(f"{t}_alo"), jj)
            last = by_token(pe, u, ACC, (aT_hi[:, slot_j], aT_lo[:, slot_j]), [0, 1], 2, D, 512, False, last_block, i=i,
                            ends_sum=last_block)
            last.then_inc(s("used"), 1)

        up(base, 0, ready=f"{t}x_lo")
        with pe.Fori(0, (JF - 1) // 2) as i:
            for q in range(2):
                up(base + 2 + 3 * q, (1 + q) % 2, i)
                down(base + 4 + 3 * q, q % 2, i * 2 + (1 + q), i)
        down(base + N_FFN - 1, (JF - 1) % 2, JF, last_block=True)

    def ffn_act(act, n, base, after, gain):
        t = f"ffn{n}"
        norm_act(act, t, lambda tt: mark(after, tt + 1))
        operand_act(act, f"{t}x", f"{t}_T", NORM_BANKS, gain, xT)
        ahead_hi(act, base - 1)

        def gate(u, parity, jj, i=None):
            act.wait_ge(s("used"), num(u + 2, i))
            if jj is not None:
                act.wait_ge(s(f"{t}_a"), jj)
            act.activation(wk(FG, 512), bank(2 * parity), ACT.Silu).then_inc(s(f"{t}_silu"), 1)

        def a_hi(slot_j, jj, used, i=None):
            act.wait_ge(s(f"{t}_a"), jj)
            if used is not None:
                act.wait_ge(s("used"), num(used, i))
            act.activation(aT_hi[:, slot_j].rearrange("p f t -> p (f t)"), wk(FG + 512, 512), ACT.Copy)\
                .then_inc(s(f"{t}_ahi"), 1)

        ahead_hi(act, base)
        ahead_hi(act, base + 1)
        gate(base, 0, None)
        a_hi(0, 1, None)
        with act.Fori(0, (JF - 1) // 2) as i:
            for q in range(2):
                u = base + 2 + 3 * q
                split_hi(act, u + SPLIT, UNIT, i)
                split_hi(act, u + SPLIT + 1, UNIT, i)
                gate(u, (1 + q) % 2, i * 2 + (1 + q), i)
                a_hi((1 + q) % 2, i * 2 + (2 + q), u, i)
                split_hi(act, u + SPLIT + 2, size[u + SPLIT + 2], i)

    def ffn_dve(dve, n, base, gain, add):
        t = f"ffn{n}"
        norm_dve(dve, t, add)
        operand_dve(dve, f"{t}x", NORM_BANKS, gain, xT)
        ahead_lo(dve, base - 1)

        def gated(parity, jj, jj0):
            dve.wait_ge(s(f"{t}_silu"), jj)
            if jj0 is not None:
                dve.wait_ge(s(f"{t}_ahi"), jj0)
                dve.wait_ge(s(f"{t}_alo"), jj0)
            dve.tensor_tensor(wk(FG + 512, 512), bank(2 * parity + 1), wk(FG, 512), ALU.mult).then_inc(s(f"{t}_a"), 1)

        def a_lo(slot_j, jj):
            dve.wait_ge(s(f"{t}_ahi"), jj)
            dve.tensor_tensor(aT_lo[:, slot_j].rearrange("p f t -> p (f t)"), wk(FG + 512, 512),
                              aT_hi[:, slot_j].rearrange("p f t -> p (f t)").bitcast(F32), ALU.subtract)\
                .then_inc(s(f"{t}_alo"), 1)

        ahead_lo(dve, base)
        ahead_lo(dve, base + 1)
        gated(0, 1, None)
        a_lo(0, 1)
        with dve.Fori(0, (JF - 1) // 2) as i:
            for q in range(2):
                u = base + 2 + 3 * q
                split_lo(dve, u + SPLIT, UNIT, i)
                split_lo(dve, u + SPLIT + 1, UNIT, i)
                gated((1 + q) % 2, i * 2 + (2 + q), i * 2 + (1 + q))
                a_lo((1 + q) % 2, i * 2 + (2 + q))
                split_lo(dve, u + SPLIT + 2, size[u + SPLIT + 2], i)

    def rstd_dve(dve, tag, groups, at, n):
        for first, count, width in groups:
            last = dve.tensor_scalar(small[:, at + first - groups[0][0]:at + first - groups[0][0] + count],
                                     small[:, first:first + count], 1.0 / width, EPS, ALU.mult, ALU.add)
        last.then_inc(s("all_mean"), 1)
        dve.wait_ge(*mark(f"{tag}_rstd", 1))

    def rstd_pool(pool, tag, at, n):
        pool.wait_ge(*mark(f"{tag}_mean", 1))
        pool.tensor_tensor(small[:, at + n:at + 2 * n], small[:, at:at + n],
                           const("half")[:, 0:1].broadcast_to([P, n]), ALU.pow).then_inc(s("all_rstd"), 1)

    CL, CQ, KPE = 0, 512, 1280
    QN, KN, VV = 2048, 4096, 6144
    QPE, QPT, KPT, RT = 8192, 9216, 10240, 10496
    ROT = 11520
    SM, PB, PT = 11648, 12416, 13184
    SCALE = (NOPE + ROPE) ** -0.5
    cos_p = lambda tt: wk(ROT + 32 * tt, 32)
    sin_p = lambda tt: wk(ROT + 64 + 32 * tt, 32)

    def rope_tables_dve(dve):
        magic = 12582912.0
        dve.wait_ge(s("params"), 16 * N_PARAMS)
        dve_step(dve, dve.tensor_copy(small[:, 20:22], pos_i[:, :]))
        ang, turns, r = wk(RT, 64), wk(RT + 64, 64), wk(RT + 128, 64)
        for tt in range(TT):
            dve_step(dve, dve.tensor_scalar(ang[:, 32 * tt:32 * tt + 32], const("freq"), small[:, 20 + tt:21 + tt], None, ALU.mult))
        dve_step(dve, dve.tensor_scalar(turns, ang, float(np.float32(1 / (2 * np.pi))), magic, ALU.mult, ALU.add))
        dve_step(dve, dve.tensor_scalar(turns, turns, -magic, None, ALU.add))
        c1 = 6.28125
        c2 = float(np.float32(np.round((2 * np.pi - c1) * 2 ** 20) / 2 ** 20))
        c3 = float(2 * np.pi - c1 - c2)
        for c, src in ((c1, ang), (c2, r), (c3, r)):
            dve_step(dve, dve.scalar_tensor_tensor(r, turns, -c, src, ALU.mult, ALU.add))
        dve_step(dve, dve.tensor_scalar(r, r, 3.1415925, -3.1415925, ALU.min, ALU.max))
        dve_step(dve, dve.tensor_scalar(ang, r, -1.0, None, ALU.mult))
        dve_step(dve, dve.tensor_tensor(ang, ang, r, ALU.max))
        dve.tensor_scalar(ang, ang, -1.0, float(np.pi / 2), ALU.mult, ALU.add).then_inc(s("angles"), 1)

    def rope_tables_act(act):
        act.wait_ge(s("angles"), 1)
        act.activation(wk(ROT, 64), wk(RT, 64), ACT.Sin).then_inc(s("rope_tables"), 1)
        act.activation(wk(ROT + 64, 64), wk(RT + 128, 64), ACT.Sin).then_inc(s("rope_tables"), 1)

    def halves_rope(dve, x, dst, tt, groups):
        cos = cos_p(tt)[:, None, :].broadcast_to([P, groups, 32])
        sin = sin_p(tt)[:, None, :].broadcast_to([P, groups, 32])
        t = [wk(RT + 256 * q, 32 * groups).rearrange("p (g c) -> p g c", c=32) for q in range(4)]
        x1, x2 = x[:, :, 0:32], x[:, :, 32:64]
        dve.tensor_tensor(t[0], x1, cos, ALU.mult)
        dve.tensor_tensor(t[1], x2, sin, ALU.mult)
        dve.tensor_tensor(t[2], x1, sin, ALU.mult)
        dve_step(dve, dve.tensor_tensor(t[3], x2, cos, ALU.mult))
        dve.tensor_tensor(dst[:, :, 0:32], t[0], t[1], ALU.subtract)
        dve_step(dve, dve.tensor_tensor(dst[:, :, 32:64], t[2], t[3], ALU.add))

    def mla_pe(pe):
        u = U_MLA
        norm_pe(pe, "mla")
        for q in range(2):
            by_token(pe, u + q, [[bank(4, QR)], [bank(5, QR)]], xS, range(4 * q, 4 * q + 4), 4, QR, QR,
                     q == 0, q == 1, ready="mlaq_lo").then_inc(s("used"), 1)
        for q in range(2):
            by_token(pe, u + 2 + q, [[bank(6, 320)], [bank(7, 320)]], xT, range(4 * q, 4 * q + 4), 4, 320, 320,
                     q == 0, q == 1, ready="mlax_lo").then_inc(s("used"), 1)
        pe.wait_ge(s("latents"), 1)
        for c in range(3):
            for tt in range(TT):
                last = pe.transpose(bank(2 + c // 2, P, (c % 2) * T + tt * P), wk(CQ + QR * tt + c * P, P), ident)
            if c:
                last.then_inc(s("lat_T"), 1)
        pe.wait_ge(*mark("cq_lo", 2))
        for q in range(4):
            if q == 2:
                pe.wait_ge(s("latents"), 2)
                for c in range(2):
                    for tt in range(TT):
                        last = pe.transpose(bank(2, P, c * T + tt * P), wk(CL + 256 * tt + c * P, P), ident)
                last.then_inc(s("lat_T"), 1)
                for tt in range(TT):
                    last = pe.transpose(bank(3, P, tt * P), wk(KPE + P * tt, P), ident)
                last.then_inc(s("lat_T"), 1)
            unit_ready(pe, u + 4 + q)
            hi, lo = weights(u + 4 + q, 3, 384)
            if q >= 2:
                pe.wait_ge(s("qn_read"), q - 1)
            for hh in range(2):
                for k in range(3):
                    cs = slice(192 * hh, 192 * hh + NOPE)
                    passes(pe, bank(q % 2, T, hh * T), hi[:, k, cs], lo[:, k, cs], xS_hi[:, k, :], xS_lo[:, k, :], k == 0, k == 2)
            for tt in range(TT):
                for k in range(3):
                    ts = slice(tt * P, tt * P + P)
                    m = [w[:, k, :].rearrange("p (h c) -> p h c", c=192)[:, :, NOPE:192] for w in (hi, lo)]
                    last = passes(pe, bank(4 + tt, P, P * q).rearrange("p (h c) -> p h c", c=ROPE), xS_hi[:, k, ts], xS_lo[:, k, ts],
                                  m[0], m[1], k == 0, k == 2)
            last.then_inc(s("used"), 1)
        pe.wait_ge(*mark("cl_lo", 1))
        pe.wait_ge(s("kpt"), 1)
        for q in range(2):
            unit_ready(pe, u + 8 + q)
            hi, lo = weights(u + 8 + q, 2, 1024)
            if q:
                pe.wait_ge(s("qn_read"), 4)
            for hh in range(4):
                for k in range(2):
                    cs = slice(256 * hh, 256 * hh + NOPE)
                    passes(pe, bank(2 - 2 * q + hh // 2, T, (hh % 2) * T), hi[:, k, cs], lo[:, k, cs], xT_hi[:, k, :], xT_lo[:, k, :], k == 0, k == 1)
            if q:
                pe.wait_ge(s("v_read"), 1)
            for tt in range(TT):
                for k in range(2):
                    ts = slice(tt * P, tt * P + P)
                    m = [w[:, k, :].rearrange("p (h c) -> p h c", c=256)[:, :, NOPE:256] for w in (hi, lo)]
                    last = passes(pe, bank(6 + tt).rearrange("p (h c) -> p h c", c=VD), xT_hi[:, k, ts], xT_lo[:, k, ts],
                                  m[0], m[1], k == 0, k == 1)
            last.then_inc(s("used"), 1)
        pe.wait_ge(s("qpe"), 1)
        pe.wait_ge(s("kn_read"), 1)
        for c in range(4):
            for tt in range(TT):
                last = pe.transpose(bank(2 + c // 2, P, (c % 2) * T + tt * P), wk(QPE + 512 * tt + c * P, P), ident)
        last.then_inc(s("qpe_T"), 1)
        pe.wait_ge(s("qpt"), 1)
        pe.wait_ge(s("kn_read"), 2)
        pe.wait_ge(s("v_read"), 2)
        for t in range(HEADS + 2):
            if t < HEADS:
                r = slice(64 * (t % 2), 64 * (t % 2) + 64)
                b = 2 + t % 2
                if t >= 2:
                    pe.wait_ge(s("sc_read"), t - 1)
                for tt in range(TT):
                    o = bank(b, P * (tt + 1), P * tt)
                    qs = slice(T * t + P * tt, T * t + P * tt + P)
                    n = P * (tt + 1)
                    pe.matmul(o, work[:, QN + qs.start:QN + qs.stop], wk(KN + T * t, n), start=True, stop=False, skip_group_check=True)
                    last = pe.matmul(o, work[r, QPT + T * (t // 2) + P * tt:QPT + T * (t // 2) + P * tt + P],
                                     work[r, KPT:KPT + n], start=False, stop=True, skip_group_check=True)
                last.then_inc(s("scores"), 1)
            if 1 <= t <= HEADS:
                v = t - 1
                pe.wait_ge(s("probs"), v + 1)
                if v >= 2:
                    pe.wait_ge(s("pt_read"), v - 1)
                for q in range(3):
                    last = pe.transpose(bank(4 + v % 2, P, q * P), wk(PB + 384 * (v % 2) + q * P, P), ident)
                last.then_inc(s("probs_T"), 1)
            if t >= 2:
                v = t - 2
                pe.wait_ge(s("pt_read"), v + 1)
                if v >= 2:
                    pe.wait_ge(s("at_lo"), v - 1)
                o = 6 + v % 2
                pt = wk(PT + 384 * (v % 2), 384)
                pe.matmul(bank(o, T), wk(VV + VD * v, VD), pt[:, 0:T], start=True, stop=False, skip_group_check=True)
                pe.matmul(bank(o, P, P), wk(VV + 1024 + VD * v, VD), pt[:, T:384], start=False, stop=True, skip_group_check=True)\
                    .then_inc(s("att"), 1)
        pe.wait_ge(s("at_lo"), HEADS)
        for q in range(4):
            by_token(pe, u + 10 + q, ACC, xT, [2 * q, 2 * q + 1], 2, D, 512, q == 0, q == 3, ends_sum=q == 3)\
                .then_inc(s("used"), 1)

    def mla_act(act):
        u = U_MLA
        norm_act(act, "mla", lambda tt: mark("ffn1_h", tt + 1))
        operand_act(act, "mlaq", "mla_T", NORM_BANKS, lambda k: col("mla_norm", k), xS)
        ahead_hi(act, u - 1)
        operand_act(act, "mlax", "mla_T", NORM_BANKS, lambda k: col("kv_norm", k), xT, also="mlaq_lo")

        def latent_squares(units, b, n, at):
            act.wait_ge(s("used"), units)
            for tt in range(TT):
                last = act.activation(wk(2048 + 512 * tt, n), bank(b + tt, n), ACT.Square, accum_out=small[:, at + tt:at + tt + 1])
            last.then_inc(s("all_ssq"), 1)

        ahead_hi(act, u)
        latent_squares(u + 2, 4, QR, 8)
        ahead_hi(act, u + 1)
        ahead_hi(act, u + 2)
        operand_act(act, "cq", "lat_T", [(2, 2), (3, 1)], lambda k: col("q_norm", k), xS)
        act.wait_ge(*mark("latq_ssq", 1))
        latent_squares(u + 4, 6, KVR, 10)
        act.wait_ge(*mark("latkv_ssq", 1))
        ahead_hi(act, u + 3)
        for q in range(4):
            if q == 2:
                operand_act(act, "cl", "lat_T", [(2, 2)], lambda k: col("kv_latent", k), xT, at=2)
                act.wait_ge(s("lat_T"), 4)
                act.activation(wk(KPT, T), bank(3, T), ACT.Copy).then_inc(s("kpt"), 1)
            ahead_hi(act, u + 4 + q)
            act.wait_ge(s("used"), u + 5 + q)
            act.activation(wk(QN + 512 * q, 512), bank(q % 2), ACT.Copy).then_inc(s("qn_read"), 1)
        for q in range(2):
            act.wait_ge(s("used"), u + 9 + q)
            act.activation(wk(KN + 1024 * q, 1024), ps[:, 2 - 2 * q:4 - 2 * q, :].rearrange("p b n -> p (b n)"), ACT.Copy)\
                .then_inc(s("kn_read"), 1)
            if q == 0:
                ahead_hi(act, u + 8)
        act.wait_ge(s("qpe_T"), 1)
        act.activation(wk(QPT, 1024), ps[:, 2:4, :].rearrange("p b n -> p (b n)"), ACT.Copy).then_inc(s("qpt"), 1)
        ahead_hi(act, u + 9)
        for t in range(HEADS + 2):
            if t < HEADS:
                m = 32 + 8 * (t % 2)
                act.wait_ge(s("smax"), t + 1)
                if t >= 2:
                    act.wait_ge(s("probs_T"), t - 1)
                for tt, (c0, n) in enumerate(((0, P), (P, T))):
                    last = act.activation(wk(PB + 384 * (t % 2) + c0, n), wk(SM + 384 * (t % 2) + c0, n), ACT.Exp,
                                          bias=small[:, m + 2 + tt:m + 3 + tt], scale=SCALE, accum_out=small[:, m + 4 + tt:m + 5 + tt])
                last.then_inc(s("exps"), 1)
            if 1 <= t <= HEADS:
                v = t - 1
                act.wait_ge(s("probs_T"), v + 1)
                if v >= 2:
                    act.wait_ge(s("att"), v - 1)
                act.activation(wk(PT + 384 * (v % 2), 384), bank(4 + v % 2, 384), ACT.Copy).then_inc(s("pt_read"), 1)
            if t >= 2:
                v = t - 2
                act.wait_ge(s("att"), v + 1)
                act.activation(xT_hi[:, v, :], bank(6 + v % 2, T), ACT.Copy).then_inc(s("at_hi"), 1)
        for q in range(3):
            ahead_hi(act, u + 10 + q)

    def mla_dve(dve):
        u = U_MLA
        norm_dve(dve, "mla", (U_FFN1 + N_FFN, "ffn1"))
        operand_dve(dve, "mlaq", NORM_BANKS, lambda k: col("mla_norm", k), xS)
        ahead_lo(dve, u - 1)
        operand_dve(dve, "mlax", NORM_BANKS, lambda k: col("kv_norm", k), xT)
        ahead_lo(dve, u)
        dve.wait_ge(*mark("latq_ssq", 1))
        rstd_dve(dve, "latq", [(8, 2, QR)], 12, 2)
        for tt in range(TT):
            last = dve.tensor_scalar(wk(CQ + QR * tt, QR), bank(4 + tt, QR), small[:, 14 + tt:15 + tt], None, ALU.mult)
        last.then_inc(s("latents"), 1)
        ahead_lo(dve, u + 1)
        ahead_lo(dve, u + 2)
        operand_dve(dve, "cq", [(2, 2), (3, 1)], lambda k: col("q_norm", k), xS)
        dve.wait_ge(*mark("latkv_ssq", 1))
        rstd_dve(dve, "latkv", [(10, 2, KVR)], 16, 2)
        for tt in range(TT):
            dve.tensor_scalar(wk(CL + 256 * tt, 256), bank(6 + tt, KVR), small[:, 18 + tt:19 + tt], None, ALU.mult)
        dve.wait_ge(s("rope_tables"), 2)
        for tt in range(TT):
            kp = wk(KPE + P * tt, P).rearrange("p (g c) -> p g c", c=64)
            halves_rope(dve, bank(6 + tt, ROPE, KVR)[:, None, :], kp[:, 0:1, :], tt, 1)
            last = dve.tensor_copy(kp[:, 1, :], kp[:, 0, :])
        last.then_inc(s("latents"), 1)
        ahead_lo(dve, u + 3)
        ahead_lo(dve, u + 4)
        ahead_lo(dve, u + 5)
        operand_dve(dve, "cl", [(2, 2)], lambda k: col("kv_latent", k), xT)
        ahead_lo(dve, u + 6)
        ahead_lo(dve, u + 7)
        dve.wait_ge(s("used"), u + 8)
        for q in range(2):
            x = bank(4 + q).rearrange("p (g c) -> p g c", c=64)
            halves_rope(dve, x, wk(QPE + 512 * q, 512).rearrange("p (g c) -> p g c", c=64), q, HEADS)
            if q:
                dve.sem_inc(s("qpe"), 1)
                ahead_lo(dve, u + 8)
            dve.wait_ge(s("used"), u + 9 + q)
            dve.tensor_copy(wk(VV, 2048).rearrange("p (t n) -> p t n", t=2)[:, :, 512 * q:512 * q + 512], ps[:, 6:8, :])\
                .then_inc(s("v_read"), 1)
        ahead_lo(dve, u + 9)
        for t in range(HEADS + 2):
            if t < HEADS:
                m = 32 + 8 * (t % 2)
                sm = wk(SM + 384 * (t % 2), 384)
                dve.wait_ge(s("scores"), t + 1)
                if t >= 2:
                    dve.wait_ge(s("exps"), t - 1)
                dve.tensor_tensor(sm, bank(2 + t % 2, 384), const("causal"), ALU.add).then_inc(s("sc_read"), 1)
                dve.wait_ge(s("sc_read"), t + 1)
                dve.tensor_reduce(small[:, m:m + 1], sm[:, 0:P], AX, ALU.max)
                dve_step(dve, dve.tensor_reduce(small[:, m + 1:m + 2], sm[:, P:384], AX, ALU.max))
                dve.tensor_scalar(small[:, m + 2:m + 4], small[:, m:m + 2], -SCALE, None, ALU.mult).then_inc(s("smax"), 1)
                dve.wait_ge(s("exps"), t + 1)
                dve_step(dve, dve.reciprocal(small[:, m + 6:m + 8], small[:, m + 4:m + 6]))
                pb = wk(PB + 384 * (t % 2), 384)
                dve.tensor_scalar(pb[:, 0:P], pb[:, 0:P], small[:, m + 6:m + 7], None, ALU.mult)
                dve.tensor_scalar(pb[:, P:384], pb[:, P:384], small[:, m + 7:m + 8], None, ALU.mult).then_inc(s("probs"), 1)
            if t >= 2:
                v = t - 2
                dve.wait_ge(s("at_hi"), v + 1)
                dve.tensor_tensor(xT_lo[:, v, :], bank(6 + v % 2, T), xT_hi[:, v, :].bitcast(F32), ALU.subtract)\
                    .then_inc(s("at_lo"), 1)
        for q in range(3):
            ahead_lo(dve, u + 10 + q)

    GROW = 9216

    def end1_dve(dve):
        dve.wait_ge(s("grow"), 16)
        for tt in range(TT):
            add_acc(dve, U_WIN, "ffn2", tt)
            tile_rstd_dve(dve, "end1", 2 * tt, tt)
            dve.scalar_tensor_tensor(h[:, tt, :], h[:, tt, :], small[:, 4 + tt:5 + tt], wk(GROW, D), ALU.mult, ALU.mult)\
                .then_inc(s("all_h"), 1)
            tile_rstd_dve(dve, "end1", 2 * tt + 1, tt)
            normed_rows(dve, tt)

    def end1_act(act):
        for tt in range(TT):
            for q in range(2):
                act.wait_ge(*mark("ffn2_h", 2 * tt + q + 1))
                square(act, "end1", 2 * tt + q, tt)

    GQ, GK, GV, SG, ZT, QK, AV = 2048, 2560, 3072, 4096, 5120, 5632, 6912
    A = [0, 1024] + [7168 + 1024 * q for q in range(7)]

    def blk(q, *dims):
        return wk(A[q], 1024)

    def dpt(q):
        return wk(A[q], 1024).rearrange("p (d r t) -> p d r t", d=2, r=2)

    def chunks(q, d):
        return wk(A[q] + 512 * d, 512).rearrange("p (g c) -> p g c", c=CH)

    REF = (CH // 2 - 1, CH // 2)
    LAST = (CH - 1, 0)

    def win_pe(pe):
        u = U_WIN
        norm_pe(pe, "n1")
        unit_ready(pe, u)
        hi, lo = weights(u, KD, 160)
        for z in range(2):
            for k in range(KD):
                if z == 0 and k % 2 == 0:
                    pe.wait_ge(*mark("n1x_lo", k // 2 + 1))
                last = passes(pe, bank(6, T, T * z), hi[:, k, 16 * z:16 * z + P], lo[:, k, 16 * z:16 * z + P],
                              xT_hi[:, k, :], xT_lo[:, k, :], k == 0, k == KD - 1)
        last.then_inc(s("used"), 1)
        by_channel(pe, u + 1, 2, xT)
        by_channel(pe, u + 2, 3, xT)
        pe.wait_ge(s("zt"), 1)
        for d in range(2):
            for r in range(2):
                last = pe.matmul(bank(d, T, T * r), up[0:16, d, P * r:P * r + P], work[0:16, ZT + T * d:ZT + T * d + T],
                                 start=True, stop=True, skip_group_check=True)
        last.then_inc(s("logits"), 1)
        by_token(pe, u + 3, [[bank(7, 256, 256 * tt)] for tt in range(TT)], xT, range(KD), KD, 256, 256, True, True)\
            .then_inc(s("used"), 1)

        def half_of_banks(first, b, q):
            outs = [[bank(b + tt, 256, 256 * q)] for tt in range(TT)]
            by_token(pe, u + first + q, outs, xT, range(KD), KD, 256, 256, True, True).then_inc(s("used"), 1)

        for q in range(2):
            half_of_banks(4, 4, q)
        pe.wait_ge(s("gqk_read"), 1)
        for q in range(2):
            half_of_banks(6, 2, q)
        pe.wait_ge(s("qe_ke"), 1)
        pe.wait_ge(s("qk_read"), 1)
        for d in range(2):
            for n in range(NCH):
                for r in range(2):
                    for par in range(2):
                        rows = slice(64 * par, 64 * par + 64)
                        at = 512 * d + T * r + CH * n
                        c = ((d * 2 + n // 2) * 2 + r) * CH
                        half = slice(64 * (n % 2), 64 * (n % 2) + 64)
                        last = pe.matmul(ps[half, 4 + par, c:c + CH], work[rows, A[1] + at:A[1] + at + CH],
                                         work[rows, A[0] + at:A[0] + at + CH], start=True, stop=True, skip_group_check=True)
        last.then_inc(s("gscores"), 1)
        half_of_banks(8, 6, 0)
        pe.wait_ge(s("kl"), 1)
        pe.wait_ge(s("gv_read"), 1)
        for d in range(2):
            for tt in range(TT):
                for r in range(2):
                    last = pe.transpose(bank(2 + d, P, P * (2 * tt + r)), wk(A[8] + 512 * d + T * r + P * tt, P), ident)
        last.then_inc(s("kl_T"), 1)
        half_of_banks(8, 6, 1)
        pe.wait_ge(s("klt"), 1)
        pe.wait_ge(s("gate_read"), 1)
        for odd in (1, 0):
            if not odd:
                pe.wait_ge(s("sg_read"), 1)
            for d, n in ((d, n) for d in range(2) for n in range(NCH) if n % 2 == odd and n != (NCH - 1, 0)[d]):
                rows = slice(64 * (n % 2), 64 * (n % 2) + 64)
                for r in range(2):
                    for par in range(2):
                        b = (6 + d) if n % 2 == 0 else d
                        c = ((n // 2) * 2 + r) * DV
                        k0 = A[6] + 512 * d + P * (2 * (n // 2) + r) + 64 * par
                        v0 = GV + 512 * (n // 2) + DV * (2 * r + par)
                        last = pe.matmul(ps[64 * par:64 * par + 64, b, c:c + DV], work[rows, k0:k0 + 64],
                                         work[rows, v0:v0 + DV], start=True, stop=True, skip_group_check=True)
        last.then_inc(s("kv"), 1)
        pe.wait_ge(s("masked"), 1)
        for tt in range(TT):
            for hd in range(GH):
                for d in range(2):
                    last = pe.matmul(bank(2 + tt, DV, DV * hd), wk(A[(3, 7)[d]] + 512 * tt + P * hd, P),
                                     wk(GV + 512 * tt + DV * hd, DV), start=d == 0, stop=d == 1, skip_group_check=True)
        last.then_inc(s("own"), 1)
        pe.wait_ge(s("states"), 1)
        for n in range(NCH):
            half = slice(64 * (n % 2), 64 * (n % 2) + 64)
            for r in range(2):
                for par in range(2):
                    rows = slice(64 * par, 64 * par + 64)
                    ds = [d for d in range(2) if n != (0, NCH - 1)[d]]
                    for d in ds:
                        q0 = A[4] + 512 * d + T * r + CH * n
                        st = A[(5, 8)[d]] + 256 * (n - 1 if d == 0 else n) + DV * r
                        c = ((n // 2) * 2 + r) * DV
                        last = pe.matmul(ps[half, 4 + par, c:c + DV], work[rows, q0:q0 + CH], work[rows, st:st + DV],
                                         start=d == ds[0], stop=d == ds[-1], skip_group_check=True)
        last.then_inc(s("past"), 1)
        gqa_pe(pe)

    def win_act(act):
        u = U_WIN
        operand_act(act, "n1x", "n1_T", NORM_BANKS, lambda k: col("norm1", k), xT)
        ahead_hi(act, u - 1)
        ahead_hi(act, u)
        ahead_hi(act, u + 1)
        act.wait_ge(s("used"), u + 3)
        act.activation(wk(GQ, 1024), ps[:, 2:4, :].rearrange("p b n -> p (b n)"), ACT.Copy).then_inc(s("gqk_read"), 1)
        ahead_hi(act, u + 2)
        act.wait_ge(s("logits"), 1)
        for d, name in enumerate(("up_f_bias", "up_b_bias")):
            for r in range(2):
                last = act.activation(dpt(2)[:, d, r, :], bank(d, T, T * r), ACT.Identity, bias=col(name, r))
        last.then_inc(s("gate_read"), 1)
        act.wait_ge(s("absx"), 1)
        act_step(act, act.activation(blk(5), blk(3), ACT.Exp, scale=-1.0))
        act.activation(blk(3), blk(5), ACT.Ln, bias=1.0).then_inc(s("softplus"), 1)
        ahead_hi(act, u + 3)
        ahead_hi(act, u + 4)
        act.wait_ge(s("used"), u + 6)
        for tt in range(TT):
            for r in range(2):
                dst = wk(QK + 640 * tt, 512).rearrange("p (i r c) -> p i r c", r=2, c=AD)[:, :, r, :]
                act.activation(dst, bank(4 + tt, 256, 256 * r).rearrange("p (i c) -> p i c", c=AD), ACT.Copy)
            act.activation(wk(QK + 640 * tt + 512, P), bank(7, P, 256 * tt), ACT.Copy)
            last = act.activation(wk(AV + P * tt, P), bank(7, P, 256 * tt + P), ACT.Copy)
        last.then_inc(s("qk_read"), 1)
        ahead_hi(act, u + 5)
        act.wait_ge(s("d1d3"), 1)
        act.activation(blk(4), blk(2), ACT.Exp).then_inc(s("e"), 1)
        act.activation(blk(6), blk(2), ACT.Exp, scale=-1.0).then_inc(s("e"), 1)
        act.activation(blk(7), blk(3), ACT.Exp).then_inc(s("e"), 1)
        act.wait_ge(s("e"), 3)
        act.activation(blk(2), blk(5), ACT.Exp).then_inc(s("e"), 1)
        ahead_hi(act, u + 6)
        ahead_hi(act, u + 7)
        act.wait_ge(s("kl_T"), 1)
        act.activation(blk(6), ps[:, 2:4, :].rearrange("p b n -> p (b n)"), ACT.Copy).then_inc(s("klt"), 1)
        ahead_hi(act, u + 8)
        act.wait_ge(s("used"), u + 10)
        act.activation(wk(SG, 1024), ps[:, 6:8, :].rearrange("p b n -> p (b n)"), ACT.Silu).then_inc(s("sg_read"), 1)
        ahead_hi(act, u + 9)
        act.wait_ge(s("past"), 1)
        act.activation(blk(0), ps[:, 4:6, :].rearrange("p b n -> p (b n)"), ACT.Copy).then_inc(s("past_read"), 1)
        gqa_act(act)
        for q in range(3):
            ahead_hi(act, U_WOUT + q)

    def win_dve(dve):
        u = U_WIN
        operand_dve(dve, "n1x", NORM_BANKS, lambda k: col("norm1", k), xT)
        ahead_lo(dve, u - 1)
        dve.wait_ge(s("used"), u + 1)
        dve.tensor_copy(work[0:16, ZT:ZT + 512], ps[0:16, 6, :]).then_inc(s("zt"), 1)
        for q in range(3):
            ahead_lo(dve, u + q)
        dve.wait_ge(s("gate_read"), 1)
        dve.wait_ge(s("gqk_read"), 1)
        dve.tensor_scalar(blk(4), blk(2), 0.0, 1.0 / 16, ALU.min, ALU.mult)
        dve_step(dve, dve.tensor_scalar(blk(3), blk(2), -1.0, None, ALU.mult))
        dve.tensor_tensor(blk(3), blk(3), blk(2), ALU.max).then_inc(s("absx"), 1)
        dve.tensor_scalar(wk(GQ, 512), wk(GQ, 512), DK ** -0.5, None, ALU.mult)
        dve.wait_ge(s("softplus"), 1)
        dve_step(dve, dve.scalar_tensor_tensor(blk(2), blk(3), -1.0 / 16, blk(4), ALU.mult, ALU.add))
        ahead_lo(dve, u + 3)
        for g in range(2 * NCH):
            dve.tensor_tensor_scan(chunks(5, 0)[:, g, :], const("ones")[:, 0:CH], chunks(2, 0)[:, g, :], 0.0, ALU.mult, ALU.add)
            last = dve.tensor_tensor_scan(chunks(4, 1)[:, g, :], const("ones")[:, 0:CH], chunks(2, 1)[:, g, :], 0.0, ALU.mult, ALU.add)
        dve_step(dve, last)
        for g in range(2 * NCH):
            last = dve.scalar_tensor_tensor(chunks(5, 1)[:, g, :], chunks(2, 1)[:, g, :], chunks(4, 1)[:, g, CH - 1:CH],
                                            chunks(4, 1)[:, g, :], ALU.add, ALU.subtract)
        dve_step(dve, last)
        for d in range(2):
            b = chunks(5, d)
            dve.tensor_tensor(chunks(2, d), b, b[:, :, REF[d]:REF[d] + 1].broadcast_to([P, 2 * NCH, CH]), ALU.subtract)
            last = dve.tensor_tensor(chunks(3, d), b[:, :, LAST[d]:LAST[d] + 1].broadcast_to([P, 2 * NCH, CH]), b, ALU.subtract)
        last.then_inc(s("d1d3"), 1)
        ahead_lo(dve, u + 4)
        dve.wait_ge(s("e"), 1)
        for d in range(2):
            dve.tensor_tensor(wk(A[0] + 512 * d, 512), wk(GQ, 512), wk(A[4] + 512 * d, 512), ALU.mult)
        dve.wait_ge(s("e"), 2)
        for d in range(2):
            last = dve.tensor_tensor(wk(A[1] + 512 * d, 512), wk(GK, 512), wk(A[6] + 512 * d, 512), ALU.mult)
        last.then_inc(s("qe_ke"), 1)
        dve.wait_ge(s("qk_read"), 1)
        parts = [(A[4], 0, 1024), (A[6], 1024, 256)]
        dve.wait_ge(s("qe_ke"), 1)
        for at, first, n in parts:
            last = dve.tensor_tensor(wk(at, n), wk(QK + first, n), wk(QK + first, n), ALU.mult)
        dve_step(dve, last)
        for at, first, n in parts:
            last = dve.tensor_reduce(small[:, 88 + first // AD:88 + (first + n) // AD],
                                     wk(at, n).rearrange("p (g c) -> p g c", c=AD), AX, ALU.add)
        dve_step(dve, last)
        dve.tensor_scalar(small[:, 170:190], small[:, 88:108], 1.0 / AD, EPS, ALU.mult, ALU.add).then_inc(s("all_mean"), 1)
        ahead_lo(dve, u + 5)
        dve.wait_ge(s("e"), 3)
        for d in range(2):
            last = dve.tensor_tensor(wk(A[8] + 512 * d, 512), wk(GK, 512), wk(A[7] + 512 * d, 512), ALU.mult)
        last.then_inc(s("kl"), 1)
        dve.wait_ge(s("kl"), 1)
        dve.memset(blk(7), 0.0)
        dve.wait_ge(s("e"), 4)
        dve_step(dve, dve.memset(blk(3), 0.0))
        for d in range(2):
            last = dve.tensor_tensor(wk(A[4] + 512 * d, 512), wk(GQ, 512), wk(A[2] + 512 * d, 512), ALU.mult)
        dve_step(dve, last)
        ahead_lo(dve, u + 6)
        dve.wait_ge(s("used"), u + 8)
        dve.tensor_copy(wk(GV, 1024), ps[:, 2:4, :].rearrange("p b n -> p (b n)")).then_inc(s("gv_read"), 1)
        ahead_lo(dve, u + 7)
        dve.wait_ge(s("gscores"), 1)
        for d in range(2):
            for half in range(2):
                rows = slice(64 * half, 64 * half + 64)
                at = CONST["keep_b" if d else "keep_f"][0]
                mask = cst[rows, at:at + 64].bitcast(U32)[:, None, :].broadcast_to([64, 4, 64])
                for par in range(2):
                    dst = work[rows, A[(3, 7)[d]]:A[(3, 7)[d]] + 1024].rearrange("p (g c) -> p g c", c=2 * P)[:, :, par * P + 64 * half:par * P + 64 * half + 64]
                    src = ps[rows, 4 + par, 256 * d:256 * d + 256].rearrange("p (g c) -> p g c", c=64)
                    last = dve.copy_predicated(dst, mask, src)
        last.then_inc(s("masked"), 1)
        ahead_lo(dve, u + 8)
        dve.wait_ge(s("kv"), 1)
        dve.wait_ge(s("kl_T"), 1)

        def added(d, n, r):
            return bank((6 + d) if n % 2 == 0 else d, DV, ((n // 2) * 2 + r) * DV)

        for q in range(3):
            for d in range(2):
                n = q + 1 if d == 0 else 2 - q
                m = n - 1 if d == 0 else n + 1
                for r in range(2):
                    dst = wk(A[(5, 8)[d]] + 256 * (n - 1 if d == 0 else n) + DV * r, DV)
                    if q == 0:
                        last = dve.tensor_copy(dst, added(d, m, r))
                    else:
                        prev = wk(A[(5, 8)[d]] + 256 * (m - 1 if d == 0 else m) + DV * r, DV)
                        at = A[2] + 512 * d + T * r + CH * m + LAST[d]
                        last = dve.scalar_tensor_tensor(dst, prev, work[:, at:at + 1], added(d, m, r), ALU.mult, ALU.add)
            if q < 2:
                dve_step(dve, last)
        last.then_inc(s("states"), 1)
        dve.wait_ge(s("past_read"), 1)
        dve.wait_ge(s("own"), 1)
        for tt in range(TT):
            for par in range(2):
                o = lambda v: v.rearrange("p (r q c) -> p r q c", q=2, c=DV)[:, :, par, :]
                last = dve.tensor_tensor(o(wk(A[1] + 512 * tt, 512)), o(bank(2 + tt)),
                                         wk(A[0] + 512 * par + 256 * tt, 256).rearrange("p (r c) -> p r c", c=DV), ALU.add)
        last.then_inc(s("osum"), 1)
        ahead_lo(dve, u + 9)
        gqa_dve(dve)
        for q in range(3):
            ahead_lo(dve, U_WOUT + q)

    QT, KT, PB2, PT2, OA, ON = A[4], ZT, A[3], A[7], A[5], A[8]

    def slot(hd):
        return hd % 4, hd // 4

    OG_AT = 4

    def gqa_pool(pool):
        steps = [0]

        def step(ins):
            steps[0] += 1
            ins.then_inc(s("pool_steps"), 1)
            pool.wait_ge(s("pool_steps"), steps[0])

        rstd_pool(pool, "qkn", 170, 20)
        pool.wait_ge(*mark("qkn_rstd", 1))
        groups = wk(QK, 1280).rearrange("p (g c) -> p g c", c=AD)
        step(pool.tensor_tensor(groups, groups, small[:, 190:210][:, :, None].broadcast_to([P, 20, AD]), ALU.mult))
        pool.wait_ge(s("rowp"), 16 * 4)
        for tt in range(TT):
            for g0, n, at in ((0, 8, 0), (8, 2, 64)):
                v = groups[:, 10 * tt + g0:10 * tt + g0 + n, :]
                last = pool.tensor_tensor(v, v, rowp[:, at:at + 64][:, None, :].broadcast_to([P, n, AD]), ALU.mult)
        step(last)
        for tt in range(TT):
            c0, s0 = CONST["ax_cos"][0] + 32 * tt, CONST["ax_sin"][0] + 32 * tt
            for g0, n in ((0, 4), (4, 4), (8, 2)):
                x = wk(QK + 640 * tt + 64 * g0, 64 * n).rearrange("p (g c e) -> p g c e", e=2, c=32)
                cos = cst[:, c0:c0 + 32][:, None, :].broadcast_to([P, n, 32])
                sin = cst[:, s0:s0 + 32][:, None, :].broadcast_to([P, n, 32])
                t = [wk(ZT + 128 * q, 32 * n).rearrange("p (g c) -> p g c", c=32) for q in range(4)]
                pool.tensor_tensor(t[0], x[:, :, :, 0], cos, ALU.mult)
                pool.tensor_tensor(t[1], x[:, :, :, 1], sin, ALU.mult)
                pool.tensor_tensor(t[2], x[:, :, :, 0], sin, ALU.mult)
                step(pool.tensor_tensor(t[3], x[:, :, :, 1], cos, ALU.mult))
                pool.tensor_tensor(x[:, :, :, 0], t[0], t[1], ALU.subtract)
                step(pool.tensor_tensor(x[:, :, :, 1], t[2], t[3], ALU.add))
        pool.sem_inc(s("qk"), 1)

    def gqa_pe(pe):
        pe.wait_ge(s("qk"), 1)
        for c in range(4):
            for tt in range(TT):
                last = pe.transpose(bank(c // 2, P, (c % 2) * T + P * tt), wk(QK + 640 * tt + P * c, P), ident)
        last.then_inc(s("aqT"), 1)
        for tt in range(TT):
            last = pe.transpose(bank(6, P, P * tt), wk(QK + 640 * tt + 512, P), ident)
        last.then_inc(s("akT"), 1)
        pe.wait_ge(s("akt"), 1)
        pe.wait_ge(s("osum"), 1)
        for t in range(AH + 2):
            if t < AH:
                c, par = slot(t)
                rows = slice(64 * par, 64 * par + 64)
                if t >= 2:
                    pe.wait_ge(s("aexps"), t - 1)
                for tt in range(TT):
                    last = pe.matmul(bank(2 + t % 2, T, T * tt), work[rows, QT + T * c + P * tt:QT + T * c + P * tt + P],
                                     work[rows, KT:KT + T], start=True, stop=True, skip_group_check=True)
                last.then_inc(s("ascores"), 1)
            if 1 <= t <= AH:
                v = t - 1
                pe.wait_ge(s("aexps"), v + 1)
                if v >= 2:
                    pe.wait_ge(s("apt_read"), v - 1)
                for kk in range(TT):
                    for tt in range(TT):
                        last = pe.transpose(bank(4 + v % 2, P, T * kk + P * tt), wk(PB2 + 512 * (v % 2) + T * tt + P * kk, P), ident)
                last.then_inc(s("aprobs_T"), 1)
            if t >= 2:
                v = t - 2
                pe.wait_ge(s("apt_read"), v + 1)
                for tt in range(TT):
                    for kk in range(TT):
                        last = pe.matmul(bank(6 + tt, AD, AD * v), wk(PT2 + 512 * (v % 2) + T * kk + P * tt, P),
                                         wk(AV + P * kk + AD * (v // 4), AD), start=kk == 0, stop=kk == 1, skip_group_check=True)
                last.then_inc(s("aatt"), 1)
            if t == OG_AT:
                pe.wait_ge(s("og"), 1)
                for hd in range(GH):
                    for tt in range(TT):
                        last = pe.transpose(bank(hd // 2, P, (hd % 2) * T + P * tt), wk(A[6] + 512 * tt + DV * hd, P), ident)
                    if hd % 2:
                        last.then_inc(s("og_T"), 1)

        def w_out(q):
            by_token(pe, U_WOUT + q, ACC, xT, [2 * q, 2 * q + 1], 2, D, 512, q == 0, q == 3, ends_sum=q == 3)\
                .then_inc(s("used"), 1)

        pe.wait_ge(s("oa"), 1)
        pe.wait_ge(*mark("og_lo", 2))
        w_out(0)
        pe.wait_ge(s("on"), 1)
        for c in range(4):
            for tt in range(TT):
                last = pe.transpose(bank(2 + c // 2, P, (c % 2) * T + P * tt), wk(ON + 512 * tt + P * c, P), ident)
            if c % 2:
                last.then_inc(s("on_T"), 1)
        w_out(1)
        pe.wait_ge(*mark("mo_lo", 2))
        w_out(2)
        w_out(3)

    def gqa_act(act):
        act.wait_ge(s("aqT"), 1)
        act.activation(wk(QT, 1024), ps[:, 0:2, :].rearrange("p b n -> p (b n)"), ACT.Copy)
        act.wait_ge(s("akT"), 1)
        act.activation(wk(KT, T), bank(6, T), ACT.Copy).then_inc(s("akt"), 1)
        for t in range(AH + 1):
            if t < AH:
                m = 128 + 4 * t
                act.wait_ge(s("amax"), t + 1)
                if t >= 2:
                    act.wait_ge(s("aprobs_T"), t - 1)
                for tt in range(TT):
                    last = act.activation(wk(PB2 + 512 * (t % 2) + T * tt, T), bank(2 + t % 2, T, T * tt), ACT.Exp,
                                          bias=small[:, m + tt:m + tt + 1], scale=AD ** -0.5,
                                          accum_out=small[:, m + 2 + tt:m + 3 + tt])
                last.then_inc(s("aexps"), 1)
            if t >= 1:
                v = t - 1
                act.wait_ge(s("aprobs_T"), v + 1)
                if v >= 2:
                    act.wait_ge(s("aatt"), v - 1)
                act.activation(wk(PT2 + 512 * (v % 2), 512), bank(4 + v % 2), ACT.Copy).then_inc(s("apt_read"), 1)
            if t == 0:
                act.wait_ge(s("osum"), 1)
                for q in range(8):
                    last = act.activation(wk(A[2] + P * q, P), wk(A[1] + P * q, P), ACT.Square, accum_out=small[:, 64 + q:65 + q])
                last.then_inc(s("all_ssq"), 1)
            if t == OG_AT:
                operand_act(act, "og", "og_T", [(0, 2), (1, 2)], lambda k: col("gla_out"), xT)
        act.wait_ge(s("oa"), 1)
        for tt in range(TT):
            last = act.activation(wk(A[2] + 512 * tt, 512), wk(OA + 512 * tt, 512), ACT.Square, accum_out=small[:, 164 + tt:165 + tt])
        last.then_inc(s("all_ssq"), 1)
        operand_act(act, "mo", "on_T", [(2, 2), (3, 2)], lambda k: col("att_out", k), xT, first=4)

    def gqa_dve(dve):
        for t in range(AH):
            if t == 2:
                dve.wait_ge(*mark("g_ssq", 1))
                rstd_dve(dve, "g", [(64, 8, DV)], 72, 8)
                for q in range(8):
                    last = dve.scalar_tensor_tensor(wk(A[6] + P * q, P), wk(A[1] + P * q, P), small[:, 80 + q:81 + q],
                                                    wk(SG + P * q, P), ALU.mult, ALU.mult)
                last.then_inc(s("og"), 1)
            m = 128 + 4 * t
            dve.wait_ge(s("ascores"), t + 1)
            dve_step(dve, dve.tensor_reduce(small[:, 210 + 2 * t:212 + 2 * t], bank(2 + t % 2).rearrange("p (t n) -> p t n", t=2), AX, ALU.max))
            dve.tensor_scalar(small[:, m:m + 2], small[:, 210 + 2 * t:212 + 2 * t], -(AD ** -0.5), None, ALU.mult).then_inc(s("amax"), 1)
            if t == OG_AT + 1:
                operand_dve(dve, "og", [(0, 2), (1, 2)], lambda k: col("gla_out"), xT)
        dve.wait_ge(s("aatt"), AH)
        sums = small[:, 128:160].rearrange("p (h c) -> p h c", c=4)[:, :, 2:4]
        inv = small[:, 112:128].rearrange("p (h c) -> p h c", c=2)
        dve_step(dve, dve.reciprocal(inv, sums))
        for tt in range(TT):
            last = dve.tensor_tensor(wk(OA + 512 * tt, 512).rearrange("p (h c) -> p h c", c=AD),
                                     bank(6 + tt).rearrange("p (h c) -> p h c", c=AD),
                                     inv[:, :, tt:tt + 1].broadcast_to([P, AH, AD]), ALU.mult)
        last.then_inc(s("oa"), 1)
        dve.wait_ge(*mark("a_ssq", 1))
        rstd_dve(dve, "a", [(164, 2, 512)], 166, 2)
        for tt in range(TT):
            last = dve.tensor_scalar(wk(ON + 512 * tt, 512), wk(OA + 512 * tt, 512), small[:, 168 + tt:169 + tt], None, ALU.mult)
        last.then_inc(s("on"), 1)
        operand_dve(dve, "mo", [(2, 2), (3, 2)], lambda k: col("att_out", k), xT, first=4)

    XN2, NROW, FROW, XT2 = 0, 3072, 4096, 5120
    LG, EL, EM = 7168, 7328, 7456
    ONE = 7584
    AA, RK, RANK, TMP = 7840, 7968, 8096, 8240
    GS, US, SI, AP_, YT, YS = 8448, 8960, 9472, 9728, 9984, 11008
    COUNT, FIRST, UPTO = 7424, 7488, 8304
    CR, CE, CW, CIN, CUP, CROW, CWR = 120, 224, 228, 232, 236, 240, 244
    x_rows = [v[:, :, :].rearrange("p k t -> p (k t)") for v in xS]
    xstat = [xT_hi[:, 4 * b:4 * b + 4, :].rearrange("p k t -> p (k t)").rearrange("p (k m) -> p k m", m=P) for b in range(2)]
    astat = xT_lo[:, 0:2, :].rearrange("p k t -> p (k t)").rearrange("p (k m) -> p k m", m=P)

    def router_pe(pe):
        norm_pe(pe, "n2")
        for tt in range(TT):
            for k in range(KD):
                if tt == 0 and k % 2 == 0:
                    pe.wait_ge(s("xt2"), k // 2 + 1)
                last = pe.matmul(bank(4 + tt, NG + NE), wk(XT2 + T * k + P * tt, P), wr[:, k, :], start=k == 0, stop=k == KD - 1,
                                 skip_group_check=True)
        last.then_inc(s("rlogits"), 1)
        pe.wait_ge(s("choices"), 1)
        a0, a1 = wk(AA, NE), wk(AA + NE, NE)
        pe.matmul(bank(6, NE), const("before"), a0, start=True, stop=True, skip_group_check=True)
        pe.matmul(bank(6, NE, NE), const("ones"), a0, start=True, stop=False, skip_group_check=True)
        pe.matmul(bank(6, NE, NE), const("before"), a1, start=False, stop=True, skip_group_check=True)
        pe.matmul(bank(6, NE, 2 * NE), const("ones"), a0, start=True, stop=False, skip_group_check=True)
        pe.matmul(bank(6, NE, 2 * NE), const("ones"), a1, start=False, stop=True, skip_group_check=True).then_inc(s("ranks"), 1)

    def router_act(act):
        norm_act(act, "n2", lambda tt: mark("mix_h", tt + 1))
        act.wait_ge(*mark("n2_xn", TT))
        act.activation(x_rows[0], wk(XN2, 2048), ACT.Copy).then_inc(s("rows_hi"), 1)
        for b in range(4):
            act.wait_ge(*mark("n2_T", b + 1))
            act.activation(wk(XT2 + 512 * b, 512), bank(b), ACT.Copy).then_inc(s("xt2"), 1)
        ahead_hi(act, U_WOUT + 3)
        act.wait_ge(s("gmax"), 1)
        for tt in range(TT):
            m = 40 * tt
            act.activation(wk(TMP + 16 * tt, NG), wk(LG + 72 * tt, NG), ACT.Exp, bias=small[:, m + 8:m + 9],
                           accum_out=small[:, m + 9:m + 10]).then_inc(s("gsum"), 1)
        act.wait_ge(s("vdiff"), 1)
        for tt in range(TT):
            m = 40 * tt
            act.activation(small[:, m + 31:m + 32], small[:, m + 30:m + 31], ACT.Exp).then_inc(s("vexp"), 1)

    def router_dve(dve):
        dve.wait_ge(s("rows_loaded"), 32)
        for tt in range(TT):
            add_acc(dve, U_WOUT + 4, "mix", tt)
            tile_rstd_dve(dve, "n2", tt, tt)
            dve.scalar_tensor_tensor(wk(XN2 + D * tt, D), h[:, tt, :], small[:, 4 + tt:5 + tt], wk(NROW, D), ALU.mult, ALU.mult)\
                .then_inc(s("all_xn"), 1)
        dve.wait_ge(s("rows_hi"), 1)
        dve.tensor_tensor(x_rows[1], wk(XN2, 2048), x_rows[0].bitcast(F32), ALU.subtract).then_inc(s("rows_lo"), 1)
        ahead_lo(dve, U_WOUT + 3)
        dve.wait_ge(s("rlogits"), 1)
        iota = const("iota")
        lg, el = wk(LG, 144).rearrange("p (t n) -> p t n", t=TT), wk(EL, 16)
        top = top_i[:, :].rearrange("p (t n) -> p t n", t=TT)
        tiles = range(TT)
        em = [wk(EM + 64 * tt, 64).rearrange("p (j g) -> p j g", g=NG) for tt in tiles]
        one_group = [wk(TMP + 32 + 8 * tt, 8) for tt in tiles]

        def each(op):
            for tt in tiles:
                last = op(tt)
            dve_step(dve, last)

        dve_step(dve, dve.tensor_tensor(lg, ps[:, 4:6, 0:NG + NE], rowp[:, None, 128:200].broadcast_to([P, TT, NG + NE]), ALU.add))
        each(lambda tt: dve.max(by_tile(0, 8)[:, tt, :], lg[:, tt, 0:NG]))
        dve.tensor_scalar(by_tile(8), by_tile(0), -1.0, None, ALU.mult).then_inc(s("gmax"), 1)
        each(lambda tt: dve.max_index(top[:, tt, 0:8], by_tile(0, 8)[:, tt, :], lg[:, tt, 0:NG]))
        dve_step(dve, dve.tensor_copy(by_tile(24), top[:, :, 0:1]))
        each(lambda tt: dve.tensor_scalar(one_group[tt], iota[:, 0:NG], by_tile(24)[:, tt, :], None, ALU.is_equal))
        each(lambda tt: dve.tensor_tensor(em[tt], lg[:, tt, NG:72].rearrange("p (g j) -> p j g", g=NG),
                                          one_group[tt][:, None, :].broadcast_to([P, EPG, NG]), ALU.mult))
        dve_step(dve, dve.tensor_reduce(el, wk(EM, 128).rearrange("p (j g) -> p j g", g=NG), AX, ALU.add))
        each(lambda tt: dve.max(by_tile(16, 8)[:, tt, :], el[:, 8 * tt:8 * tt + 8]))
        each(lambda tt: dve.max_index(top[:, tt, 8:16], by_tile(16, 8)[:, tt, :], el[:, 8 * tt:8 * tt + 8]))
        dve_step(dve, dve.tensor_copy(by_tile(26, 2), top[:, :, 8:10]))
        dve_step(dve, dve.scalar_tensor_tensor(by_tile(28, 2), by_tile(24).broadcast_to([P, TT, 2]), float(EPG), by_tile(26, 2),
                                               ALU.mult, ALU.add))
        for c in range(2):
            for tt in tiles:
                last = dve.tensor_scalar(wk(ONE + 128 * tt + 64 * c, 64), iota, by_tile(28 + c)[:, tt, :], None, ALU.is_equal)
        dve_step(dve, last)
        ones = wk(ONE, 256).rearrange("p (t c n) -> p t c n", t=TT, c=2)
        chosen = wk(AA, 128)
        dve.tensor_tensor(chosen.rearrange("p (t n) -> p t n", t=TT), ones[:, :, 0, :], ones[:, :, 1, :], ALU.add)\
            .then_inc(s("choices"), 1)
        dve.tensor_tensor(by_tile(30), by_tile(17), by_tile(16), ALU.subtract).then_inc(s("vdiff"), 1)
        dve.wait_ge(s("choices"), 1)
        dve.wait_ge(s("ranks"), 1)
        dve_step(dve, dve.scalar_tensor_tensor(wk(EM, 128), bank(6, 128), 1.0, chosen, ALU.add, ALU.mult))
        dve_step(dve, dve.tensor_scalar(wk(RANK, 128), wk(EM, 128), -1.0, None, ALU.add))

    def by_tile(at, n=1):
        return small[:, 0:80].rearrange("p (t c) -> p t c", c=40)[:, :, at:at + n]

    def choices_dve(dve):
        dve.wait_ge(s("gsum"), 2)
        dve.wait_ge(s("vexp"), 2)
        dve_step(dve, dve.tensor_scalar(by_tile(32), by_tile(31), 1.0, None, ALU.add))
        dve.reciprocal(by_tile(33), by_tile(32))
        dve_step(dve, dve.reciprocal(by_tile(34), by_tile(9)))
        dve_step(dve, dve.tensor_tensor(by_tile(36), by_tile(33), by_tile(34), ALU.mult))
        dve_step(dve, dve.tensor_tensor(by_tile(37), by_tile(36), by_tile(31), ALU.mult))
        for tt in range(TT):
            last = dve.tensor_tensor(wk(LG + 128 * tt, 128).rearrange("p (c n) -> p c n", c=2),
                                     wk(ONE + 128 * tt, 128).rearrange("p (c n) -> p c n", c=2),
                                     bank(6, 64, 64 * tt)[:, None, :].broadcast_to([P, 2, NE]), ALU.mult)
        dve_step(dve, last)
        dve_step(dve, dve.tensor_reduce(small[:, CR:CR + 4], wk(LG, 256).rearrange("p (c n) -> p c n", n=NE), AX, ALU.add))
        dve_step(dve, dve.tensor_copy(wk(COUNT, NE), bank(6, NE, 2 * NE)))
        dve_step(dve, dve.tensor_tensor_scan(wk(UPTO, NE), const("ones")[:, 0:NE], wk(COUNT, NE), 0.0, ALU.mult, ALU.add))
        dve.tensor_copy(tables_i[:, 0:NE], wk(COUNT, NE))
        dve_step(dve, dve.tensor_tensor(wk(FIRST, NE), wk(UPTO, NE), wk(COUNT, NE), ALU.subtract))
        dve.tensor_copy(tables_i[:, NE:2 * NE], wk(FIRST, NE)).then_inc(s("tables"), 1)
        dve_step(dve, dve.tensor_tensor(wk(LG, 256).rearrange("p (c n) -> p c n", n=NE), wk(ONE, 256).rearrange("p (c n) -> p c n", n=NE),
                                        wk(FIRST, NE)[:, None, :].broadcast_to([P, 4, NE]), ALU.mult))
        dve.tensor_reduce(small[:, CE:CE + 4], wk(LG, 256).rearrange("p (c n) -> p c n", n=NE), AX, ALU.add)
        dve.tensor_copy(small[:, CW:CW + 4].rearrange("p (t c) -> p t c", t=TT), by_tile(36, 2))
        dve_step(dve, dve.tensor_reduce(small[:, 130:131], bank(6, NE, 2 * NE), AX, ALU.max))
        for q in range(3):
            last = dve.tensor_scalar(small[:, 131 + q:132 + q], small[:, 130:131], float(CAP * (q + 1)), None, ALU.is_gt)
        dve_step(dve, last)
        dve_step(dve, dve.tensor_reduce(small[:, 134:135], small[:, 131:134], AX, ALU.add))
        dve_step(dve, dve.tensor_scalar(small[:, 135:136], small[:, 134:135], 1.0, None, ALU.add))
        dve.tensor_copy(rounds_i[:, :], small[:, 135:136]).then_inc(s("rounds"), 1)

    MU = U_MOE
    STEP = U_MOE + 4
    assert NE % 2 == 0 and RAW == 6

    def rounds(eng, one_round):
        one_round(0)
        eng.wait_ge(s("rounds"), 1)
        n = eng.value_load(rounds_i[0:1, 0:1], min_val=1, max_val=T // CAP)
        with eng.If(n > 1):
            with eng.Fori(1, n) as r:
                one_round(r)

    def expert_steps(eng, r, step):
        with eng.Fori(0, NE // 2 - 1) as i:
            for p in range(2):
                step(i * 2 + (1 + p), r * NE + i * 2 + (1 + p), r * NE + i * 2 + p, (1 + p) % 2, False)
        step(NE - 1, r * NE + (NE - 1), r * NE + (NE - 2), (NE - 1) % 2, True)

    def moe_sp(sp):
        def one_round(r):
            for q in range(4):
                load(sp, MU + q, moe_unit(q, 0), r * NE)
            with sp.Fori(0, NE - 1) as i:
                for q in range(6):
                    load(sp, MU + 4 + q, moe_unit(q, i + 1 if q < 4 else i), r * NE + i)
            for q in range(2):
                load(sp, MU + 4 + q, moe_unit(4 + q, NE - 1), r * NE + (NE - 1))

        rounds(sp, one_round)

    def moe_pe(pe):
        pe.wait_ge(s("rows_lo"), 1)

        def products(u, g, out_bank, stat, first, last_half):
            unit_ready(pe, u, g)
            hi, lo = weights(u, 4, 512)
            for k in range(4):
                st = stat(k)
                pe.matmul(bank(out_bank), st, hi[:, k, :], start=first and k == 0, stop=False, skip_group_check=True)
                last = pe.matmul(bank(out_bank), st, lo[:, k, :], start=False, stop=last_half and k == 3, skip_group_check=True)
            last.then_inc(s("used"), 1)

        def up_like(u, g, out_bank, par, q):
            products(u, g, out_bank, lambda k: xstat[par][:, 4 * q + k, :], q == 0, q == 1)

        def gather(E, ks):
            if ks[0] == 0:
                pe.wait_ge(s("sel"), E + 1)
            for k in ks:
                for part in range(2):
                    for tt in range(TT):
                        last = pe.matmul(bank(2 + k // 4, CAP, (k % 4) * P + CAP * part),
                                         x_rows[part][:, D * tt + P * k:D * tt + P * k + P], sel[:, tt, :],
                                         start=tt == 0, stop=tt == 1, skip_group_check=True)
                if k == 3:
                    last.then_inc(s("x_first"), 1)
                if k == 7:
                    last.then_inc(s("x_second"), 1)

        def fold_g(E):
            pe.wait_ge(s("g_read"), E + 1)
            for k in range(4):
                last = pe.matmul(bank(4, CAP, CAP * k), wk(GS + P * k, P), const("fold"),
                                 start=True, stop=True, skip_group_check=True)
            last.then_inc(s("g_T"), 1)

        def fold_u(E):
            pe.wait_ge(s("u_read"), E + 1)
            for k in range(4):
                last = pe.matmul(bank(7, CAP, CAP * k), wk(US + P * k, P), const("fold"),
                                 start=True, stop=True, skip_group_check=True)
            last.then_inc(s("u_T"), 1)

        def down(u, g, q):
            products(u + q, g, 5 + q, lambda k: astat[:, k, :], True, True)

        def step(e, E, g, par, last):
            pe.wait_ge(s("xa"), E + 1)
            pe.wait_ge(s("xd"), E + 1)
            up_like(STEP, g, 0, par, 0)
            fold_u(g)
            up_like(STEP + 1, g, 0, par, 1)
            if not last:
                gather(E + 1, (0, 1))
            up_like(STEP + 2, g, 1, par, 0)
            pe.wait_ge(s("si"), E)
            fold_g(E)
            up_like(STEP + 3, g, 1, par, 1)
            if not last:
                gather(E + 1, (2, 3, 4, 5))
            pe.wait_ge(s("a_lo"), E)
            down(STEP + 4, g, 0)
            if not last:
                gather(E + 1, (6, 7))
            down(STEP + 4, g, 1)

        def one_round(r):
            g = r * NE
            gather(g, range(KD))
            pe.wait_ge(s("xa"), g + 1)
            pe.wait_ge(s("xd"), g + 1)
            for q in range(2):
                up_like(MU + q, g, 0, 0, q)
            gather(g + 1, (0, 1, 2, 3))
            up_like(MU + 2, g, 1, 0, 0)
            fold_g(g)
            up_like(MU + 3, g, 1, 0, 1)
            gather(g + 1, (4, 5, 6, 7))
            expert_steps(pe, r, step)
            fold_u(g + (NE - 1))
            pe.wait_ge(s("a_lo"), g + NE)
            for q in range(2):
                down(MU + 4, g + (NE - 1), q)

        rounds(pe, one_round)

    def moe_act(act):
        act.wait_ge(s("rows_hi"), 1)
        act.activation(small[:, 250:251], cst[:, 0:1], ACT.Silu)
        def x_half(E, par):
            act.wait_ge(s("x_first"), E + 1)
            act.activation(xstat[par][:, 0:4, :].rearrange("p k m -> p (k m)"), bank(2), ACT.Copy).then_inc(s("xa"), 1)

        def g_out(u, g):
            act.wait_ge(s("used"), num(u + 1, g))
            act.activation(wk(GS, 512), bank(0), ACT.Copy).then_inc(s("g_read"), 1)

        def u_out(u, g):
            act.wait_ge(s("used"), num(u + 1, g))
            act.activation(wk(US, 512), bank(1), ACT.Copy).then_inc(s("u_read"), 1)

        def silu(E):
            act.wait_ge(s("g_T"), E + 1)
            act.activation(wk(SI, 256), bank(4, 256), ACT.Silu).then_inc(s("si"), 1)

        def a_hi(E):
            act.wait_ge(s("a_mul"), E + 1)
            act.activation(astat[:, :, 0:CAP], wk(AP_, 256).rearrange("p (k m) -> p k m", k=4), ACT.Copy).then_inc(s("a_hi"), 1)

        def y_out(u, g, q):
            act.wait_ge(s("used"), num(u + q + 1, g))
            if q == 0:
                act.wait_ge(s("y_room"), g + 1)
            half = slice(512 * q, 512 * q + 512)
            act.activation(work[0:CAP, YT:YT + D][:, half], ps[CAP:P, 5 + q, :], ACT.Copy)
            act.activation(work[0:CAP, YS:YS + D][:, half], ps[0:CAP, 5 + q, :], ACT.Copy).then_inc(s("y_out"), 1)

        def step(e, E, g, par, last):
            u = STEP
            split_hi(act, u + 3, UNIT, g)
            g_out(u + 1, g)
            a_hi(g)
            split_hi(act, u + 4, UNIT, g)
            split_hi(act, u + 5, UNIT, g)
            silu(E)
            u_out(u + 3, g)
            split_hi(act, u + 6, UNIT, g)
            if not last:
                x_half(E + 1, 1 - par)
            y_out(u + 4, g, 0)
            split_hi(act, u + 7, UNIT, g)
            y_out(u + 4, g, 1)
            if not last:
                split_hi(act, u + 8, UNIT, g)

        def one_round(r):
            g = r * NE
            if not isinstance(r, int):
                for q in range(3):
                    split_hi(act, MU + q, UNIT, g)
            x_half(g, 0)
            split_hi(act, MU + 3, UNIT, g)
            g_out(MU + 1, g)
            split_hi(act, MU + 4, UNIT, g)
            split_hi(act, MU + 5, UNIT, g)
            silu(g)
            u_out(MU + 3, g)
            x_half(g + 1, 1)
            split_hi(act, MU + 6, UNIT, g)
            expert_steps(act, r, step)
            a_hi(g + (NE - 1))
            for q in range(2):
                y_out(MU + 4, g + (NE - 1), q)

        rounds(act, one_round)

    def moe_dve(dve):
        def select(e, E, first=False):
            if not first:
                dve.wait_ge(s("x_second"), E)
            for tt in range(TT):
                if isinstance(e, int):
                    rank = wk(RANK + NE * tt + e, 1)
                else:
                    rank = work[:, bass.ds(e + (RANK + NE * tt), 1)]
                last = dve.tensor_scalar(sel[:, tt, :], const("iota"), rank, None, ALU.is_equal)
            last.then_inc(s("sel"), 1)

        def x_half(E, par):
            dve.wait_ge(s("x_second"), E + 1)
            dve.tensor_copy(xstat[par][:, 4:8, :].rearrange("p k m -> p (k m)"), bank(3)).then_inc(s("xd"), 1)

        def a_mul(E):
            dve.wait_ge(s("si"), E + 1)
            dve.wait_ge(s("u_T"), E + 1)
            dve.tensor_tensor(wk(AP_, 256), bank(7, 256), wk(SI, 256), ALU.mult).then_inc(s("a_mul"), 1)

        def a_lo(E):
            dve.wait_ge(s("a_hi"), E + 1)
            dve.tensor_tensor(astat[:, :, CAP:P], wk(AP_, 256).rearrange("p (k m) -> p k m", k=4),
                              astat[:, :, 0:CAP].bitcast(F32), ALU.subtract).then_inc(s("a_lo"), 1)

        def round_step(r, q, ins):
            ins.then_inc(s("round_steps"), 1)
            dve.wait_ge(s("round_steps"), r * ROUND_STEPS + (q + 1))

        def choices_in_round(r):
            c = lambda at: small[:, at:at + 4]
            round_step(r, 0, dve.tensor_scalar(c(CIN), c(CR), 0.0, None, ALU.is_ge))
            round_step(r, 1, dve.tensor_scalar(c(CUP), c(CR), float(CAP), None, ALU.is_lt))
            round_step(r, 2, dve.tensor_tensor(c(CIN), c(CIN), c(CUP), ALU.mult))
            round_step(r, 3, dve.tensor_tensor(c(CUP), c(CIN), c(CR), ALU.mult))
            round_step(r, 4, dve.tensor_tensor(c(CROW), c(CE), c(CUP), ALU.add))
            round_step(r, 5, dve.tensor_tensor(c(CWR), c(CW), c(CIN), ALU.mult))
            dve.tensor_copy(slot_i[:, :], c(CROW)).then_inc(s("slots"), 1)

        def add_rows(r):
            for tt in range(TT):
                for c in range(2):
                    q = 2 * tt + c
                    dve.wait_ge(s(f"gathered{q}"), r * 16 + 16)
                    last = dve.scalar_tensor_tensor(h[:, tt, :], wk(GY[q], D), small[:, CWR + q:CWR + q + 1], h[:, tt, :],
                                                    ALU.mult, ALU.add)
                    round_step(r, 6 + q, last)
            dve.tensor_scalar(small[:, CR:CR + 4], small[:, CR:CR + 4], -float(CAP), None, ALU.add)
            round_step(r, 10, dve.tensor_scalar(wk(RANK, 2 * NE), wk(RANK, 2 * NE), -float(CAP), None, ALU.add))

        def step(e, E, g, par, last):
            u = STEP
            if not last:
                select(e + 1, E + 1)
            split_lo(dve, u + 3, UNIT, g)
            a_mul(g)
            split_lo(dve, u + 4, UNIT, g)
            a_lo(g)
            split_lo(dve, u + 5, UNIT, g)
            split_lo(dve, u + 6, UNIT, g)
            if not last:
                x_half(E + 1, 1 - par)
            split_lo(dve, u + 7, UNIT, g)
            if not last:
                split_lo(dve, u + 8, UNIT, g)

        ROUND_STEPS = 11

        def one_round(r):
            g = r * NE
            select(0, g, True)
            if not isinstance(r, int):
                for q in range(3):
                    split_lo(dve, MU + q, UNIT, g)
            x_half(g, 0)
            select(1, g + 1)
            if isinstance(r, int):
                choices_dve(dve)
            split_lo(dve, MU + 3, UNIT, g)
            split_lo(dve, MU + 4, UNIT, g)
            choices_in_round(r)
            split_lo(dve, MU + 5, UNIT, g)
            x_half(g + 1, 1)
            split_lo(dve, MU + 6, UNIT, g)
            expert_steps(dve, r, step)
            a_mul(g + (NE - 1))
            a_lo(g + (NE - 1))
            add_rows(r)

        rounds(dve, one_round)
        dve.sem_inc(s("out_h"), 1)

    FEW = 16

    def moe_pool(pool, r):
        if isinstance(r, int):
            pool.wait_ge(s("tables"), 1)
        with pool.Fori(0, NE) as e:
            E = r * NE + e
            for q in range(2):
                pool.wait_ge(s("y_out"), E * 2 + (q + 1))
                y = work[0:CAP, YS + 512 * q:YS + 512 * q + 512]
                pool.tensor_tensor(y, y, work[0:CAP, YT + 512 * q:YT + 512 * q + 512], ALU.add).then_inc(s("y_sum"), 1)
            pool.wait_ge(s("y_sum"), E * 2 + 2)
            left = pool.value_load(tables_i[0:1, bass.ds(e, 1)], min_val=0, max_val=T) - r * CAP
            row = pool.value_load(tables_i[0:1, bass.ds(e + NE, 1)], min_val=0, max_val=2 * T)
            for few in (True, False):
                with pool.If(left <= FEW if few else left > FEW):
                    n = FEW if few else CAP
                    pool.dma_start(y_slots[bass.ds(row, n), :], work[0:n, YS:YS + D]).then_inc(s("y_stored"), 16)
            pool.wait_ge(s("y_stored"), r * (16 * NE) + e * 16 + 16)
            pool.sem_inc(s("y_room"), 1)

    GY = (5120, 6144, 12032, 13056)

    def end_pool(pool):
        def one_round(r):
            moe_pool(pool, r)
            pool.wait_ge(s("slots"), r + 1)
            pool.sem_inc(s("gathers_may_start"), 1)
            for q in range(4):
                pool.indirect_dma_start(out=wk(GY[q], D), out_offset=None, in_=y_slots,
                                        in_offset=bass.IndirectOffsetOnAxis(ap=slot_i[:, q:q + 1], axis=0))\
                    .then_inc(s(f"gathered{q}"), 16)

        rounds(pool, one_round)
        norm_pool(pool, "end")

    def end_dve(dve):
        for tt in range(TT):
            tile_rstd_dve(dve, "end", tt, tt)
            dve.scalar_tensor_tensor(wk(D * tt, D), h[:, tt, :], small[:, 4 + tt:5 + tt], wk(FROW, D), ALU.mult, ALU.mult)\
                .then_inc(s("result"), 1)

    def end_act(act):
        norm_act(act, "end", lambda tt: (s("out_h"), 1))

    up = sb("up", [16, 2, 256])
    rowp = sb("rowp", [P, 2 * AD + NG + NE])
    pos_i = sb("pos_i", [P, TT], I32)
    top_i = sb("top_i", [P, 32], U32)
    slot_i = sb("slot_i", [P, 4], U32)
    rounds_i = sb("rounds_i", [P, 1], I32)
    tables_i = sb("tables_i", [P, 2 * NE], I32)
    sel = sb("sel", [P, TT, CAP], F32R)

    with nc.Block() as block:
        def load_rows(eng, names):
            for name, src in names:
                v = a[src]
                v = v.rearrange({1: "(k p) -> k p", 2: "a (k p) -> (a k) p", 3: "a b (k p) -> (a b k) p"}[len(v.shape)], p=P)
                first = names is FIRST_ROWS
                row = ROWS[name] - (0 if first else N_FIRST)
                at = ROW_AT + (0 if first else P)
                eng.dma_start(work[row:row + v.shape[0], at:at + P], v).then_inc(s("first_params" if first else "params"), 16)

        @block.sync
        def _(sp):
            for tt in range(TT):
                sp.dma_start(h[:, tt, :], a["x"][0, P * tt:P * tt + P, :]).then_inc(s(f"h_loaded{tt}"), 16)
            sp.dma_start(cst[:, :], consts_d).then_inc(s("consts_loaded"), 16)
            for j in range(JC):
                u = conv_first_unit(j)
                for q in range(3):
                    load(sp, u + q, conv_unit(CONV_ORDER[q], j))
                if j:
                    load(sp, u + 3, conv_unit(3, j - 1))
            load(sp, U_CONV + N_CONV - 1, conv_unit(3, JC - 1))
            for base, w13, w2, units, first in ((U_FFN1, "conv_ffn_w13", "conv_ffn_w2", mla_units, U_MLA),
                                                (U_FFN2, "mla_ffn_w13", "mla_ffn_w2", win_units + wout_units, U_WIN)):
                w13, w2 = a[w13][0], a[w2][0]
                for q in range(2):
                    load(sp, base + q, ffn_unit(w13, w2, q, 0))
                with sp.Fori(0, (JF - 1) // 2) as i:
                    for q in range(2):
                        j = i * 2 + (1 + q)
                        load(sp, base + 2 + 3 * q, ffn_unit(w13, w2, 0, j), i)
                        load(sp, base + 3 + 3 * q, ffn_unit(w13, w2, 1, j), i)
                        load(sp, base + 4 + 3 * q, ffn_unit(w13, w2, 2, i * 2 + q), i)
                load(sp, base + N_FFN - 1, ffn_unit(w13, w2, 2, JF - 1))
                for q, unit in enumerate(units):
                    load(sp, first + q, unit)
            moe_sp(sp)
            for tt in range(TT):
                sp.wait_ge(s("result"), tt + 1)
                sp.dma_start(out[0, P * tt:P * tt + P, :], wk(D * tt, D)).then_inc(s("stored"), 16)
            sp.wait_ge(s("stored"), 32)

        @block.gpsimd
        def _(pool):
            pool.wait_ge(s("consts_loaded"), 16)
            pool.memset(zeros[:, :].bitcast(F32), 0.0).then_inc(s("zeros"), 1)
            norm_pool(pool, "cv")
            load_rows(pool, OTHER_ROWS)
            with nc.allow_non_contiguous_dma(reason="256 words"):
                pool.dma_start(pos_i[:, :], a["positions"][0].rearrange("(t p) -> p t", p=P)).then_inc(s("params"), 16)
            pool.dma_start(up[:, 0, :], a["gla_up_fwd_2"][0]).then_inc(s("params"), 16)
            pool.dma_start(up[:, 1, :], a["gla_up_bwd_2"][0]).then_inc(s("params"), 16)
            pool.dma_start(wr[:, :, 0:NG], rows_by_chunk(a["w_group_2"][0])).then_inc(s("params"), 16)
            pool.dma_start(wr[:, :, NG:NG + NE], rows_by_chunk(a["w_expert_2"][0])).then_inc(s("params"), 16)
            for at, n, src in ((0, AD, "q_norm_gain_2"), (AD, AD, "k_norm_gain_2"), (2 * AD, NG, "b_group_2"),
                               (2 * AD + NG, NE, "b_expert_2")):
                pool.dma_start(rowp[:, at:at + n], a[src].broadcast_to([P, n])).then_inc(s("rowp"), 16)
            blank = wk(12288, D)
            pool.memset(blank, 0.0).then_inc(s("blank"), 1)
            pool.wait_ge(s("blank"), 1)
            rows = 2 * T + CAP
            for q in range(0, rows, P):
                pool.dma_start(y_slots[q:min(q + P, rows), :], blank[0:min(P, rows - q)]).then_inc(s("y_blank"), 16)
            pool.wait_ge(s("y_blank"), 16 * -(-rows // P))
            for t in ("ffn1", "mla"):
                norm_pool(pool, t)
            rstd_pool(pool, "latq", 12, 2)
            rstd_pool(pool, "latkv", 16, 2)
            norm_pool(pool, "ffn2")
            pool.wait_ge(*mark("mla_h", TT))
            pool.dma_start(wk(GROW, D), a["final_norm_g"][None, :].broadcast_to([P, D])).then_inc(s("grow"), 16)
            for q in range(2 * TT):
                tile_rstd_pool(pool, "end1", q, q // 2)
            gqa_pool(pool)
            rstd_pool(pool, "g", 72, 8)
            pool.wait_ge(s("osum"), 1)
            pool.wait_ge(s("og"), 1)
            pool.dma_start(wk(NROW, D), a["norm2_gain_2"].broadcast_to([P, D])).then_inc(s("rows_loaded"), 16)
            pool.dma_start(wk(FROW, D), a["final_gain_2"][None, :].broadcast_to([P, D])).then_inc(s("rows_loaded"), 16)
            rstd_pool(pool, "a", 166, 2)
            norm_pool(pool, "n2")
            pool.sem_inc(s("y_room"), 1)
            end_pool(pool)

        @block.scalar
        def _(act):
            load_rows(act, FIRST_ROWS)
            conv_act(act)
            ffn_act(act, 1, U_FFN1, "cv_h", lambda k: col("ffn1_norm", k))
            mla_act(act)
            ffn_act(act, 2, U_FFN2, "mla_h", lambda k: col("ffn2_norm", k))
            end1_act(act)
            win_act(act)
            router_act(act)
            moe_act(act)
            end_act(act)

        @block.vector
        def _(dve):
            conv_dve(dve)
            ffn_dve(dve, 1, U_FFN1, lambda k: col("ffn1_norm", k), (U_CONV + N_CONV, "cv"))
            mla_dve(dve)
            ffn_dve(dve, 2, U_FFN2, lambda k: col("ffn2_norm", k), (U_FFN2, "mla"))
            end1_dve(dve)
            win_dve(dve)
            router_dve(dve)
            moe_dve(dve)
            end_dve(dve)

        @block.tensor
        def _(pe):
            pe.wait_ge(s("consts_loaded"), 16)
            parameter_columns(pe, 0, 7)
            conv_pe(pe)
            ffn_pe(pe, 1, U_FFN1)
            mla_pe(pe)
            ffn_pe(pe, 2, U_FFN2)
            win_pe(pe)
            router_pe(pe)
            moe_pe(pe)


_INS = ["x", "positions", "conv_norm_g", "conv_w_in", "conv_w", "conv_w_out", "conv_ffn_norm_g", "conv_ffn_w13",
        "conv_ffn_w2", "kv_norm_g", "w_dkv", "kv_latent_norm_g", "w_ukv", "mla_norm_g", "mla_w_dq", "mla_q_norm_g",
        "mla_w_uq", "mla_w_o", "mla_ffn_norm_g", "mla_ffn_w13", "mla_ffn_w2", "final_norm_g", "norm1_gain_2",
        "w_in_2", "gla_up_fwd_2", "gla_up_fwd_bias_2", "gla_up_bwd_2", "gla_up_bwd_bias_2", "gla_out_gain_2",
        "q_norm_gain_2", "k_norm_gain_2", "att_out_gain_2", "w_out_2", "norm2_gain_2", "w_group_2", "b_group_2",
        "w_expert_2", "b_expert_2", "w_gate_2", "w_up_2", "w_down_2", "final_gain_2"]


def kernel(**inputs):
    import concourse.bacc as bacc
    from concourse.bass_utils import run_bass_kernel_spmd

    nc = bacc.Bacc("TRN2", target_bir_lowering=False, num_devices=1)
    arrays, aps = {}, {}
    for name in _INS:
        v = np.ascontiguousarray(inputs[name])
        arrays[f"in_{name}"] = v
        aps[name] = nc.dram_tensor(f"in_{name}", v.shape, mybir.dt.from_np(v.dtype), kind="ExternalInput").ap()
    arrays["consts"] = shape_constants()
    consts_d = nc.dram_tensor("consts", (P, NCONST), F32, kind="ExternalInput").ap()
    out = nc.dram_tensor("out_0", (1, T, D), F32, kind="ExternalOutput").ap()
    program(nc, aps, consts_d, out)
    r = run_bass_kernel_spmd(nc, [arrays], core_ids=[0])
    return r.results[0]["out_0"]
```
